# Optimizing a Trainium2 kernel written in Bass

```python
import jax, jax.numpy as jnp
from jax import lax
import numpy as np

D_MODEL = 1024
BATCH = 1
SEQ = 2048
DEPTH = 1

HEAD_DIM = 64
ROPE_THETA = 10000.0
RMS_EPS = 1e-6
NEG_INF = -1e30
DIL_PAIRS = ((128, 1), (512, 4), (2048, 16))
DIL_HEADS = 4
DIL_TOTAL_HEADS = len(DIL_PAIRS) * DIL_HEADS
DIL_W = DIL_TOTAL_HEADS * HEAD_DIM
DIL_BLOCK = 64
SWA_Q_HEADS = 8
SWA_KV_HEADS = 2
SWA_WINDOW = 128
SWA_BLOCK = 128
SWA_QW = SWA_Q_HEADS * HEAD_DIM
SWA_KVW = SWA_KV_HEADS * HEAD_DIM
N_BRANCHES = 2
IN_SPLITS = tuple(int(v) for v in np.cumsum([DIL_W, DIL_W, DIL_W, SWA_QW, SWA_KVW, SWA_KVW, D_MODEL]))
IN_WIDTH = 3 * DIL_W + SWA_QW + 2 * SWA_KVW + N_BRANCHES * D_MODEL
MOE_GROUPS = 4
EXPERTS_PER_GROUP = 8
N_EXPERTS = MOE_GROUPS * EXPERTS_PER_GROUP
TOP_K = 2
D_EXPERT = 512
MOE_BLOCK = 128
N_MOD = 6

kernel_name = 'hybrid_dilated_swa_hmoe_adaln_encoder'

def rms_norm(x, g):
    x32 = x.astype(jnp.float32)
    y = x32 * lax.rsqrt(jnp.mean(x32 * x32, axis=-1, keepdims=True) + RMS_EPS)
    return y.astype(x.dtype) * g

def rope(t, positions):
    half = HEAD_DIM // 2
    inv_freq = ROPE_THETA ** (-jnp.arange(half, dtype=jnp.float32) * (2.0 / HEAD_DIM))
    ang = positions.astype(jnp.float32)[..., None] * inv_freq
    cos = jnp.cos(ang)[:, :, None, :]
    sin = jnp.sin(ang)[:, :, None, :]
    t32 = t.astype(jnp.float32)
    t1, t2 = t32[..., :half], t32[..., half:]
    return jnp.concatenate([t1 * cos - t2 * sin, t2 * cos + t1 * sin], axis=-1).astype(t.dtype)

def band_attention(q, k, v, window, block, sink=None):
    bt, length, hq, dh = q.shape
    hkv = k.shape[2]
    grp = hq // hkv
    nb = -(-length // block)
    lp = nb * block
    ks = block + 2 * window
    q = jnp.pad(q, ((0, 0), (0, lp - length), (0, 0), (0, 0)))
    kv_pad = ((0, 0), (window, lp - length + window), (0, 0), (0, 0))
    k = jnp.pad(k, kv_pad)
    v = jnp.pad(v, kv_pad)
    slab = jnp.arange(nb)[:, None] * block + jnp.arange(ks)[None, :]
    kb = k[:, slab]
    vb = v[:, slab]
    qb = q.reshape(bt, nb, block, hkv, grp, dh)
    s = jnp.einsum('bnqhgd,bnkhd->bnhgqk', qb, kb, preferred_element_type=jnp.float32) * (dh ** -0.5)
    rel = jnp.arange(ks)[None, :] - window - jnp.arange(block)[:, None]
    kpos = slab - window
    mask = (jnp.abs(rel) <= window)[None] & ((kpos >= 0) & (kpos < length))[:, None, :]
    s = jnp.where(mask[None, :, None, None], s, NEG_INF)
    m = jnp.max(s, axis=-1)
    if sink is not None:
        sk = sink.astype(jnp.float32).reshape(hkv, grp)[None, None, :, :, None]
        m = jnp.maximum(m, sk)
    e = jnp.exp(s - m[..., None])
    denom = jnp.sum(e, axis=-1)
    if sink is not None:
        denom = denom + jnp.exp(sk - m)
    o = jnp.einsum('bnhgqk,bnkhd->bnqhgd', e, vb.astype(jnp.float32))
    o = o / jnp.moveaxis(denom, -1, 2)[..., None]
    o = o.reshape(bt, lp, hq, dh)[:, :length]
    lse = jnp.moveaxis(m + jnp.log(denom), -1, 2).reshape(bt, lp, hq)[:, :length]
    return o.astype(q.dtype), lse

def to_strided(t, d):
    b, s = t.shape[0], t.shape[1]
    t = t.reshape((b, s // d, d) + t.shape[2:])
    t = jnp.swapaxes(t, 1, 2)
    return t.reshape((b * d, s // d) + t.shape[3:])

def from_strided(t, d, batch):
    length = t.shape[1]
    t = t.reshape((batch, d) + t.shape[1:])
    t = jnp.swapaxes(t, 1, 2)
    return t.reshape((batch, length * d) + t.shape[3:])

def dilated_attention(q, k, v):
    batch = q.shape[0]
    outs, lses = [], []
    for g, (w, d) in enumerate(DIL_PAIRS):
        sl = slice(g * DIL_HEADS, (g + 1) * DIL_HEADS)
        o, l = band_attention(to_strided(q[:, :, sl], d), to_strided(k[:, :, sl], d),
                              to_strided(v[:, :, sl], d), w // (2 * d), DIL_BLOCK)
        outs.append(from_strided(o, d, batch))
        lses.append(from_strided(l, d, batch))
    alpha = jax.nn.softmax(jnp.stack(lses), axis=0)
    o = jnp.stack(outs).astype(jnp.float32)
    return jnp.einsum('gbsh,gbshd->bshd', alpha, o).astype(q.dtype)

def token_mixer(h, positions, w_in, sink_logits, w_branch_a, w_branch_b, w_out):
    b, s, _ = h.shape
    p = h @ w_in
    qa, ka, va, qb, kb, vb, ga, gb = jnp.split(p, IN_SPLITS, axis=-1)
    heads = lambda t, n: t.reshape(b, s, n, HEAD_DIM)
    o_a = dilated_attention(rope(heads(qa, DIL_TOTAL_HEADS), positions),
                            rope(heads(ka, DIL_TOTAL_HEADS), positions),
                            heads(va, DIL_TOTAL_HEADS))
    o_b, _ = band_attention(rope(heads(qb, SWA_Q_HEADS), positions),
                            rope(heads(kb, SWA_KV_HEADS), positions),
                            heads(vb, SWA_KV_HEADS), SWA_WINDOW, SWA_BLOCK, sink_logits)
    y_a = o_a.reshape(b, s, -1) @ w_branch_a
    y_b = o_b.reshape(b, s, -1) @ w_branch_b
    merged = jax.nn.sigmoid(ga) * y_a + jax.nn.sigmoid(gb) * y_b
    return merged @ w_out

def hier_moe(h, w_group, b_group, w_route, b_route, w_gate, w_up, w_down):
    b, s, d = h.shape
    n = b * s
    t = h.reshape(n, d)
    glog = (t @ w_group).astype(jnp.float32) + b_group
    gprob = jax.nn.softmax(glog, axis=-1)
    gsel = jnp.argmax(glog, axis=-1)
    gw = jnp.take_along_axis(gprob, gsel[:, None], axis=1)[:, 0]
    elog = ((t @ w_route).astype(jnp.float32) + b_route).reshape(n, MOE_GROUPS, EXPERTS_PER_GROUP)
    elog = jnp.take_along_axis(elog, gsel[:, None, None], axis=1)[:, 0]
    topw, topi = lax.top_k(jax.nn.softmax(elog, axis=-1), TOP_K)
    topw = topw / jnp.sum(topw, axis=-1, keepdims=True) * gw[:, None]
    expert = gsel[:, None] * EXPERTS_PER_GROUP + topi
    a = n * TOP_K
    flat_e = expert.reshape(a).astype(jnp.int32)
    flat_tok = jnp.repeat(jnp.arange(n, dtype=jnp.int32), TOP_K)
    order = jnp.argsort(flat_e, stable=True)
    se = flat_e[order]
    counts = jnp.zeros((N_EXPERTS,), jnp.int32).at[flat_e].add(1)
    starts = jnp.cumsum(counts) - counts
    padded = (counts + MOE_BLOCK - 1) // MOE_BLOCK * MOE_BLOCK
    pend = jnp.cumsum(padded)
    pstarts = pend - padded
    dest_sorted = pstarts[se] + (jnp.arange(a, dtype=jnp.int32) - starts[se])
    dest = jnp.zeros((a,), jnp.int32).at[order].set(dest_sorted)
    rows = (-(-a // MOE_BLOCK) + N_EXPERTS) * MOE_BLOCK
    nblk = rows // MOE_BLOCK
    row_tok = jnp.full((rows,), n, jnp.int32).at[dest].set(flat_tok)
    t_pad = jnp.concatenate([t, jnp.zeros((1, d), t.dtype)], axis=0)
    x_rows = t_pad[row_tok].reshape(nblk, MOE_BLOCK, d)
    blk_e = jnp.clip(jnp.searchsorted(pend, jnp.arange(nblk) * MOE_BLOCK, side='right'), 0, N_EXPERTS - 1)

    def expert_block(args):
        xb, e = args
        return (jax.nn.silu(xb @ w_gate[e]) * (xb @ w_up[e])) @ w_down[e]

    y_rows = lax.map(expert_block, (x_rows, blk_e)).reshape(rows, d)
    picked = y_rows[dest].reshape(n, TOP_K, d)
    out = jnp.einsum('nk,nkd->nd', topw.astype(h.dtype), picked)
    return out.reshape(b, s, d)

def setup_inputs(seed: int = 0) -> dict:
    key = jax.random.key(seed)
    ks = jax.random.split(key, 20)
    f32 = jnp.float32
    nrm = lambda k, shape, fan: jax.random.normal(k, shape, f32) * (fan ** -0.5)
    L, D = DEPTH, D_MODEL
    return {
        'x': jax.random.normal(ks[0], (BATCH, SEQ, D), f32),
        'c': jax.random.normal(ks[1], (BATCH, D), f32),
        'positions': jnp.broadcast_to(jnp.arange(SEQ, dtype=jnp.int32), (BATCH, SEQ)),
        'w_ada': nrm(ks[2], (L, D, N_MOD * D), D),
        'b_ada': 0.02 * jax.random.normal(ks[3], (L, N_MOD * D), f32),
        'g_mix': 1.0 + 0.05 * jax.random.normal(ks[4], (L, D), f32),
        'w_in': nrm(ks[5], (L, D, IN_WIDTH), D),
        'sink_logits': jax.random.normal(ks[6], (L, SWA_Q_HEADS), f32),
        'w_branch_a': nrm(ks[7], (L, DIL_HEADS * HEAD_DIM, D), DIL_HEADS * HEAD_DIM),
        'w_branch_b': nrm(ks[8], (L, SWA_QW, D), SWA_QW),
        'w_out': nrm(ks[9], (L, D, D), D),
        'g_ffn': 1.0 + 0.05 * jax.random.normal(ks[10], (L, D), f32),
        'w_group': nrm(ks[11], (L, D, MOE_GROUPS), D),
        'b_group': 0.01 * jax.random.normal(ks[12], (L, MOE_GROUPS), f32),
        'w_route': nrm(ks[13], (L, D, N_EXPERTS), D),
        'b_route': 0.01 * jax.random.normal(ks[14], (L, N_EXPERTS), f32),
        'w_expert_gate': nrm(ks[15], (L, N_EXPERTS, D, D_EXPERT), D),
        'w_expert_up': nrm(ks[16], (L, N_EXPERTS, D, D_EXPERT), D),
        'w_expert_down': nrm(ks[17], (L, N_EXPERTS, D_EXPERT, D), D_EXPERT),
        'g_final': 1.0 + 0.05 * jax.random.normal(ks[18], (D,), f32),
    }

def reference(x, c, positions, w_ada, b_ada, g_mix, w_in, sink_logits, w_branch_a, w_branch_b,
              w_out, g_ffn, w_group, b_group, w_route, b_route, w_expert_gate, w_expert_up,
              w_expert_down, g_final):
    cs = jax.nn.silu(c)
    for l in range(DEPTH):
        mod = cs @ w_ada[l] + b_ada[l]
        sh1, sc1, gt1, sh2, sc2, gt2 = jnp.split(mod, N_MOD, axis=-1)
        h = rms_norm(x, g_mix[l]) * (1.0 + sc1[:, None]) + sh1[:, None]
        x = x + gt1[:, None] * token_mixer(h, positions, w_in[l], sink_logits[l],
                                           w_branch_a[l], w_branch_b[l], w_out[l])
        h = rms_norm(x, g_ffn[l]) * (1.0 + sc2[:, None]) + sh2[:, None]
        x = x + gt2[:, None] * hier_moe(h, w_group[l], b_group[l], w_route[l], b_route[l],
                                        w_expert_gate[l], w_expert_up[l], w_expert_down[l])
    return rms_norm(x, g_final)


_drawn_inputs = setup_inputs


def setup_inputs(seed=0):
    import zlib

    import numpy as np

    out = dict(_drawn_inputs(seed))
    spreads = {}
    factors = {'sink_logits': 8.0, 'b_group': 3.189, 'b_route': 3.824}
    for name, (base, spread) in spreads.items():
        noise = np.random.default_rng([zlib.crc32(name.encode()), seed]).standard_normal(out[name].shape)
        drawn = base * np.exp(spread * noise) if base else spread * noise
        out[name] = __import__('jax').numpy.asarray(drawn.astype(out[name].dtype))
    for name, factor in factors.items():
        out[name] = (out[name] * factor).astype(out[name].dtype)
    return out
```

```python
import numpy as np
import concourse.bass as bass
from concourse import mybir
from contextlib import ExitStack

F32 = mybir.dt.float32
F32R = mybir.dt.float32r
BF16 = mybir.dt.bfloat16
F16 = mybir.dt.float16
I32 = mybir.dt.int32
ALU = mybir.AluOpType
ACT = mybir.ActivationFunctionType
AX = mybir.AxisListType
ds = bass.ds

P = 128
SEQ = 2048
D = 1024
KD = D // P
TT = SEQ // P
HD = 64
HALF = HD // 2
DILATIONS = (1, 4, 16)
DIL_HEADS = 4
SWA_HEADS = 8
SCALE = HD ** -0.5
EPS = 1e-6
NEG = -1e30
THETA = 10000.0
N_MOD = 6
E = 32
GROUPS = 4
PER_GROUP = E // GROUPS
DE = 512
KE = DE // P
BLK = 128
MAX_BLOCKS = SEQ * 2 // BLK + E
PAD_ROWS = P

PASSES = 8
PASS_COLS = 384
TILES_PER_GROUP = 2 * TT
PIECE = PASS_COLS // 2
SWA_T0 = 3 * TILES_PER_GROUP
STEPS = 4 * TILES_PER_GROUP
STAT = HD + 2

OUT_K = 6
GATE_COLS = KD * 2 * P + OUT_K * P
CHUNK = 512
CHUNKS = SEQ // CHUNK


def wait(eng, sem, n):
    if not (isinstance(n, int) and n <= 0):
        eng.wait_ge(sem, n)


class Chain:

    def __init__(self, eng, sem):
        self.eng, self.sem, self.n = eng, sem, 0

    def __call__(self, ins):
        ins.then_inc(self.sem, 1)
        self.n = self.n + 1
        return ins

    def join(self):
        wait(self.eng, self.sem, self.n)


def two_pi_parts():
    rest, parts = 2 * np.pi, []
    for bits in (8, 10, 24):
        scale = 2.0 ** (bits - 1 - np.floor(np.log2(rest)))
        parts.append(float(np.float32(np.floor(rest * scale) / scale)))
        rest -= parts[-1]
    return parts


def build(nc, A, out, debug=False):
    ctx = ExitStack()
    with ctx:
        body(nc, A, out, ctx, debug)


def body(nc, A, out, ctx, debug):
    kind = "ExternalOutput" if debug else "Internal"

    def dram(name, shape, dt=F32):
        return nc.dram_tensor(name, shape, dt, kind=kind).ap()

    o_dil = dram("o_dil", [3, SEQ, DIL_HEADS * STAT])
    o_swa = dram("o_swa", [SEQ, SWA_HEADS * HD])
    rows_d = dram("mod_rows", [5, D])
    oT_d = dram("oT_d", [P, OUT_K, SEQ])
    mT_d = dram("mT_d", [P, KD, SEQ])
    x1_d = dram("x1_d", [SEQ, D])
    h2_d = dram("h2_d", [SEQ + PAD_ROWS // 2, D])
    y_d = dram("y_d", [2 * SEQ + PAD_ROWS, D])

    class Plan:
        def __init__(self, at):
            self.at = at

        def __call__(self, name, shape, dt=F32):
            size = int(np.prod(shape[1:])) * {F32: 4, F32R: 4, I32: 4, BF16: 2, F16: 2}[dt]
            t = nc.alloc_sbuf_tensor_at("sb_" + name, shape, dt, offset=self.at)
            self.at += (size + 31) // 32 * 32
            return t

    base = nc.sbuf_base
    base = (base + 31) // 32 * 32
    keep = Plan(base)
    ident = keep("ident", [P, P])
    ones_row = keep("ones_row", [1, 2])
    A1 = keep("A1", [P, KD])
    B1 = keep("B1", [P, KD])
    hT = keep("hT", [P, KD, SEQ])
    after_hT = keep.at

    m0 = Plan(after_hT - KD * SEQ * 4)
    wada = [m0(f"wada{i}", [P, KD, CHUNK]) for i in range(4)]
    m0b = Plan(after_hT)
    c_col = m0b("c_col", [P, KD])
    c_sil = m0b("c_sil", [P, KD])
    ones = m0b("ones", [P, P])
    c_bc = m0b("c_bc", [P, KD, P])
    mod = m0b("mod", [P, N_MOD * D])
    b_bc = m0b("b_bc", [P, N_MOD * D])
    g_bc = m0b("g_bc", [P, 3, D])

    m1 = Plan(after_hT)
    xt = [m1(f"xt{c}", [P, D]) for c in range(2)]
    sq = m1("sq", [P, D])
    xn = m1("xn", [P, D])
    stat1 = m1("stat1", [P, 4])

    m2 = Plan(after_hT)
    w_raw = [m2(f"w_raw{c}", [P, PIECE]) for c in range(2)]
    w_hi = m2("w_hi", [P, 2 * KD, PASS_COLS], F32R)
    w_lo = m2("w_lo", [P, 2 * KD, PASS_COLS], F32R)
    h_hi = [m2(f"h_hi{c}", [P, KD, P], F32R) for c in range(2)]
    h_lo = [m2(f"h_lo{c}", [P, KD, P], F32R) for c in range(2)]
    kT_dil = m2("kT_dil", [P, SEQ + 2 * HD])
    v_dil = m2("v_dil", [P, TT + 1, P])
    kT_swa = m2("kT_swa", [P, SEQ + 2 * P])
    v_swa = m2("v_swa", [P, TT + 2, HD])
    qk_raw = m2("qk_raw", [P, 320])
    qk_tmp = m2("qk_tmp", [P, 320])
    qk_rot = m2("qk_rot", [P, 320])
    cos_t = m2("cos_t", [P, 3 * TT, HALF])
    sin_t = m2("sin_t", [P, 3 * TT, HALF])
    qst = [m2(f"qst{c}", [P, 4, P]) for c in range(2)]
    mask_dil = m2("mask_dil", [P, 4, 256], BF16)
    mask_swa = m2("mask_swa", [P, 3, 384], BF16)
    e_sb = [m2(f"e_sb{u}", [P, 2, 384]) for u in range(2)]
    eT = m2("eT", [P, 2, 384])
    o_row = [[m2(f"o_row{c}{u}", [P, 2, STAT]) for u in range(2)] for c in range(2)]
    mx = m2("mx", [P, 2])
    nm = m2("nm", [P, 2])
    snk = [[m2(f"snk{c}{u}", [P, 2]) for u in range(2)] for c in range(2)]
    esk = [[m2(f"esk{c}{u}", [P, 2]) for u in range(2)] for c in range(2)]
    rden = m2("rden", [P, 2])
    sink_bc = m2("sink_bc", [P, SWA_HEADS])
    nsink = m2("nsink", [P, SWA_HEADS])
    assert m2.at <= nc.sbuf_usable_end, (m2.at, nc.sbuf_usable_end)
    mt = Plan(after_hT + 2 * PIECE * 4)
    pos_i = mt("pos_i", [P, 3 * TT], I32)
    pos_f = mt("pos_f", [P, 3 * TT])
    invf = mt("invf", [P, HALF])
    ang = mt("ang", [P, 3 * TT, HALF])
    turn = mt("turn", [P, 3 * TT, HALF])

    m3 = Plan(after_hT)
    od = [m3(f"od{c}", [P, 3, DIL_HEADS * STAT]) for c in range(2)]
    ob = [m3(f"ob{c}", [P, SWA_HEADS * HD]) for c in range(2)]
    wsum = m3("wsum", [P, 3, DIL_HEADS * HD])
    oa = m3("oa", [P, DIL_HEADS * HD])
    oT = [m3(f"oT{c}", [P, OUT_K, P]) for c in range(2)]
    nmin = m3("nmin", [P, DIL_HEADS])
    wg = m3("wg", [P, 3, DIL_HEADS])
    wden = m3("wden", [P, 3, DIL_HEADS])
    dsum = m3("dsum", [P, DIL_HEADS])

    m4 = Plan(after_hT)
    x_hi = m4("x_hi", [P, KD, CHUNK], F32R)
    x_lo = m4("x_lo", [P, KD, CHUNK], F32R)
    o_hi = m4("o_hi", [P, OUT_K, CHUNK], F32R)
    o_lo = m4("o_lo", [P, OUT_K, CHUNK], F32R)
    o_in = m4("o_in", [P, OUT_K, CHUNK])
    g_raw = [m4(f"g_raw{j}", [P, GATE_COLS // 2]) for j in range(2)]
    g_hi = [m4(f"g_hi{c}", [P, GATE_COLS], F32R) for c in range(2)]
    g_lo = [m4(f"g_lo{c}", [P, GATE_COLS], F32R) for c in range(2)]
    sig = m4("sig", [P, 2, CHUNK])
    mg = [m4(f"mg{c}", [P, CHUNK]) for c in range(2)]
    assert m4.at <= nc.sbuf_usable_end, m4.at

    m5 = Plan(after_hT - KD * SEQ * 4)
    wo_raw = [m5(f"wo_raw{c}", [P, D]) for c in range(2)]
    wo_hi = m5("wo_hi", [P, KD, D], F32R)
    wo_lo = m5("wo_lo", [P, KD, D], F32R)
    gt1b = m5("gt1b", [P, D])
    A2b = m5("A2b", [P, D])
    B2b = m5("B2b", [P, D])
    m_in = [m5(f"m_in{c}", [P, KD, P]) for c in range(2)]
    m_hi = [m5(f"m_hi{c}", [P, KD, P], F32R) for c in range(2)]
    m_lo = [m5(f"m_lo{c}", [P, KD, P], F32R) for c in range(2)]
    x_in = [m5(f"x_in{c}", [P, D]) for c in range(2)]
    x1 = [m5(f"x1{c}", [P, D]) for c in range(2)]
    h2 = [m5(f"h2{c}", [P, D]) for c in range(2)]
    h2T = m5("h2T", [P, KD, P])
    sq2 = m5("sq2", [P, D])
    zero_rows = m5("zero_rows", [PAD_ROWS // 2, D])
    w_rt = m5("w_rt", [P, KD, GROUPS + E])
    st2 = m5("st2", [P, 8])
    sb_off_logits = m5.at
    logits = m5("logits", [P, TT, GROUPS + E])
    pair_w = m5("pair_w", [P, TT, 2])
    scatter_idx = m5("scatter_idx", [P, MAX_BLOCKS + 1], I32)
    gather_idx = m5("gather_idx", [P, MAX_BLOCKS + 1], I32)
    expert_of = m5("expert_of", [1, MAX_BLOCKS + 1], I32)
    ends = m5("ends", [1, E], I32)
    after_m5 = m5.at

    m6 = Plan(after_hT - KD * SEQ * 4)
    ug = lambda name, n, dt=F32: m6(name, [P, TT, n], dt)
    r_bias = m6("r_bias", [P, GROUPS + E])
    iota_e = m6("iota_e", [P, TT, E])
    iota_r = m6("iota_r", [P, P])
    iota_b = m6("iota_b", [P, MAX_BLOCKS])
    flat_id = m6("flat_id", [P, TT, 2])
    pad_id = m6("pad_id", [P, 2])
    tri = m6("tri", [P, P], BF16)
    all_ones = m6("all_ones", [P, P], BF16)
    gmax = ug("gmax", 1)
    geq = ug("geq", GROUPS)
    gsel = ug("gsel", GROUPS)
    gex = ug("gex", GROUPS)
    gsum = ug("gsum", 1)
    gidx = ug("gidx", 1)
    el = ug("el", E)
    eeq = ug("eeq", E)
    oh = [ug(f"oh{k}", E) for k in range(2)]
    top = [ug(f"top{k}", 1) for k in range(2)]
    eidx = ug("eidx", 1)
    ratio = ug("ratio", 1)
    rinv = ug("rinv", 1)
    both = ug("both", E, BF16)
    posn = ug("posn", E)
    prod = ug("prod", E)
    slot_f = ug("slot_f", 2)
    slot_i = ug("slot_i", 2, I32)
    lane_i = ug("lane_i", 2, I32)
    blk_i = ug("blk_i", 2, I32)
    lane_f = ug("lane_f", 2)
    blk_f = ug("blk_f", 2)
    cnt = m6("cnt", [P, E])
    cnt_i = m6("cnt_i", [P, E], I32)
    nblk = m6("nblk", [P, E])
    pend = m6("pend", [P, E])
    pbase = m6("pbase", [P, E])
    cmp_e = m6("cmp_e", [P, MAX_BLOCKS, E])
    e_f = m6("e_f", [P, MAX_BLOCKS])
    lane_oh = [m6(f"lane_oh{k}", [P, P], F16) for k in range(2)]
    blk_oh = [m6(f"blk_oh{k}", [P, 2, MAX_BLOCKS], F16) for k in range(2)]
    tab = m6("tab", [P, 2, MAX_BLOCKS])
    idx_f = m6("idx_f", [P, MAX_BLOCKS])

    m7 = Plan(m6.at)
    gu = m7("gu", [P, 2 * KD, 2 * DE])
    dn = m7("dn", [P, 2 * KE, D])
    assert m7.at <= sb_off_logits, (m7.at, sb_off_logits)
    m8 = Plan(after_hT - KD * SEQ * 4)
    xg = m8("xg", [P, D])
    xTs = m8("xTs", [P, KD, P])
    hg = m8("hg", [P, DE])
    hs = m8("hs", [P, DE])
    hTs = m8("hTs", [P, KE, P])
    y_sb = m8("y_sb", [P, D])
    gi = m8("gi", [P, 1], I32)
    si = m8("si", [P, 1], I32)
    assert m8.at <= m6.at
    m9 = Plan(after_hT - KD * SEQ * 4)
    yp = [m9(f"yp{c}", [P, 2, D]) for c in range(2)]
    xl = [m9(f"xl{c}", [P, D]) for c in range(2)]
    acc = [m9(f"acc{c}", [P, D]) for c in range(2)]
    sq3 = m9("sq3", [P, D])
    gt2b = m9("gt2b", [P, D])
    gfb = m9("gfb", [P, D])
    st3 = m9("st3", [P, 8])

    bank = [ctx.enter_context(nc.psum_tensor(f"bank{i}", [P, 512], F32)) for i in range(3)]
    S_ps = ctx.enter_context(nc.psum_tensor("S_ps", [P, 2, 512], F32))
    E_ps = ctx.enter_context(nc.psum_tensor("E_ps", [P, 2, 512], F32))
    O_ps = ctx.enter_context(nc.psum_tensor("O_ps", [P, 512], F32))

    PS = [bank[0], bank[1], bank[2], S_ps[:, 0, :], S_ps[:, 1, :], E_ps[:, 0, :], E_ps[:, 1, :], O_ps]

    sems = {}

    def sem(name):
        if name not in sems:
            sems[name] = ctx.enter_context(nc.semaphore(name))
        return sems[name]

    inv_freq = (np.float32(THETA) ** (-np.arange(HALF, dtype=np.float32) * np.float32(2.0 / HD))).astype(np.float32)
    PI2 = two_pi_parts()
    MAGIC = 1.5 * 2.0 ** 23

    block = ctx.enter_context(nc.Block())

    def dilation(g):
        return DILATIONS[g] if g < 3 else 1

    def tile_of(T):
        return T % TT

    def first_token(g, t):
        d = dilation(g)
        per = TT // d
        return (t % per) * (P * d) + t // per

    def mask_index(g, t):
        if g == 2:
            return 3
        per = TT // dilation(g)
        m = t % per
        return (m + per - 1) // per + m // (per - 1)

    def unit(g, T, u):
        return T if g < 3 else 2 * T - SWA_T0 + u

    def units(g):
        return (0,) if g < 3 else (0, 1)

    def weight_row(n):
        return ((n // TT) % 2) * KD + (n % TT) // 2

    def group_of(T):
        return min(max(T, 0) // TILES_PER_GROUP, 3)

    def schedule(eng, step):
        def straight(T):
            gs = [group_of(x) if 0 <= x < STEPS else None for x in (T + 1, T, T - 1, T - 2, T - 3)]
            step(T, T % 2, gs, T < STEPS - TT)

        def looped(g, first, last, loads):
            with eng.Fori(first // 2, last // 2) as i:
                for c in range(2):
                    step(2 * i + c, c, [g] * 5, loads)

        for g in range(4):
            T0 = g * TILES_PER_GROUP
            for T in range(T0, T0 + 4):
                straight(T)
            end = T0 + TILES_PER_GROUP - 2
            if g < 3:
                looped(g, T0 + 4, end, True)
            else:
                looped(g, T0 + 4, STEPS - TT - 2, True)
                straight(STEPS - TT - 2)
                straight(STEPS - TT - 1)
                looped(g, STEPS - TT, end, False)
            for T in range(end, T0 + TILES_PER_GROUP):
                straight(T)
        for T in range(STEPS, STEPS + 3):
            straight(T)

    @block.sync
    def _(sp):
        sp.dma_start(c_col[:], A["c"].rearrange("a (k p) -> p (a k)", p=P), allow_slow_non_contiguous=True).then_inc(sem("c_in"), 16)
        wv = A["w_ada"].rearrange("a (k p) n -> p (a k) n", p=P)
        for j in range(N_MOD * D // CHUNK):
            wait(sp, sem("mod_mm"), j - 3)
            sp.dma_start(wada[j % 4][:], wv[:, :, j * CHUNK:(j + 1) * CHUNK]).then_inc(sem(f"wada_in{j % 4}"), 16)
            if j == 1:
                sp.dma_start(b_bc[:], A["b_ada"][0:1, :].broadcast_to([P, N_MOD * D])).then_inc(sem("b_in"), 16)
                for n, g in enumerate(("g_mix", "g_ffn", "g_final")):
                    src = A[g] if g != "g_final" else A[g].rearrange("(a n) -> a n", a=1)
                    sp.dma_start(g_bc[:, n, :], src[0:1, :].broadcast_to([P, D])).then_inc(sem("g_in"), 16)
        sp.wait_ge(sem("mod_rows_ready"), 1)
        for n, src in enumerate((mod[0:1, 2 * D:3 * D], mod[0:1, 5 * D:6 * D], mod[0:1, 4 * D:5 * D], mod[0:1, 3 * D:4 * D], g_bc[0:1, 2, :])):
            sp.dma_start(rows_d[n:n + 1, :], src).then_inc(sem("rows_out"), 16)
        sp.wait_ge(sem("rows_out"), 80)
        sp.wait_ge(sem("cols_ready"), 1)
        xv = A["x"].rearrange("a (t p) n -> p (a t) n", p=P)
        with sp.Fori(0, TT // 2) as i:
            for c in range(2):
                sp.wait_ge(sem(f"x_free{c}"), i + 1)
                sp.dma_start(xt[c][:], xv[:, ds(2 * i + c, 1), :].rearrange("p a n -> p (a n)")).then_inc(sem(f"x_in{c}"), 16)
        sp.wait_ge(sem("h_all"), TT + 1)
        pos = A["positions"]
        sp.dma_start(pos_i[:, 0:TT], pos.rearrange("a (t i) -> i (a t)", i=P), allow_slow_non_contiguous=True).then_inc(sem("pos_in"), 16)
        for r in range(4):
            sp.dma_start(pos_i[:, TT + 4 * r:TT + 4 * r + 4], pos.rearrange("a (b i r) -> r i (a b)", i=P, r=4)[r], allow_slow_non_contiguous=True).then_inc(sem("pos_in"), 16)
        sp.dma_start(pos_i[:, 2 * TT:3 * TT], pos.rearrange("a (i r) -> i (a r)", i=P)).then_inc(sem("pos_in"), 16)
        sp.dma_start(sink_bc[:], A["sink_logits"][0:1, :].broadcast_to([P, SWA_HEADS])).then_inc(sem("sink_in"), 16)

        wq = A["w_qkv"].rearrange("n (k p) m -> p n k m", p=P)

        def piece(n, c):
            wait(sp, sem("w_lo_ready"), n - 1)
            t = n % TT
            sp.dma_start(w_raw[c][:].rearrange("p (a b m) -> p a b m", a=1, b=1), wq[:, ds(n // TT, 1), ds(t // 2, 1), c * PIECE:(c + 1) * PIECE]).then_inc(sem(f"w_in{c}"), 16)

        for n in range(TT + 2):
            if n == 0:
                sp.wait_ge(sem("angles_ready"), 1)
            piece(n, n % 2)

        def step(T, c, gs, loads):
            g = gs[4]
            if g is not None:
                S = T - 3
                s, t = (S // TT) % 2, tile_of(S)
                tok = first_token(g, t)
                for u in units(g):
                    sp.wait_ge(sem("o_done"), unit(g, S, u) + 1)
                    if g < 3:
                        d = dilation(g)
                        dst = o_dil[g:g + 1, ds(tok, P, step=d), ds(s * (2 * STAT), 2 * STAT)]
                        src = o_row[1 - c][u][:].rearrange("p h m -> p (h m)")
                        dst = dst.rearrange("a p m -> (a p) m")
                    else:
                        dst = o_swa[ds(tok, P), ds(s * 256 + u * 128, 128)].rearrange("p (h m) -> p h m", h=2)
                        src = o_row[1 - c][u][:, :, 0:HD]
                    sp.dma_start(dst, src).then_inc(sem(f"o_out{1 - c}{u}"), 16)
            if loads and not (isinstance(T, int) and T + TT + 2 >= PASSES * TT):
                piece(T + TT + 2, c)

        schedule(sp, step)
        for c in range(2):
            sp.wait_ge(sem(f"o_out{c}0"), 16 * STEPS // 2)
            sp.wait_ge(sem(f"o_out{c}1"), 16 * TILES_PER_GROUP // 2)
        odv = o_dil.rearrange("g (t p) m -> p t g m", p=P)
        obv = o_swa.rearrange("(t p) m -> p t m", p=P)

        def merge_in(t, c):
            sp.dma_start(od[c][:], odv[:, ds(t, 1)].rearrange("p a g m -> p (a g) m")).then_inc(sem(f"od_in{c}"), 16)
            sp.dma_start(ob[c][:], obv[:, ds(t, 1)].rearrange("p a m -> p (a m)")).then_inc(sem(f"od_in{c}"), 16)

        def merge_out(t, c):
            sp.wait_ge(sem("oT_ready"), t + 2)
            sp.dma_start(oT_d[:, :, ds(t * P, P)], oT[c][:]).then_inc(sem(f"oT_out{c}"), 16)

        for c in range(2):
            sp.sem_inc(sem(f"oT_out{c}"), 16)
            merge_in(c, c)
        with sp.Fori(0, TT // 2 - 1) as i:
            for c in range(2):
                merge_out(2 * i + c, c)
                merge_in(2 * i + c + 2, c)
        for c in range(2):
            merge_out(TT - 2 + c, c)
        for c in range(2):
            sp.wait_ge(sem(f"oT_out{c}"), 16 * (TT // 2 + 1))

        gv = A["w_gb"]

        def gate_piece(tile, j, last_use):
            wait(sp, sem("g_lo_ready"), last_use)
            cols = slice(j * (GATE_COLS // 2), (j + 1) * (GATE_COLS // 2))
            sp.dma_start(g_raw[j][:], gv[ds(tile, 1), :, cols].rearrange("a p m -> (a p) m")).then_inc(sem(f"g_in{j}"), 16)

        for j in range(2):
            gate_piece(0, j, 0)
        with sp.Fori(0, CHUNKS) as q:
            sp.wait_ge(sem("o_lo_ready"), q + 1)
            sp.dma_start(o_in[:], oT_d[:, :, ds(q * CHUNK, CHUNK)]).then_inc(sem("o_in"), 16)
            with sp.Fori(0, KD // 2) as i:
                for c in range(2):
                    for j in range(2):
                        gate_piece((2 * i + c + 1) % KD, j, 2 * (KD * q + 2 * i + c) + j + 1)

        wov = A["w_out"].rearrange("a (k p) n -> p (a k) n", p=P)
        sp.wait_ge(sem("merged"), CHUNKS * KD)
        sp.wait_ge(sem("g_lo_ready"), 2 * CHUNKS * KD + 2)
        for c in range(2):
            sp.wait_ge(sem(f"mT_out{c}"), 16 * (CHUNKS * KD // 2 + 1))
        for k in range(KD):
            wait(sp, sem("wo_lo_ready"), k - 1)
            sp.dma_start(wo_raw[k % 2][:], wov[:, k, :]).then_inc(sem(f"w_in{k % 2}"), 16)
            if k == 1:
                for n, (t, row) in enumerate(((gt1b, 0), (A2b, 2), (B2b, 3))):
                    sp.dma_start(t[:], rows_d[row:row + 1, :].broadcast_to([P, D])).then_inc(sem("rows_in"), 16)
                sp.dma_start(w_rt[:], A["w_rt"].rearrange("(k p) n -> p k n", p=P)).then_inc(sem("w_rt_in"), 16)
                sp.wait_ge(sem("zero_rows"), 1)
                sp.dma_start(h2_d[SEQ:SEQ + PAD_ROWS // 2, :], zero_rows[:]).then_inc(sem("pads_out"), 16)

        def tile_in(t, c):
            sp.dma_start(m_in[c][:], mT_d[:, :, ds(t * P, P)]).then_inc(sem(f"m_in{c}"), 16)
            sp.dma_start(x_in[c][:], xv[:, ds(t, 1), :].rearrange("p a n -> p (a n)")).then_inc(sem(f"x_in{c}"), 16)

        def tile_out(t, c):
            sp.wait_ge(sem("h2_ready"), t + 1)
            sp.dma_start(x1_d[ds(t * P, P), :], x1[c][:]).then_inc(sem(f"x1_out{c}"), 16)
            sp.dma_start(h2_d[ds(t * P, P), :], h2[c][:]).then_inc(sem(f"x1_out{c}"), 16)

        tile_in(0, 0)
        tile_in(1, 1)
        with sp.Fori(0, TT // 2 - 1) as i:
            for c in range(2):
                tile_out(2 * i + c, c)
                tile_in(2 * i + c + 2, c)
        for c in range(2):
            tile_out(TT - 2 + c, c)
        for c in range(2):
            sp.wait_ge(sem(f"x1_out{c}"), 32 * (TT // 2))
        sp.wait_ge(sem("pads_out"), 16)
        sp.sem_inc(sem("h2_stored"), 1)

        sp.wait_ge(sem("logits_ready"), TT)
        sp.dma_start(r_bias[:], A["b_rt"][0:1, :].broadcast_to([P, GROUPS + E])).then_inc(sem("r_bias_in"), 16)
        wg_v = A["w_expert_gate"].rearrange("a e (k p) n -> p (a e) k n", p=P)
        wu_v = A["w_expert_up"].rearrange("a e (k p) n -> p (a e) k n", p=P)
        wd_v = A["w_expert_down"].rearrange("a e (k p) n -> p (a e) k n", p=P)

        def expert_in(e, c, free):
            if free is not None:
                sp.wait_ge(sem("gu_done"), free)
            sp.dma_start(gu[:, c * KD:(c + 1) * KD, 0:DE], wg_v[:, ds(e, 1)].rearrange("p a k n -> p (a k) n")).then_inc(sem(f"gu_in{c}"), 16)
            sp.dma_start(gu[:, c * KD:(c + 1) * KD, DE:2 * DE], wu_v[:, ds(e, 1)].rearrange("p a k n -> p (a k) n")).then_inc(sem(f"gu_in{c}"), 16)
            if free is not None:
                sp.wait_ge(sem("down_done"), free)
            sp.dma_start(dn[:, c * KE:(c + 1) * KE, :], wd_v[:, ds(e, 1)].rearrange("p a k n -> p (a k) n")).then_inc(sem(f"dn_in{c}"), 16)

        sp.sem_inc(sem("gu_in1"), 32)
        sp.sem_inc(sem("dn_in1"), 16)
        expert_in(0, 0, None)
        expert_in(1, 1, None)
        sp.wait_ge(sem("tables_ready"), 1)
        with sp.Fori(1, E // 2) as i:
            for c in range(2):
                last_block = sp.value_load(ends[0:1, ds(2 * i + c - 2, 1)], min_val=1, max_val=MAX_BLOCKS)
                expert_in(2 * i + c, c, last_block)

        sp.wait_ge(sem("experts_done"), 1)
        for n, (t, row) in enumerate(((gt2b, 1), (gfb, 4))):
            sp.dma_start(t[:], rows_d[row:row + 1, :].broadcast_to([P, D])).then_inc(sem("rows2_in"), 16)
        yv = y_d[0:2 * SEQ, :].rearrange("(t p two) n -> p t two n", p=P, two=2)
        x1v = x1_d.rearrange("(t p) n -> p t n", p=P)
        ov = out.rearrange("a (t p) n -> p (a t) n", p=P)

        def last_in(t, c):
            sp.dma_start(yp[c][:], yv[:, ds(t, 1)].rearrange("p a two n -> p (a two) n")).then_inc(sem(f"yp_in{c}"), 16)
            sp.dma_start(xl[c][:], x1v[:, ds(t, 1)].rearrange("p a n -> p (a n)")).then_inc(sem(f"yp_in{c}"), 16)

        def last_out(t, c):
            sp.wait_ge(sem("out_ready"), t + 1)
            sp.dma_start(ov[:, ds(t, 1), :].rearrange("p a n -> p (a n)"), acc[c][:]).then_inc(sem(f"out_stored{c}"), 16)

        for c in range(2):
            sp.sem_inc(sem(f"out_stored{c}"), 16)
            last_in(c, c)
        with sp.Fori(0, TT // 2 - 1) as i:
            for c in range(2):
                last_out(2 * i + c, c)
                last_in(2 * i + c + 2, c)
        for c in range(2):
            last_out(TT - 2 + c, c)
        for c in range(2):
            sp.wait_ge(sem(f"out_stored{c}"), 16 * (TT // 2 + 1))

    @block.gpsimd
    def _(pool):
        ch = Chain(pool, sem("pool_chain"))
        ch(nc.gpsimd.memset(ident[:], 0.0))
        ch(nc.gpsimd.memset(ones_row[:], 1.0))
        ch(nc.gpsimd.memset(ones[:], 1.0))
        ch.join()
        nc.gpsimd.affine_select(out=ident[:], in_=ident[:], compare_op=ALU.not_equal, fill=1.0, base=0,
                                pattern=[[-1, P]], channel_multiplier=1).then_inc(sem("ident_ready"), 1)
        pool.wait_ge(sem("h_all"), TT + 1)
        for k in range(HALF):
            last = nc.gpsimd.memset(invf[:, k:k + 1], float(inv_freq[k]))
        last.then_inc(sem("invf_ready"), 1)
        for q in qst:
            ch(nc.gpsimd.memset(q[:], 0.0))
        for t, lo, hi in ((kT_dil, 0, HD), (kT_dil, HD + SEQ, 2 * HD + SEQ), (kT_swa, 0, P), (kT_swa, P + SEQ, 2 * P + SEQ)):
            ch(nc.gpsimd.memset(t[:, lo:hi], 0.0))
        ch(nc.gpsimd.memset(v_dil[0:HD, 0, :], 0.0))
        ch.join()
        ch(nc.gpsimd.memset(v_dil[HD:P, TT, :], 0.0))
        ch.join()
        ch(nc.gpsimd.memset(v_swa[:, 0, :], 0.0))
        ch(nc.gpsimd.memset(v_swa[:, TT + 1, :], 0.0))
        for m, w, var in ((mask_dil, HD, 4), (mask_swa, P, 3)):
            n = P + 2 * w
            ch(nc.gpsimd.memset(m[:], 0.0))
            ch.join()
            for v in range(var):
                cuts = [(1, -1, 0), (-1, 1, 2 * w)]
                if v in (0, 3):
                    cuts.append((1, 0, -w))
                if v in (2, 3):
                    cuts.append((-1, 0, P + w - 1))
                for step_c, step_i, b in cuts:
                    ch(nc.gpsimd.affine_select(out=m[:, v, :], in_=m[:, v, :], compare_op=ALU.is_ge, fill=NEG, base=b,
                                               pattern=[[step_c, n]], channel_multiplier=step_i))
                    ch.join()
        nc.gpsimd.memset(mx[:], 0.0).then_inc(sem("attn_consts"), 1)

        def tile_src(g, T):
            tok = first_token(g, tile_of(T))
            return hT[:, :, ds(tok, P, step=dilation(g))]

        def lower_tile(T, c, g):
            pool.wait_ge(sem("h_hi_ready"), T + 1)
            nc.gpsimd.tensor_tensor(h_lo[c][:], tile_src(g, T), h_hi[c][:].bitcast(F32), ALU.subtract).then_inc(sem("h_lo_ready"), 1)

        def lower_piece(n, c):
            pool.wait_ge(sem("w_hi_ready"), n + 1)
            k = weight_row(n)
            cols = slice(c * PIECE, (c + 1) * PIECE)
            raw = w_raw[c][:].rearrange("p (a m) -> p a m", a=1)
            nc.gpsimd.tensor_tensor(w_lo[:, ds(k, 1), cols], raw, w_hi[:, ds(k, 1), cols].bitcast(F32), ALU.subtract).then_inc(sem("w_lo_ready"), 1)

        for n in range(TT):
            lower_piece(n, n % 2)
        lower_tile(0, 0, 0)

        def step(T, c, gs, loads):
            if gs[0] is not None:
                lower_tile(T + 1, 1 - c, gs[0])
            if loads and not (isinstance(T, int) and T + TT >= PASSES * TT):
                lower_piece(T + TT, c)

        schedule(pool, step)

        def lower_gate(n, c):
                for j in range(2):
                    pool.wait_ge(sem("g_hi_ready"), 2 * n + j + 1)
                    cols = slice(j * (GATE_COLS // 2), (j + 1) * (GATE_COLS // 2))
                    nc.gpsimd.tensor_tensor(g_lo[c][:, cols], g_raw[j][:], g_hi[c][:, cols].bitcast(F32), ALU.subtract).then_inc(sem("g_lo_ready"), 1)

        lower_gate(0, 0)
        with pool.Fori(0, CHUNKS * KD // 2) as i:
            for c in range(2):
                lower_gate(2 * i + c + 1, 1 - c)
        pool.wait_ge(sem("wo_hi_ready"), 1)
        nc.gpsimd.memset(zero_rows[:], 0.0).then_inc(sem("zero_rows"), 1)
        for k in range(KD):
            pool.wait_ge(sem("wo_hi_ready"), k + 1)
            nc.gpsimd.tensor_tensor(wo_lo[:, k, :], wo_raw[k % 2][:], wo_hi[:, k, :].bitcast(F32), ALU.subtract).then_inc(sem("wo_lo_ready"), 1)
        with pool.Fori(0, TT // 2) as i:
            for c in range(2):
                pool.wait_ge(sem("m_hi_ready"), 2 * i + c + 1)
                nc.gpsimd.tensor_tensor(m_lo[c][:], m_in[c][:], m_hi[c][:].bitcast(F32), ALU.subtract).then_inc(sem("m_lo_ready"), 1)

        pool.wait_ge(sem("logits_ready"), TT)
        exact = dict(allow_small_or_imprecise_dtypes=True)
        ch(nc.gpsimd.iota(iota_e[:], pattern=[[0, TT], [1, E]], base=0, channel_multiplier=0, **exact))
        ch(nc.gpsimd.iota(iota_r[:], pattern=[[1, P]], base=0, channel_multiplier=0, **exact))
        ch(nc.gpsimd.iota(iota_b[:], pattern=[[1, MAX_BLOCKS]], base=0, channel_multiplier=0, **exact))
        ch(nc.gpsimd.iota(flat_id[:], pattern=[[2 * P, TT], [1, 2]], base=-SEQ, channel_multiplier=2, **exact))
        ch(nc.gpsimd.iota(pad_id[:, 0:1], pattern=[[0, 1]], base=2 * SEQ, channel_multiplier=1, **exact))
        ch(nc.gpsimd.iota(pad_id[:, 1:2], pattern=[[0, 1]], base=SEQ - 2 * SEQ, channel_multiplier=-1, **exact))
        ch(nc.gpsimd.memset(all_ones[:], 1.0))
        ch(nc.gpsimd.memset(tri[:], 1.0))
        ch.join()
        nc.gpsimd.affine_select(out=tri[:], in_=tri[:], compare_op=ALU.is_gt, fill=0.0, base=0,
                                pattern=[[1, P]], channel_multiplier=-1).then_inc(sem("route_consts"), 1)

        pool.wait_ge(sem("tables_ready"), 1)
        pool.wait_ge(sem("h2_stored"), 1)
        total = pool.value_load(ends[0:1, E - 1:E], min_val=E, max_val=MAX_BLOCKS)

        def gather_block(g):
            nc.gpsimd.tensor_copy(gi[:], gather_idx[:, ds(g, 1)]).then_inc(sem("gi_ready"), 1)
            pool.wait_ge(sem("gi_ready"), g + 1)
            pool.sem_inc(sem("row_dmas"), 1)
            nc.gpsimd.indirect_dma_start(xg[:], None, h2_d, bass.IndirectOffsetOnAxis(ap=gi[:, 0:1], axis=0)).then_inc(sem("xg_in"), 16)

        def scatter_block(g):
            nc.gpsimd.tensor_copy(si[:], scatter_idx[:, ds(g, 1)]).then_inc(sem("si_ready"), 1)
            pool.wait_ge(sem("si_ready"), g + 1)
            pool.wait_ge(sem("y_ready"), g + 2)
            pool.sem_inc(sem("row_dmas"), 1)
            nc.gpsimd.indirect_dma_start(y_d, bass.IndirectOffsetOnAxis(ap=si[:, 0:1], axis=0), y_sb[:], None).then_inc(sem("y_out"), 16)

        pool.sem_inc(sem("y_free"), 1)
        gather_block(0)
        pool.wait_ge(sem("xgT_done"), 1)
        gather_block(1)
        with pool.Fori(1, total) as g:
            pool.wait_ge(sem("xgT_done"), g + 1)
            gather_block(g + 1)
            scatter_block(g - 1)
            pool.wait_ge(sem("y_out"), 16 * g)
            pool.sem_inc(sem("y_free"), 1)
        scatter_block(total - 1)
        pool.wait_ge(sem("y_out"), 16 * total)
        pool.sem_inc(sem("experts_done"), 1)

    @block.scalar
    def _(act):
        ch = Chain(act, sem("act_chain"))
        act.wait_ge(sem("c_in"), 16)
        nc.scalar.activation(c_sil[:], c_col[:], ACT.Silu).then_inc(sem("c_silu"), 1)
        act.sem_inc(sem("x_free0"), 1)
        act.sem_inc(sem("x_free1"), 1)
        with act.Fori(0, TT // 2) as i:
            for c in range(2):
                act.wait_ge(sem(f"x_in{c}"), 16 * (i + 1))
                nc.scalar.activation(sq[:], xt[c][:], ACT.Square, accum_out=stat1[:, 0:1]).then_inc(sem("sumsq"), 1)
                act.wait_ge(sem("meansq"), 2 * i + c + 1)
                nc.scalar.activation(stat1[:, 2:3], stat1[:, 1:2], ACT.Sqrt).then_inc(sem("rms"), 1)
                act.wait_ge(sem("rstd"), 2 * i + c + 1)
                act.wait_ge(sem("xn_used"), 2 * i + c + 1)
                nc.scalar.activation(xn[:], xt[c][:], ACT.Copy, scale=stat1[:, 3:4]).then_inc(sem("xn_ready"), 1)
                act.wait_ge(sem("xn_ready"), 2 * i + c + 1)
                act.sem_inc(sem(f"x_free{c}"), 1)
        act.wait_ge(sem("reduced"), 1)
        nc.scalar.activation(sin_t[:], ang[:], ACT.Sin)
        act.wait_ge(sem("reduced"), 2)
        nc.scalar.activation(cos_t[:], turn[:], ACT.Sin).then_inc(sem("angles_ready"), 1)

        def raise_tile(T, c, g):
            tok = first_token(g, tile_of(T))
            nc.scalar.activation(h_hi[c][:], hT[:, :, ds(tok, P, step=dilation(g))], ACT.Copy).then_inc(sem("h_hi_ready"), 1)

        def raise_piece(n, c):
            act.wait_ge(sem(f"w_in{c}"), 16 * (n // 2 + 1))
            k = weight_row(n)
            raw = w_raw[c][:].rearrange("p (a m) -> p a m", a=1)
            nc.scalar.activation(w_hi[:, ds(k, 1), c * PIECE:(c + 1) * PIECE], raw, ACT.Copy).then_inc(sem("w_hi_ready"), 1)

        act.wait_ge(sem("attn_consts"), 1)
        act.wait_ge(sem("angles_ready"), 1)
        for n in range(TT):
            raise_piece(n, n % 2)
        raise_tile(0, 0, 0)

        def step(T, c, gs, loads):
            g1 = gs[2]
            if g1 is not None:
                act.wait_ge(sem("proj_done"), T)
                wait(act, sem("rot_done"), T - 1)
                t = tile_of(T - 1)
                src = bank[1 - c]
                nq = 256 if g1 < 3 else 320
                nc.scalar.activation(qk_raw[:, 0:nq], src[:, 0:nq], ACT.Copy)
                if g1 < 3:
                    nc.scalar.activation(v_dil[HD:P, ds(t, 1), :], src[0:HD, 256:384].rearrange("p (a m) -> p a m", a=1), ACT.Copy)
                    last = nc.scalar.activation(v_dil[0:HD, ds(t + 1, 1), :], src[HD:P, 256:384].rearrange("p (a m) -> p a m", a=1), ACT.Copy)
                else:
                    last = nc.scalar.activation(v_swa[:, ds(t + 1, 1), :], src[:, 320:384].rearrange("p (a m) -> p a m", a=1), ACT.Copy)
                last.then_inc(sem("proj_evicted"), 1)
            if gs[0] is not None:
                raise_tile(T + 1, 1 - c, gs[0])
            if loads and not (isinstance(T, int) and T + TT >= PASSES * TT):
                raise_piece(T + TT, c)
            for u in (0, 1):
                g3, g2 = gs[4], gs[3]
                if g3 is not None and u in units(g3):
                    n = unit(g3, T - 3, u)
                    act.wait_ge(sem("eT_done"), n + 1)
                    w = 256 if g3 < 3 else 384
                    src = E_ps[:, 0, :] if g3 < 3 else E_ps[:, :, 0:384]
                    dst = eT[:, :, 0:w]
                    if g3 < 3:
                        src = src.rearrange("p (h w) -> p h w", h=2)
                    nc.scalar.activation(dst, src, ACT.Copy).then_inc(sem("eT_ready"), 1)
                if g2 is not None and u in units(g2):
                    n = unit(g2, T - 2, u)
                    act.wait_ge(sem("max_ready"), n + 1)
                    w = 256 if g2 < 3 else 384
                    row = o_row[c][u]
                    for h in range(2):
                        last = nc.scalar.activation(e_sb[u][:, h, 0:w], e_sb[u][:, h, 0:w], ACT.Exp, bias=row[:, h, HD:HD + 1],
                                                    scale=SCALE, accum_out=row[:, h, HD + 1:HD + 2])
                    if g2 == 3:
                        last = nc.scalar.activation(esk[c][u][:], snk[c][u][:], ACT.Exp)
                    last.then_inc(sem("exp_done"), 1)

        schedule(act, step)

        act.sem_inc(sem("oT_ready"), 1)
        with act.Fori(0, TT // 2) as i:
            for c in range(2):
                t = 2 * i + c
                act.wait_ge(sem("wg_in"), t + 1)
                nc.scalar.activation(wg[:], wg[:], ACT.Exp).then_inc(sem("wg_exp"), 1)
                act.wait_ge(sem("oT_done"), t + 2)
                act.wait_ge(sem(f"oT_out{c}"), 16 * (i + 1))
                nc.scalar.activation(oT[c][:, 0:2, :], PS[0][:, 0:2 * P].rearrange("p (k s) -> p k s", k=2), ACT.Copy)
                nc.scalar.activation(oT[c][:, 2:OUT_K, :], PS[1][:, 0:4 * P].rearrange("p (k s) -> p k s", k=4), ACT.Copy).then_inc(sem("oT_ready"), 1)

        def raise_gate(n, c):
            act.wait_ge(sem("gates_done"), n + 1)
            for j in range(2):
                act.wait_ge(sem(f"g_in{j}"), 16 * (n + 1))
                cols = slice(j * (GATE_COLS // 2), (j + 1) * (GATE_COLS // 2))
                nc.scalar.activation(g_hi[c][:, cols], g_raw[j][:], ACT.Copy).then_inc(sem("g_hi_ready"), 1)

        for c in range(2):
            act.sem_inc(sem(f"mT_out{c}"), 16)
        raise_gate(0, 0)
        with act.Fori(0, CHUNKS) as q:
            act.wait_ge(sem("gates_done"), KD * q + 2)
            for k in range(KD):
                last = nc.scalar.activation(x_hi[:, k, :], hT[:, k, ds(q * CHUNK, CHUNK)], ACT.Copy)
            last.then_inc(sem("x_hi_ready"), 1)
            act.wait_ge(sem("o_in"), 16 * (q + 1))
            nc.scalar.activation(o_hi[:], o_in[:], ACT.Copy).then_inc(sem("o_hi_ready"), 1)
            with act.Fori(0, KD // 2) as i:
                for c in range(2):
                    n = KD * q + 2 * i + c
                    raise_gate(n + 1, 1 - c)
                    act.wait_ge(sem("gates_done"), n + 3)
                    for j in range(2):
                        last = nc.scalar.activation(sig[:, j, :], PS[4 * c + j][:], ACT.Sigmoid)
                    last.then_inc(sem("sig_ready"), 1)
                    act.wait_ge(sem("merged"), n + 1)
                    act.dma_start(mT_d[:, ds(2 * i + c, 1), ds(q * CHUNK, CHUNK)], mg[c][:].rearrange("p (a s) -> p a s", a=1)).then_inc(sem(f"mT_out{c}"), 16)

        def high_out(k):
            act.wait_ge(sem(f"w_in{k % 2}"), 16 * (PASSES * TT // 2 + k // 2 + 1))
            nc.scalar.activation(wo_hi[:, k, :], wo_raw[k % 2][:], ACT.Copy).then_inc(sem("wo_hi_ready"), 1)

        for k in range(KD):
            high_out(k)

        def high_tile(t, c, i):
            act.wait_ge(sem(f"m_in{c}"), 16 * (i + 1))
            wait(act, sem("y_done"), t - 1)
            nc.scalar.activation(m_hi[c][:], m_in[c][:], ACT.Copy).then_inc(sem("m_hi_ready"), 1)

        def norm_tile(t, c):
            act.wait_ge(sem("x1_ready"), t + 1)
            nc.scalar.activation(sq2[:], x1[c][:], ACT.Square, accum_out=st2[:, 0:1]).then_inc(sem("sumsq"), 1)
            act.wait_ge(sem("meansq"), 1 * TT + t + 1)
            nc.scalar.activation(st2[:, 2:3], st2[:, 1:2], ACT.Sqrt).then_inc(sem("rms"), 1)

        def evict_tile(t):
            act.wait_ge(sem("h2T_done"), t + 1)
            for j in range(2):
                last = nc.scalar.activation(h2T[:, 4 * j:4 * j + 4, :], PS[4 + j][:].rearrange("p (k s) -> p k s", k=4), ACT.Copy)
            last.then_inc(sem("h2T_ready"), 1)

        high_tile(0, 0, 0)
        high_tile(1, 1, 0)
        norm_tile(0, 0)
        high_tile(2, 0, 1)
        evict_tile(0)
        norm_tile(1, 1)

        def out_pair(i, more):
            for c in range(2):
                t = 2 * i + c
                if c == 0 or more:
                    high_tile(t + 1, 1 - c, i + c)
                evict_tile(t - 1)
                norm_tile(t, c)

        with act.Fori(1, TT // 2 - 1) as i:
            out_pair(i, True)
        out_pair(TT // 2 - 1, False)
        evict_tile(TT - 1)

        for n, t in enumerate((gex, ratio)):
            act.wait_ge(sem("differences"), n + 1)
            nc.scalar.activation(t[:], t[:], ACT.Exp).then_inc(sem("exponentials"), 1)

        act.wait_ge(sem("tables_ready"), 1)
        total = act.value_load(ends[0:1, E - 1:E], min_val=E, max_val=MAX_BLOCKS)

        def rows_T(g):
            act.wait_ge(sem("xgT_done"), g + 1)
            if not isinstance(g, int) or g > 0:
                act.wait_ge(sem("gu_done"), g)
            for j in range(2):
                last = nc.scalar.activation(xTs[:, 4 * j:4 * j + 4, :], PS[2 + j][:].rearrange("p (k s) -> p k s", k=4), ACT.Copy)
            last.then_inc(sem("xT_ready"), 1)

        def block(g):
            act.wait_ge(sem("gu_done"), g + 1)
            wait(act, sem("h_ready"), g)
            nc.scalar.activation(hg[:], PS[0][:], ACT.Silu).then_inc(sem("silu_done"), 1)
            rows_T(g + 1)
            act.wait_ge(sem("hT_done"), g + 1)
            nc.scalar.activation(hTs[:], PS[6][:].rearrange("p (k s) -> p k s", k=KE), ACT.Copy).then_inc(sem("hT_ready"), 1)

        rows_T(0)
        block(0)
        with act.Fori(1, total) as g:
            block(g)

        with act.Fori(0, TT // 2) as i:
            for c in range(2):
                t = 2 * i + c
                act.wait_ge(sem("acc_ready"), t + 1)
                nc.scalar.activation(sq3[:], acc[c][:], ACT.Square, accum_out=st3[:, 0:1]).then_inc(sem("sumsq"), 1)
                act.wait_ge(sem("meansq"), 2 * TT + t + 1)
                nc.scalar.activation(st3[:, 2:3], st3[:, 1:2], ACT.Sqrt).then_inc(sem("rms"), 1)

    @block.vector
    def _(dve):
        ch = Chain(dve, sem("dve_chain"))
        dve.wait_ge(sem("ident_ready"), 1)
        dve.wait_ge(sem("c_silu"), 1)
        for k in range(KD):
            last = nc.vector.tensor_scalar(c_bc[:, k, :], ones[:], c_sil[:, k:k + 1], None, ALU.mult)
        last.then_inc(sem("c_bc_ready"), 1)
        dve.wait_ge(sem("b_in"), 16)
        for j in range(N_MOD * D // CHUNK):
            dve.wait_ge(sem("mod_mm"), j + 1)
            ch(nc.vector.tensor_tensor(mod[:, j * CHUNK:(j + 1) * CHUNK], bank[j % 2][:], b_bc[:, j * CHUNK:(j + 1) * CHUNK], ALU.add))
        ch.join()
        dve.wait_ge(sem("g_in"), 48)
        for n, g in ((1, 0), (4, 1)):
            ch(nc.vector.scalar_tensor_tensor(mod[:, n * D:(n + 1) * D], mod[:, n * D:(n + 1) * D], 1.0, g_bc[:, g, :], ALU.add, ALU.mult))
        ch.join()
        dve.sem_inc(sem("mod_rows_ready"), 1)
        dve.wait_ge(sem("cols_mm"), 1)
        nc.vector.tensor_copy(A1[:], bank[2][:, 0:KD])
        ch(nc.vector.tensor_copy(B1[:], bank[2][:, KD:2 * KD]))
        ch.join()
        dve.wait_ge(sem("rows_out"), 80)
        dve.sem_inc(sem("cols_ready"), 1)
        dve.sem_inc(sem("h_all"), 1)
        with dve.Fori(0, TT // 2) as i:
            for c in range(2):
                T = 2 * i + c
                dve.wait_ge(sem("sumsq"), T + 1)
                nc.vector.tensor_scalar(stat1[:, 1:2], stat1[:, 0:1], 1.0 / D, EPS, ALU.mult, ALU.add).then_inc(sem("meansq"), 1)
                dve.wait_ge(sem("rms"), T + 1)
                nc.vector.reciprocal(stat1[:, 3:4], stat1[:, 2:3]).then_inc(sem("rstd"), 1)
                dve.wait_ge(sem("xn_ready"), T + 1)
                dve.wait_ge(sem("xT_done"), T + 1)
                for k in range(KD):
                    src = bank[k // 4][:, (k % 4) * P:(k % 4 + 1) * P]
                    last = nc.vector.tensor_scalar(hT[:, k, ds(T * P, P)], src, A1[:, k:k + 1], B1[:, k:k + 1], ALU.mult, ALU.add)
                last.then_inc(sem("h_all"), 1)
        dve.wait_ge(sem("pos_in"), 96)
        dve.wait_ge(sem("invf_ready"), 1)
        link = lambda ins: (ch(ins), ch.join())
        link(nc.vector.tensor_copy(pos_f[:], pos_i[:]))
        pf = pos_f[:].rearrange("p (t a) -> p t a", a=1).broadcast_to([P, 3 * TT, HALF])
        fr = invf[:].rearrange("p (a f) -> p a f", a=1).broadcast_to([P, 3 * TT, HALF])
        link(nc.vector.tensor_tensor(ang[:], pf, fr, ALU.mult))
        link(nc.vector.tensor_scalar(turn[:], ang[:], float(1 / (2 * np.pi)), MAGIC, ALU.mult, ALU.add))
        link(nc.vector.tensor_scalar(turn[:], turn[:], -MAGIC, None, ALU.add))
        for part in PI2:
            link(nc.vector.scalar_tensor_tensor(ang[:], turn[:], -part, ang[:], ALU.mult, ALU.add))
        lim = 3.1415925
        nc.vector.tensor_scalar(ang[:], ang[:], lim, -lim, ALU.min, ALU.max).then_inc(sem("reduced"), 1)
        dve.wait_ge(sem("reduced"), 1)
        link(nc.vector.scalar_tensor_tensor(turn[:], ang[:], -1.0, ang[:], ALU.mult, ALU.max))
        nc.vector.tensor_scalar(turn[:], turn[:], -1.0, float(np.pi / 2), ALU.mult, ALU.add).then_inc(sem("reduced"), 1)
        dve.wait_ge(sem("sink_in"), 16)
        dve.wait_ge(sem("attn_consts"), 1)
        link(nc.vector.tensor_scalar(nsink[:], sink_bc[:], -1.0, None, ALU.mult))
        dve.wait_ge(sem("angles_ready"), 1)

        def step(T, c, gs, loads):
            g1, g2, g3 = gs[2], gs[3], gs[4]
            if g1 is not None:
                S = T - 1
                row = tile_of(S) + (0 if g1 == 3 else TT * g1)
                nh = 4 if g1 < 3 else 5
                dve.wait_ge(sem("proj_evicted"), S + 1)
                wait(dve, sem("qkT_done"), S)
                cos_b = cos_t[:, ds(row, 1), :].broadcast_to([P, 2 * nh, HALF])
                sin_b = sin_t[:, ds(row, 1), :].broadcast_to([P, nh, HALF])
                raw = qk_raw[:, 0:nh * HD]
                r4 = raw.rearrange("p (h m) -> p h m", h=nh)
                tmp4 = qk_tmp[:, 0:nh * HD].rearrange("p (h m) -> p h m", h=nh)
                nc.vector.tensor_tensor(qk_rot[:, 0:nh * HD].rearrange("p (h m) -> p h m", m=HALF), raw.rearrange("p (h m) -> p h m", m=HALF), cos_b, ALU.mult)
                nc.vector.scalar_tensor_tensor(tmp4[:, :, 0:HALF], r4[:, :, HALF:HD], -1.0, sin_b, ALU.mult, ALU.mult)
                nc.vector.tensor_tensor(tmp4[:, :, HALF:HD], r4[:, :, 0:HALF], sin_b, ALU.mult).then_inc(sem("rot_parts"), 1)
                dve.wait_ge(sem("rot_parts"), S + 1)
                nc.vector.tensor_tensor(qk_rot[:, 0:nh * HD], qk_rot[:, 0:nh * HD], qk_tmp[:, 0:nh * HD], ALU.add).then_inc(sem("rot_done"), 1)
                dve.wait_ge(sem("qkT_done"), S + 1)
                t = tile_of(S)
                q = qst[1 - c]
                tb = bank[2]
                for pair in range(1 if g1 < 3 else 2):
                    nc.vector.tensor_copy(q[0:HD, 2 * pair, :], tb[0:HD, pair * P:(pair + 1) * P])
                    nc.vector.tensor_copy(q[HD:P, 2 * pair + 1, :], tb[HD:P, pair * P:(pair + 1) * P])
                if g1 < 3:
                    last = nc.vector.tensor_copy(kT_dil[:, ds(HD + t * P, P)], tb[:, P:2 * P])
                else:
                    nc.vector.tensor_copy(kT_swa[0:HD, ds(P + t * P, P)], tb[0:HD, 2 * P:3 * P])
                    last = nc.vector.tensor_copy(kT_swa[HD:P, ds(P + t * P, P)], tb[0:HD, 2 * P:3 * P])
                last.then_inc(sem("qk_ready"), 1)
            for u in (0, 1):
                if g2 is not None and u in units(g2):
                    S = T - 2
                    n = unit(g2, S, u)
                    dve.wait_ge(sem("s_done"), n + 1)
                    w = 256 if g2 < 3 else 384
                    e = e_sb[u][:, :, 0:w]
                    if g2 < 3:
                        src = S_ps[:, 0, :].rearrange("p (h w) -> p h w", h=2)
                        mk = mask_dil
                    else:
                        src, mk = S_ps[:, :, 0:384], mask_swa
                    m = mk[:, ds(mask_index(g2, tile_of(S)), 1), :].broadcast_to([P, 2, w])
                    nc.vector.tensor_tensor(e, src, m, ALU.add).then_inc(sem("masked"), 1)
                    dve.wait_ge(sem("masked"), n + 1)
                    wait(dve, sem("max_ready"), n)
                    nc.vector.tensor_reduce(mx[:], e, AX.X, ALU.max).then_inc(sem("maxed"), 1)
                    dve.wait_ge(sem("maxed"), n + 1)
                    wait(dve, sem(f"o_out{c}{u}"), 8 * (S - c) if u == 0 else 8 * (S - c) - 8 * SWA_T0)
                    negm = o_row[c][u][:, :, HD:HD + 1].rearrange("p h a -> p (h a)")
                    if g2 < 3:
                        nc.vector.tensor_scalar(negm, mx[:], -SCALE, None, ALU.mult).then_inc(sem("max_ready"), 1)
                    else:
                        head = ((S // TT) % 2) * 4 + 2 * u
                        nc.vector.tensor_scalar(nm[:], mx[:], -SCALE, None, ALU.mult).then_inc(sem("nm_step"), 1)
                        dve.wait_ge(sem("nm_step"), 2 * (n - SWA_T0) + 1)
                        nc.vector.tensor_tensor(negm, nm[:], nsink[:, ds(head, 2)], ALU.min).then_inc(sem("nm_step"), 1)
                        dve.wait_ge(sem("nm_step"), 2 * (n - SWA_T0) + 2)
                        nc.vector.tensor_tensor(snk[c][u][:], negm, sink_bc[:, ds(head, 2)], ALU.add).then_inc(sem("max_ready"), 1)
                if g3 is not None and u in units(g3):
                    S = T - 3
                    n = unit(g3, S, u)
                    row = o_row[1 - c][u]
                    dve.wait_ge(sem("pv_done"), n + 1)
                    src = O_ps[:, 0:P].rearrange("p (h m) -> p h m", h=2)
                    if g3 < 3:
                        nc.vector.tensor_copy(row[:, :, 0:HD], src).then_inc(sem("o_done"), 1)
                    else:
                        den = row[:, :, HD + 1:HD + 2].rearrange("p h a -> p (h a)")
                        nc.vector.tensor_tensor(rden[:], den, esk[1 - c][u][:], ALU.add).then_inc(sem("den_step"), 1)
                        dve.wait_ge(sem("den_step"), 2 * (n - SWA_T0) + 1)
                        nc.vector.reciprocal(rden[:], rden[:]).then_inc(sem("den_step"), 1)
                        dve.wait_ge(sem("den_step"), 2 * (n - SWA_T0) + 2)
                        rb = rden[:].rearrange("p (h a) -> p h a", a=1).broadcast_to([P, 2, HD])
                        nc.vector.tensor_tensor(row[:, :, 0:HD], src, rb, ALU.mult).then_inc(sem("o_done"), 1)

        schedule(dve, step)

        def b3(ap, shape):
            return ap.broadcast_to(shape)

        with dve.Fori(0, TT // 2) as i:
            for c in range(2):
                t = 2 * i + c
                dve.wait_ge(sem(f"od_in{c}"), 32 * (i + 1))
                rows = od[c][:].rearrange("p g (h m) -> p g h m", m=STAT)
                negm = rows[:, :, :, HD:HD + 1].rearrange("p g h a -> p g (h a)")
                den = rows[:, :, :, HD + 1:HD + 2].rearrange("p g h a -> p g (h a)")
                flat = lambda t4: t4[:].rearrange("p g (h a) -> p (g h) a", a=1).broadcast_to([P, 3 * DIL_HEADS, HD])
                per_h = lambda t2: t2[:].rearrange("p (a h) -> p a h", a=1).broadcast_to([P, 3, DIL_HEADS])
                link_n = [0]

                def link5(ins, last=6):
                    link_n[0] += 1
                    ins.then_inc(sem("merge_step"), 1)
                    dve.wait_ge(sem("merge_step"), 8 * t + link_n[0])

                link5(nc.vector.tensor_tensor(nmin[:], negm[:, 0, :], negm[:, 1, :], ALU.min))
                link5(nc.vector.tensor_tensor(nmin[:], nmin[:], negm[:, 2, :], ALU.min))
                nc.vector.tensor_tensor(wg[:], per_h(nmin), negm, ALU.subtract).then_inc(sem("wg_in"), 1)
                dve.wait_ge(sem("wg_exp"), t + 1)
                link5(nc.vector.tensor_tensor(wden[:], wg[:], den, ALU.mult))
                link5(nc.vector.tensor_reduce(dsum[:], wden[:].rearrange("p g h -> p h g"), AX.X, ALU.add))
                link5(nc.vector.reciprocal(dsum[:], dsum[:]))
                link5(nc.vector.tensor_tensor(wg[:], wg[:], per_h(dsum), ALU.mult))
                link5(nc.vector.tensor_tensor(wsum[:].rearrange("p g (h m) -> p (g h) m", m=HD), rows.rearrange("p g h m -> p (g h) m")[:, :, 0:HD], flat(wg), ALU.mult))
                link5(nc.vector.tensor_tensor(wsum[:, 0, :], wsum[:, 0, :], wsum[:, 1, :], ALU.add))
                dve.wait_ge(sem("oT_done"), t + 1)
                nc.vector.tensor_tensor(oa[:], wsum[:, 0, :], wsum[:, 2, :], ALU.add).then_inc(sem("oa_ready"), 1)

        dve.sem_inc(sem("o_lo_ready"), 1)
        dve.sem_inc(sem("gated"), 2)
        with dve.Fori(0, CHUNKS) as q:
            dve.wait_ge(sem("x_hi_ready"), q + 1)
            for k in range(KD):
                last = nc.vector.tensor_tensor(x_lo[:, k, :], hT[:, k, ds(q * CHUNK, CHUNK)], x_hi[:, k, :].bitcast(F32), ALU.subtract)
            last.then_inc(sem("x_lo_ready"), 1)
            dve.wait_ge(sem("o_hi_ready"), q + 1)
            nc.vector.tensor_tensor(o_lo[:], o_in[:], o_hi[:].bitcast(F32), ALU.subtract).then_inc(sem("o_lo_ready"), 1)
            with dve.Fori(0, KD // 2) as i:
                for c in range(2):
                    n = KD * q + 2 * i + c
                    dve.wait_ge(sem("sig_ready"), n + 1)
                    dve.wait_ge(sem(f"mT_out{c}"), 16 * ((KD // 2) * q + i + 1))
                    nc.vector.tensor_tensor(sig[:, 0, :], sig[:, 0, :], PS[4 * c + 2][:], ALU.mult)
                    nc.vector.tensor_tensor(sig[:, 1, :], sig[:, 1, :], PS[4 * c + 3][:], ALU.mult).then_inc(sem("gated"), 1)
                    dve.wait_ge(sem("gated"), n + 3)
                    nc.vector.tensor_tensor(mg[c][:], sig[:, 0, :], sig[:, 1, :], ALU.add).then_inc(sem("merged"), 1)

        dve.wait_ge(sem("rows_in"), 48)

        def residual(t, c, i):
            dve.wait_ge(sem("y_done"), t + 1)
            wait(dve, sem(f"x1_out{c}"), 32 * i)
            for j in range(2):
                last = nc.vector.tensor_tensor(x1[c][:, j * 512:(j + 1) * 512], PS[2 * c + j][:], gt1b[:, j * 512:(j + 1) * 512], ALU.mult)
            last.then_inc(sem("y_evicted"), 1)
            dve.wait_ge(sem("y_evicted"), t + 1)
            dve.wait_ge(sem(f"x_in{c}"), 16 * (TT // 2 + i + 1))
            nc.vector.tensor_tensor(x1[c][:], x1[c][:], x_in[c][:], ALU.add).then_inc(sem("x1_ready"), 1)
            dve.wait_ge(sem("sumsq"), 1 * TT + t + 1)
            nc.vector.tensor_scalar(st2[:, 1:2], st2[:, 0:1], 1.0 / D, EPS, ALU.mult, ALU.add).then_inc(sem("meansq"), 1)
            dve.wait_ge(sem("rms"), 1 * TT + t + 1)
            nc.vector.reciprocal(st2[:, 3:4], st2[:, 2:3]).then_inc(sem("rstd"), 1)
            dve.wait_ge(sem("rstd"), 1 * TT + t + 1)
            nc.vector.scalar_tensor_tensor(h2[c][:], x1[c][:], st2[:, 3:4], A2b[:], ALU.mult, ALU.mult).then_inc(sem("h2_scaled"), 1)
            dve.wait_ge(sem("h2_scaled"), t + 1)
            nc.vector.tensor_tensor(h2[c][:], h2[c][:], B2b[:], ALU.add).then_inc(sem("h2_ready"), 1)

        def take_logits(t):
            dve.wait_ge(sem("logits_done"), t + 1)
            nc.vector.tensor_copy(logits[:, ds(t, 1), :], PS[6][:, 0:GROUPS + E].rearrange("p (a n) -> p a n", a=1)).then_inc(sem("logits_ready"), 1)

        residual(0, 0, 0)
        residual(1, 1, 0)
        take_logits(0)
        with dve.Fori(1, TT // 2) as i:
            for c in range(2):
                residual(2 * i + c, c, i)
                take_logits(2 * i + c - 1)
        take_logits(TT - 1)

        dve.wait_ge(sem("r_bias_in"), 16)
        dve.wait_ge(sem("route_consts"), 1)
        dve.wait_ge(sem("dve_chain"), ch.n)
        rb = r_bias[:].rearrange("p (a n) -> p a n", a=1).broadcast_to([P, TT, GROUPS + E])
        link(nc.vector.tensor_tensor(logits[:], logits[:], rb, ALU.add))
        gl = logits[:, :, 0:GROUPS]

        def wide(ap, n):
            return ap[:].broadcast_to([P, TT, n])

        def first_best(vals, n, best, eq, idx, oh_out):
            link(nc.vector.tensor_reduce(best[:].rearrange("p t a -> p (t a)"), vals, AX.X, ALU.max))
            link(nc.vector.tensor_tensor(eq[:], vals, wide(best, n), ALU.is_equal))
            link(nc.vector.scalar_tensor_tensor(eq[:], eq[:], -float(n), iota_e[:, :, 0:n], ALU.mult, ALU.add))
            link(nc.vector.tensor_reduce(idx[:].rearrange("p t a -> p (t a)"), eq[:], AX.X, ALU.min))
            link(nc.vector.tensor_tensor(oh_out[:], eq[:], wide(idx, n), ALU.is_equal))

        first_best(gl, GROUPS, gmax, geq, gidx, gsel)
        nc.vector.tensor_tensor(gex[:], gl, wide(gmax, GROUPS), ALU.subtract).then_inc(sem("differences"), 1)
        link(nc.vector.tensor_scalar(gsel[:], gsel[:], -NEG, NEG, ALU.mult, ALU.add))
        pen = gsel[:].rearrange("p t (g a) -> p (t g) a", a=1).broadcast_to([P, TT * GROUPS, PER_GROUP])
        link(nc.vector.tensor_copy(el[:], logits[:, :, GROUPS:]))
        el3 = el[:].rearrange("p t (g a) -> p (t g) a", a=PER_GROUP)
        link(nc.vector.tensor_tensor(el3, el3, pen, ALU.add))
        first_best(el[:], E, top[0], eeq, eidx, oh[0])
        link(nc.vector.scalar_tensor_tensor(el[:], oh[0][:], 2 * NEG, el[:], ALU.mult, ALU.add))
        first_best(el[:], E, top[1], eeq, eidx, oh[1])
        nc.vector.tensor_tensor(ratio[:], top[1][:], top[0][:], ALU.subtract).then_inc(sem("differences"), 1)
        nc.vector.tensor_tensor(both[:], oh[0][:], oh[1][:], ALU.add).then_inc(sem("both_ready"), 1)
        dve.wait_ge(sem("exponentials"), 1)
        link(nc.vector.tensor_reduce(gsum[:].rearrange("p t a -> p (t a)"), gex[:], AX.X, ALU.add))
        dve.wait_ge(sem("exponentials"), 2)
        link(nc.vector.tensor_scalar(rinv[:], ratio[:], 1.0, None, ALU.add))
        link(nc.vector.tensor_tensor(rinv[:], rinv[:], gsum[:], ALU.mult))
        link(nc.vector.reciprocal(pair_w[:, :, 0:1], rinv[:]))
        link(nc.vector.tensor_tensor(pair_w[:, :, 1:2], pair_w[:, :, 0:1], ratio[:], ALU.mult))
        dve.wait_ge(sem("ranks_done"), 1)
        link(nc.vector.tensor_scalar(cnt_i[:], PS[1][:, 0:E], float(BLK - 1), None, ALU.add))
        link(nc.vector.tensor_scalar(cnt_i[:], cnt_i[:], 7, None, ALU.logical_shift_right))
        link(nc.vector.tensor_copy(nblk[:], cnt_i[:]))
        link(nc.vector.tensor_scalar(nblk[:], nblk[:], 1.0, None, ALU.max))
        link(nc.vector.memset(cnt[:], 1.0))
        link(nc.vector.tensor_tensor_scan(pend[:], cnt[:], nblk[:], 0.0, ALU.mult, ALU.add))
        link(nc.vector.tensor_copy(ends[:], pend[0:1, :]))
        link(nc.vector.tensor_tensor(pbase[:], pend[:], nblk[:], ALU.subtract))
        link(nc.vector.tensor_scalar(pbase[:], pbase[:], float(BLK), None, ALU.mult))
        pe_b = pend[:].rearrange("p (a e) -> p a e", a=1).broadcast_to([P, MAX_BLOCKS, E])
        ib_b = iota_b[:].rearrange("p (b a) -> p b a", a=1).broadcast_to([P, MAX_BLOCKS, E])
        link(nc.vector.tensor_tensor(cmp_e[:], pe_b, ib_b, ALU.is_le))
        link(nc.vector.tensor_reduce(e_f[:], cmp_e[:], AX.X, ALU.add))
        link(nc.vector.tensor_scalar(e_f[:], e_f[:], float(E - 1), None, ALU.min))
        link(nc.vector.tensor_copy(expert_of[0:1, 0:MAX_BLOCKS], e_f[0:1, :]))
        rk = PS[0][:, 0:TT * E].rearrange("p (t e) -> p t e", e=E)
        pb = pbase[:].rearrange("p (a e) -> p a e", a=1).broadcast_to([P, TT, E])
        link(nc.vector.tensor_tensor(posn[:], rk, pb, ALU.add))
        for k in range(2):
            link(nc.vector.tensor_tensor(prod[:], posn[:], oh[k][:], ALU.mult))
            link(nc.vector.tensor_reduce(slot_f[:, :, k:k + 1].rearrange("p t a -> p (t a)"), prod[:], AX.X, ALU.add))
        link(nc.vector.tensor_copy(slot_i[:], slot_f[:]))
        link(nc.vector.tensor_scalar(lane_i[:], slot_i[:], BLK - 1, None, ALU.bitwise_and))
        link(nc.vector.tensor_scalar(blk_i[:], slot_i[:], 7, None, ALU.logical_shift_right))
        link(nc.vector.tensor_copy(lane_f[:], lane_i[:]))
        link(nc.vector.tensor_copy(blk_f[:], blk_i[:]))
        with dve.Fori(0, TT) as t:
            for k in range(2):
                dve.wait_ge(sem("oh_free"), 2 * t + k + 1)
                lane = lane_f[:, ds(t, 1), k:k + 1].rearrange("p a b -> p (a b)")
                blk = blk_f[:, ds(t, 1), k:k + 1].rearrange("p a b -> p (a b)")
                ident_k = flat_id[:, ds(t, 1), k:k + 1].rearrange("p a b -> p (a b)")
                nc.vector.tensor_scalar(lane_oh[k][:], iota_r[:], lane, None, ALU.is_equal)
                nc.vector.tensor_scalar(blk_oh[k][:, 0, :], iota_b[:], blk, ident_k, ALU.is_equal, ALU.mult)
                nc.vector.tensor_scalar(blk_oh[k][:, 1, :], iota_b[:], blk, None, ALU.is_equal).then_inc(sem("oh_ready"), 1)
        dve.wait_ge(sem("oh_free"), 2 * TT + 2)
        link(nc.vector.tensor_copy(tab[:], PS[2][:, 0:2 * MAX_BLOCKS].rearrange("p (a b) -> p a b", a=2)))
        link(nc.vector.scalar_tensor_tensor(idx_f[:], tab[:, 1, :], pad_id[:, 1:2], tab[:, 0, :], ALU.mult, ALU.add))
        link(nc.vector.tensor_scalar(idx_f[:], idx_f[:], pad_id[:, 0:1], None, ALU.add))
        link(nc.vector.tensor_copy(scatter_idx[:, 0:MAX_BLOCKS], idx_f[:]))
        link(nc.vector.tensor_copy(scatter_idx[:, MAX_BLOCKS:], pad_id[:, 0:1]))
        link(nc.vector.tensor_scalar(gather_idx[:], scatter_idx[:], 1, None, ALU.logical_shift_right))
        dve.sem_inc(sem("tables_ready"), 1)

        total = dve.value_load(ends[0:1, E - 1:E], min_val=E, max_val=MAX_BLOCKS)

        def gated(g):
            dve.wait_ge(sem("silu_done"), g + 1)
            wait(dve, sem("hT_done"), g)
            nc.vector.tensor_tensor(hs[:], hg[:], PS[1][:], ALU.mult).then_inc(sem("h_ready"), 1)

        def rows_out(g):
            dve.wait_ge(sem("down_done"), g + 1)
            dve.wait_ge(sem("y_free"), g + 1)
            for j in range(2):
                last = nc.vector.tensor_copy(y_sb[:, j * 512:(j + 1) * 512], PS[4 + j][:])
            last.then_inc(sem("y_ready"), 1)

        dve.sem_inc(sem("y_ready"), 1)
        gated(0)
        with dve.Fori(1, total) as g:
            gated(g)
            rows_out(g - 1)
        rows_out(total - 1)

        dve.wait_ge(sem("rows2_in"), 32)
        with dve.Fori(0, TT // 2) as i:
            for c in range(2):
                t = 2 * i + c
                dve.wait_ge(sem(f"yp_in{c}"), 32 * (i + 1))
                w0 = pair_w[:, ds(t, 1), 0:1].rearrange("p a b -> p (a b)")
                w1 = pair_w[:, ds(t, 1), 1:2].rearrange("p a b -> p (a b)")
                steps_done = [0]

                def link3(ins):
                    steps_done[0] += 1
                    ins.then_inc(sem("last_step"), 1)
                    dve.wait_ge(sem("last_step"), 3 * t + steps_done[0])

                dve.wait_ge(sem(f"out_stored{c}"), 16 * (i + 1))
                link3(nc.vector.tensor_scalar(acc[c][:], yp[c][:, 0, :], w0, None, ALU.mult))
                link3(nc.vector.scalar_tensor_tensor(acc[c][:], yp[c][:, 1, :], w1, acc[c][:], ALU.mult, ALU.add))
                link3(nc.vector.tensor_tensor(acc[c][:], acc[c][:], gt2b[:], ALU.mult))
                nc.vector.tensor_tensor(acc[c][:], acc[c][:], xl[c][:], ALU.add).then_inc(sem("acc_ready"), 1)
                dve.wait_ge(sem("sumsq"), 2 * TT + t + 1)
                nc.vector.tensor_scalar(st3[:, 1:2], st3[:, 0:1], 1.0 / D, EPS, ALU.mult, ALU.add).then_inc(sem("meansq"), 1)
                dve.wait_ge(sem("rms"), 2 * TT + t + 1)
                nc.vector.reciprocal(st3[:, 3:4], st3[:, 2:3]).then_inc(sem("rstd"), 1)
                dve.wait_ge(sem("rstd"), 2 * TT + t + 1)
                nc.vector.scalar_tensor_tensor(acc[c][:], acc[c][:], st3[:, 3:4], gfb[:], ALU.mult, ALU.mult).then_inc(sem("out_ready"), 1)

    @block.tensor
    def _(pe):
        pe.wait_ge(sem("ident_ready"), 1)
        pe.wait_ge(sem("c_bc_ready"), 1)
        for j in range(N_MOD * D // CHUNK):
            pe.wait_ge(sem(f"wada_in{j % 4}"), 16 * (j // 4 + 1))
            wait(pe, sem("dve_chain"), j - 1)
            for k in range(KD):
                last = nc.tensor.matmul(bank[j % 2][:], c_bc[:, k, :], wada[j % 4][:, k, :], start=(k == 0), stop=(k == KD - 1))
            last.then_inc(sem("mod_mm"), 1)
        pe.wait_ge(sem("mod_rows_ready"), 1)
        for col in range(2 * KD):
            k = col % KD
            src = mod[0:1, D + k * P:D + (k + 1) * P] if col < KD else mod[0:1, k * P:(k + 1) * P]
            last = nc.tensor.matmul(bank[2][:, col:col + 1], src, ones_row[0:1, 0:1], start=True, stop=True)
        last.then_inc(sem("cols_mm"), 1)
        pe.sem_inc(sem("xn_used"), 1)
        with pe.Fori(0, TT // 2) as i:
            for c in range(2):
                T = 2 * i + c
                pe.wait_ge(sem("xn_ready"), T + 1)
                pe.wait_ge(sem("h_all"), T + 1)
                for k in range(KD):
                    last = nc.tensor.transpose(bank[k // 4][:, (k % 4) * P:(k % 4 + 1) * P], xn[:, k * P:(k + 1) * P], ident[:])
                last.then_inc(sem("xT_done"), 1)
                pe.wait_ge(sem("xT_done"), T + 1)
                pe.sem_inc(sem("xn_used"), 1)

        def project(T, c, g, ks):
            row = ((T // TT) % 2) * KD
            for k in ks:
                for a, (x, w) in enumerate(((h_hi, w_hi), (h_hi, w_lo), (h_lo, w_hi))):
                    last = nc.tensor.matmul(bank[c][:, 0:PASS_COLS].rearrange("p (a m) -> p a m", a=1), x[c][:, k, :], w[:, ds(row + k, 1), :], start=(k == 0 and a == 0), stop=(k == KD - 1 and a == 2))
            if ks[-1] == KD - 1:
                last.then_inc(sem("proj_done"), 1)

        def step(T, c, gs, loads):
            g, g1, g2, g3 = gs[1], gs[2], gs[3], gs[4]
            if g is not None:
                pe.wait_ge(sem("h_lo_ready"), T + 1)
                pe.wait_ge(sem("w_lo_ready"), TT * (T // TT) + TT)
                wait(pe, sem("proj_evicted"), T - 1)
                project(T, c, g, (0, 1, 2, 3))
            if g1 is not None:
                pe.wait_ge(sem("rot_done"), T)
                tb = bank[2]
                if g1 < 3:
                    nc.tensor.transpose(tb[:, 0:P], qk_rot[:, 0:P], ident[:])
                    last = nc.tensor.transpose(tb[:, P:2 * P], qk_rot[:, P:2 * P], ident[:])
                else:
                    nc.tensor.transpose(tb[:, 0:P], qk_rot[:, 0:P], ident[:])
                    nc.tensor.transpose(tb[:, P:2 * P], qk_rot[:, P:2 * P], ident[:])
                    last = nc.tensor.transpose(tb[0:HD, 2 * P:3 * P], qk_rot[:, 2 * P:2 * P + HD], ident[:])
                last.then_inc(sem("qkT_done"), 1)
            if g is not None:
                project(T, c, g, (4, 5))
            two = (g2 == 3 or g3 == 3)
            for u in (0, 1):
                if g3 is not None and u in units(g3):
                    n = unit(g3, T - 3, u)
                    pe.wait_ge(sem("exp_done"), n + 1)
                    for h in range(2):
                        for j in range(2 if g3 < 3 else 3):
                            dst = E_ps[:, 0, (2 * h + j) * P:(2 * h + j + 1) * P] if g3 < 3 else E_ps[:, h, j * P:(j + 1) * P]
                            last = nc.tensor.transpose(dst, e_sb[u][:, h, j * P:(j + 1) * P], ident[:])
                    last.then_inc(sem("eT_done"), 1)
                if g2 is not None and u in units(g2):
                    S = T - 2
                    n = unit(g2, S, u)
                    if isinstance(T, int) and T - 1 >= STEPS:
                        pe.wait_ge(sem("qk_ready"), STEPS)
                    else:
                        pe.wait_ge(sem("qk_ready"), T)
                    wait(pe, sem("masked"), n)
                    t = tile_of(S)
                    for h in range(2):
                        if g2 < 3:
                            last = nc.tensor.matmul(S_ps[:, 0, h * 256:(h + 1) * 256], qst[c][:, h, :], kT_dil[:, ds(t * P, 256)], start=True, stop=True)
                        else:
                            last = nc.tensor.matmul(S_ps[:, h, 0:384], qst[c][:, 2 * u + h, :], kT_swa[:, ds(t * P, 384)], start=True, stop=True)
                    last.then_inc(sem("s_done"), 1)
                if g is not None:
                    if u == 0:
                        project(T, c, g, (6,) if two else (6, 7))
                    elif two:
                        project(T, c, g, (7,))
                if g3 is not None and u in units(g3):
                    S = T - 3
                    n = unit(g3, S, u)
                    pe.wait_ge(sem("eT_ready"), n + 1)
                    wait(pe, sem("o_done"), n)
                    t = tile_of(S)
                    nj = 2 if g3 < 3 else 3
                    for h in range(2):
                        for j in range(nj):
                            v = v_dil[:, ds(t + j, 1), h * HD:(h + 1) * HD] if g3 < 3 else v_swa[:, ds(t + j, 1), :]
                            last = nc.tensor.matmul(O_ps[:, h * HD:(h + 1) * HD].rearrange("p (a m) -> p a m", a=1), eT[:, h, j * P:(j + 1) * P], v,
                                                    start=(j == 0), stop=(j == nj - 1))
                    last.then_inc(sem("pv_done"), 1)

        schedule(pe, step)

        pe.sem_inc(sem("oT_done"), 1)
        with pe.Fori(0, TT // 2) as i:
            for c in range(2):
                t = 2 * i + c
                pe.wait_ge(sem("oa_ready"), t + 1)
                pe.wait_ge(sem("oT_ready"), t + 1)
                for k in range(2):
                    nc.tensor.transpose(PS[0][:, k * P:(k + 1) * P], oa[:, k * P:(k + 1) * P], ident[:])
                for k in range(4):
                    last = nc.tensor.transpose(PS[1][:, k * P:(k + 1) * P], ob[c][:, k * P:(k + 1) * P], ident[:])
                last.then_inc(sem("oT_done"), 1)

        parts = lambda w, x: ((w[0], x[0]), (w[0], x[1]), (w[1], x[0]))
        pe.sem_inc(sem("gates_done"), 2)
        with pe.Fori(0, CHUNKS) as q:
            with pe.Fori(0, KD // 2) as i:
                for c in range(2):
                    pe.wait_ge(sem("x_lo_ready"), q + 1)
                    pe.wait_ge(sem("o_lo_ready"), q + 2)
                    n = KD * q + 2 * i + c
                    pe.wait_ge(sem("g_lo_ready"), 2 * n + 2)
                    pe.wait_ge(sem("gated"), n + 1)
                    gw = (g_hi[c], g_lo[c])
                    off = KD * 2 * P
                    jobs = [(0, k, k * 2 * P, k == 0, k == KD - 1, (x_hi, x_lo)) for k in range(KD)]
                    jobs += [(1, k, k * 2 * P + P, k == 0, k == KD - 1, (x_hi, x_lo)) for k in range(KD)]
                    jobs += [(2, k, off + k * P, k == 0, k == 1, (o_hi, o_lo)) for k in range(2)]
                    jobs += [(3, k, off + k * P, k == 2, k == OUT_K - 1, (o_hi, o_lo)) for k in range(2, OUT_K)]
                    for dst, k, col, first, last_k, xs in jobs:
                        for a, (w, x) in enumerate(parts(gw, xs)):
                            last = nc.tensor.matmul(PS[4 * c + dst][:], w[:, col:col + P], x[:, k, :],
                                                    start=first and a == 0, stop=last_k and a == 2)
                    last.then_inc(sem("gates_done"), 1)

        pe.wait_ge(sem("wo_lo_ready"), KD)

        def out_tile(t, c, halves):
            for j in halves:
                for k in range(KD):
                    for a, (x, w) in enumerate(((m_hi, wo_hi), (m_hi, wo_lo), (m_lo, wo_hi))):
                        last = nc.tensor.matmul(PS[2 * c + j][:], x[c][:, k, :], w[:, k, j * 512:(j + 1) * 512],
                                                start=(k == 0 and a == 0), stop=(k == KD - 1 and a == 2))
            if halves[-1] == 1:
                last.then_inc(sem("y_done"), 1)

        def turn_tile(t, c):
            pe.wait_ge(sem("h2_ready"), t + 1)
            wait(pe, sem("h2T_ready"), t)
            for k in range(KD):
                last = nc.tensor.transpose(PS[4 + k // 4][:, (k % 4) * P:(k % 4 + 1) * P], h2[c][:, k * P:(k + 1) * P], ident[:])
            last.then_inc(sem("h2T_done"), 1)

        def route_tile(t):
            pe.wait_ge(sem("h2T_ready"), t + 1)
            wait(pe, sem("logits_ready"), t)
            for k in range(KD):
                last = nc.tensor.matmul(PS[6][:, 0:GROUPS + E], h2T[:, k, :], w_rt[:, k, :], start=(k == 0), stop=(k == KD - 1))
            last.then_inc(sem("logits_done"), 1)

        pe.wait_ge(sem("w_rt_in"), 16)
        pe.wait_ge(sem("m_lo_ready"), 1)
        out_tile(0, 0, (0, 1))
        pe.wait_ge(sem("m_lo_ready"), 2)
        out_tile(1, 1, (0,))
        turn_tile(0, 0)
        out_tile(1, 1, (1,))
        route_tile(0)
        with pe.Fori(1, TT // 2) as i:
            for c in range(2):
                t = 2 * i + c
                pe.wait_ge(sem("m_lo_ready"), t + 1)
                pe.wait_ge(sem("y_evicted"), t - 1)
                out_tile(t, c, (0,))
                turn_tile(t - 1, 1 - c)
                out_tile(t, c, (1,))
                route_tile(t - 1)
        turn_tile(TT - 1, 1)
        route_tile(TT - 1)

        pe.wait_ge(sem("both_ready"), 1)
        M = both[:].rearrange("p t e -> p (t e)")
        nc.tensor.matmul(PS[0][:, 0:TT * E], tri[:], M, start=True, stop=False)
        for back in range(1, TT):
            nc.tensor.matmul(PS[0][:, back * E:TT * E], all_ones[:], M[:, 0:(TT - back) * E], start=False, stop=(back == TT - 1))
        for t in range(TT):
            last = nc.tensor.matmul(PS[1][:, 0:E], all_ones[:], M[:, t * E:(t + 1) * E], start=(t == 0), stop=(t == TT - 1))
        last.then_inc(sem("ranks_done"), 1)
        pe.sem_inc(sem("oh_free"), 2)

        def place(t):
            for k in range(2):
                pe.wait_ge(sem("oh_ready"), 2 * t + k + 1)
                edge = isinstance(t, int)
                nc.tensor.matmul(PS[2][:, 0:2 * MAX_BLOCKS], lane_oh[k][:], blk_oh[k][:].rearrange("p a b -> p (a b)"),
                                 start=(edge and t == 0 and k == 0), stop=(edge and t == TT - 1 and k == 1)).then_inc(sem("oh_free"), 1)

        place(0)
        with pe.Fori(1, TT - 1) as t:
            place(t)
        place(TT - 1)

        pe.wait_ge(sem("tables_ready"), 1)
        total = pe.value_load(ends[0:1, E - 1:E], min_val=E, max_val=MAX_BLOCKS)

        def turn_rows(g):
            pe.wait_ge(sem("xg_in"), 16 * (g + 1))
            wait(pe, sem("xT_ready"), g)
            for k in range(KD):
                last = nc.tensor.transpose(PS[2 + k // 4][:, (k % 4) * P:(k % 4 + 1) * P], xg[:, k * P:(k + 1) * P], ident[:])
            last.then_inc(sem("xgT_done"), 1)

        def gate_up(g, e):
            pe.wait_ge(sem("xT_ready"), g + 1)
            wait(pe, sem("h_ready"), g)
            for k in range(KD):
                for j in range(2):
                    last = nc.tensor.matmul(PS[j][:].rearrange("p (a n) -> p a n", a=1), xTs[:, k, :], gu[:, ds((e % 2) * KD + k, 1), j * DE:(j + 1) * DE],
                                            start=(k == 0), stop=(k == KD - 1))
            last.then_inc(sem("gu_done"), 1)

        def down(g, e):
            pe.wait_ge(sem("hT_ready"), g + 1)
            pe.wait_ge(sem("y_ready"), g + 1)
            for k in range(KE):
                for j in range(2):
                    last = nc.tensor.matmul(PS[4 + j][:].rearrange("p (a n) -> p a n", a=1), hTs[:, k, :], dn[:, ds((e % 2) * KE + k, 1), j * 512:(j + 1) * 512],
                                            start=(k == 0), stop=(k == KE - 1))
            last.then_inc(sem("down_done"), 1)

        def turn_hidden(g):
            pe.wait_ge(sem("h_ready"), g + 1)
            for k in range(KE):
                last = nc.tensor.transpose(PS[6][:, k * P:(k + 1) * P], hs[:, k * P:(k + 1) * P], ident[:])
            last.then_inc(sem("hT_done"), 1)

        turn_rows(0)
        pe.wait_ge(sem("gu_in0"), 32)
        gate_up(0, 0)
        turn_rows(1)
        pe.wait_ge(sem("dn_in0"), 16)
        turn_hidden(0)
        with pe.Fori(1, total) as g:
            e = pe.value_load(expert_of[0:1, ds(g, 1)], min_val=0, max_val=E - 1)
            e_was = pe.value_load(expert_of[0:1, ds(g - 1, 1)], min_val=0, max_val=E - 1)
            pe.wait_ge(sem("gu_in0"), 32 * (e // 2 + 1))
            pe.wait_ge(sem("gu_in1"), 32 * ((e + 1) // 2 + 1))
            gate_up(g, e)
            turn_rows(g + 1)
            pe.wait_ge(sem("dn_in0"), 16 * (e_was // 2 + 1))
            pe.wait_ge(sem("dn_in1"), 16 * ((e_was + 1) // 2 + 1))
            down(g - 1, e_was)
            turn_hidden(g)
        pe.wait_ge(sem("dn_in1"), 16 * (E // 2 + 1))
        down(total - 1, E - 1)


def kernel(**inputs):
    import numpy as _np
    import concourse.bacc as _bacc
    from concourse import mybir as _mybir
    from concourse.bass_utils import run_bass_kernel_spmd as _run

    a = {n: _np.asarray(v) for n, v in inputs.items()}
    w = a["w_in"][0]
    dil, qw, kvw = DIL_HEADS * HD, SWA_HEADS * HD, 2 * HD
    q0, k0, v0 = 0, 3 * dil, 6 * dil
    qb, kb, vb, gates = 9 * dil, 9 * dil + qw, 9 * dil + qw + kvw, 9 * dil + qw + 2 * kvw

    def columns(*runs):
        return _np.concatenate([w[:, at:at + n] for at, n in runs], axis=1)

    passes = [columns((q0 + p * P, P), (k0 + p * P, P), (v0 + p * P, P)) for p in range(6)]
    passes += [columns((qb + p * 4 * HD, 4 * HD), (kb + p * HD, HD), (vb + p * HD, HD)) for p in range(2)]
    gate = w[:, gates:].reshape(KD, P, 2, KD, P).transpose(3, 1, 0, 2, 4).reshape(KD, P, KD * 2 * P)
    branch = _np.concatenate([a["w_branch_a"][0], a["w_branch_b"][0]], axis=0)
    branch = branch.reshape(OUT_K, P, KD, P).transpose(2, 1, 0, 3).reshape(KD, P, OUT_K * P)
    laid = {n: a[n] for n in ("x", "c", "positions", "w_ada", "b_ada", "g_mix", "g_ffn", "g_final", "sink_logits", "w_out",
                              "w_expert_gate", "w_expert_up", "w_expert_down")}
    laid["w_qkv"] = _np.stack(passes)
    laid["w_gb"] = _np.concatenate([gate, branch], axis=2)
    laid["w_rt"] = _np.concatenate([a["w_group"][0], a["w_route"][0]], axis=1)
    laid["b_rt"] = _np.concatenate([a["b_group"], a["b_route"]], axis=1)

    nc = _bacc.Bacc("TRN2", target_bir_lowering=False, num_devices=1)
    arrays, A = {}, {}
    for n, v in laid.items():
        arrays[f"in_{n}"] = v = _np.ascontiguousarray(v)
        A[n] = nc.dram_tensor(f"in_{n}", v.shape, _mybir.dt.from_np(v.dtype), kind="ExternalInput").ap()
    out = nc.dram_tensor("out_0", (1, SEQ, D), _mybir.dt.float32, kind="ExternalOutput").ap()
    build(nc, A, out)
    r = _run(nc, [arrays], core_ids=[0])
    return r.results[0]["out_0"]
```

```python
import numpy as np
import concourse.bass as bass
from concourse import mybir
from contextlib import ExitStack

F32 = mybir.dt.float32
F32R = mybir.dt.float32r
BF16 = mybir.dt.bfloat16
F16 = mybir.dt.float16
I32 = mybir.dt.int32
ALU = mybir.AluOpType
ACT = mybir.ActivationFunctionType
AX = mybir.AxisListType
ds = bass.ds

P = 128
SEQ = 2048
D = 1024
KD = D // P
TT = SEQ // P
HD = 64
HALF = HD // 2
DILATIONS = (1, 4, 16)
DIL_HEADS = 4
SWA_HEADS = 8
SCALE = HD ** -0.5
EPS = 1e-6
NEG = -1e30
THETA = 10000.0
N_MOD = 6
E = 32
GROUPS = 4
PER_GROUP = E // GROUPS
DE = 512
KE = DE // P
BLK = 128
MAX_BLOCKS = SEQ * 2 // BLK + E
PAD_ROWS = P
ROUND = 4
LAG = ROUND + 1
RING = 6
PIECES = KD + KE
assert PIECES == 2 * RING

CHUNK = 512

MOD_LOADS = N_MOD * D // CHUNK // 4
OUT_LOADS = KD // 4

PASSES = 8
PASS_COLS = 384
TILES_PER_GROUP = 2 * TT
PIECE = PASS_COLS // 2
SWA_T0 = 3 * TILES_PER_GROUP
STEPS = 4 * TILES_PER_GROUP
STAT = HD + 2

OUT_K = 6
GATE_COLS = KD * 2 * P + OUT_K * P
CHUNKS = SEQ // CHUNK


def wait(eng, sem, n):
    if not (isinstance(n, int) and n <= 0):
        eng.wait_ge(sem, n)


class Chain:

    def __init__(self, eng, sem):
        self.eng, self.sem, self.n = eng, sem, 0

    def __call__(self, ins):
        ins.then_inc(self.sem, 1)
        self.n = self.n + 1
        return ins

    def join(self):
        wait(self.eng, self.sem, self.n)


def two_pi_parts():
    rest, parts = 2 * np.pi, []
    for bits in (8, 10, 24):
        scale = 2.0 ** (bits - 1 - np.floor(np.log2(rest)))
        parts.append(float(np.float32(np.floor(rest * scale) / scale)))
        rest -= parts[-1]
    return parts


def build(nc, A, out, debug=False):
    ctx = ExitStack()
    with ctx:
        body(nc, A, out, ctx, debug)


def body(nc, A, out, ctx, debug):
    kind = "ExternalOutput" if debug else "Internal"

    def dram(name, shape, dt=F32):
        return nc.dram_tensor(name, shape, dt, kind=kind).ap()

    o_dil = dram("o_dil", [3, SEQ, DIL_HEADS * STAT])
    o_swa = dram("o_swa", [SEQ, SWA_HEADS * HD])
    rows_d = dram("mod_rows", [5, D])
    oT_d = dram("oT_d", [P, OUT_K, SEQ])
    mT_d = dram("mT_d", [P, KD, SEQ])
    x1_d = dram("x1_d", [SEQ, D])
    h2_d = dram("h2_d", [SEQ + PAD_ROWS // 2, D])
    y_d = dram("y_d", [2 * SEQ + PAD_ROWS, D])

    class Plan:
        def __init__(self, at):
            self.at = at

        def __call__(self, name, shape, dt=F32):
            size = int(np.prod(shape[1:])) * {F32: 4, F32R: 4, I32: 4, BF16: 2, F16: 2}[dt]
            t = nc.alloc_sbuf_tensor_at("sb_" + name, shape, dt, offset=self.at)
            self.at += (size + 31) // 32 * 32
            return t

    base = nc.sbuf_base
    base = (base + 31) // 32 * 32
    keep = Plan(base)
    ident = keep("ident", [P, P])
    ones_row = keep("ones_row", [1, 2])
    A1 = keep("A1", [P, KD])
    B1 = keep("B1", [P, KD])
    hT = keep("hT", [P, KD, SEQ])
    after_hT = keep.at

    m0 = Plan(after_hT - KD * SEQ * 4)
    wada = [m0(f"wada{i}", [P, KD, CHUNK]) for i in range(4)]
    m0b = Plan(after_hT)
    c_col = m0b("c_col", [P, KD])
    c_sil = m0b("c_sil", [P, KD])
    ones = m0b("ones", [P, P])
    c_bc = m0b("c_bc", [P, KD, P])
    mod = m0b("mod", [P, N_MOD * D])
    b_bc = m0b("b_bc", [P, N_MOD * D])
    g_bc = m0b("g_bc", [P, 3, D])

    m1 = Plan(after_hT)
    xt = [m1(f"xt{c}", [P, D]) for c in range(2)]
    sq = m1("sq", [P, D])
    xn = m1("xn", [P, D])
    stat1 = m1("stat1", [P, 4])

    m2 = Plan(after_hT)
    w_raw = [m2(f"w_raw{c}", [P, PIECE]) for c in range(2)]
    w_hi = m2("w_hi", [P, 2 * KD, PASS_COLS], F32R)
    w_lo = m2("w_lo", [P, 2 * KD, PASS_COLS], F32R)
    h_hi = [m2(f"h_hi{c}", [P, KD, P], F32R) for c in range(2)]
    h_lo = [m2(f"h_lo{c}", [P, KD, P], F32R) for c in range(2)]
    kT_dil = m2("kT_dil", [P, SEQ + 2 * HD])
    v_dil = m2("v_dil", [P, TT + 1, P])
    kT_swa = m2("kT_swa", [P, SEQ + 2 * P])
    v_swa = m2("v_swa", [P, TT + 2, HD])
    qk_raw = m2("qk_raw", [P, 320])
    qk_tmp = m2("qk_tmp", [P, 320])
    qk_rot = m2("qk_rot", [P, 320])
    cos_t = m2("cos_t", [P, 3 * TT, HALF])
    sin_t = m2("sin_t", [P, 3 * TT, HALF])
    qst = [m2(f"qst{c}", [P, 4, P]) for c in range(2)]
    mask_dil = m2("mask_dil", [P, 4, 256], BF16)
    mask_swa = m2("mask_swa", [P, 3, 384], BF16)
    e_sb = [m2(f"e_sb{u}", [P, 2, 384]) for u in range(2)]
    eT = m2("eT", [P, 2, 384])
    o_row = [[m2(f"o_row{c}{u}", [P, 2, STAT]) for u in range(2)] for c in range(2)]
    mx = m2("mx", [P, 2])
    nm = m2("nm", [P, 2])
    snk = [[m2(f"snk{c}{u}", [P, 2]) for u in range(2)] for c in range(2)]
    esk = [[m2(f"esk{c}{u}", [P, 2]) for u in range(2)] for c in range(2)]
    rden = m2("rden", [P, 2])
    sink_bc = m2("sink_bc", [P, SWA_HEADS])
    nsink = m2("nsink", [P, SWA_HEADS])
    assert m2.at <= nc.sbuf_usable_end, (m2.at, nc.sbuf_usable_end)
    mt = Plan(after_hT + 2 * PIECE * 4)
    pos_i = mt("pos_i", [P, 3 * TT], I32)
    pos_f = mt("pos_f", [P, 3 * TT])
    invf = mt("invf", [P, HALF])
    ang = mt("ang", [P, 3 * TT, HALF])
    turn = mt("turn", [P, 3 * TT, HALF])

    m4 = Plan(after_hT)
    x_hi = [m4(f"x_hi{c}", [P, KD, CHUNK], F32R) for c in range(2)]
    g_raw = [m4(f"g_raw{j}", [P, GATE_COLS // 2]) for j in range(2)]
    g_hi = [m4(f"g_hi{c}", [P, GATE_COLS], F32R) for c in range(2)]
    g_lo = [m4(f"g_lo{c}", [P, GATE_COLS], F32R) for c in range(2)]
    sig = m4("sig", [P, 2, CHUNK])
    mg = [m4(f"mg{c}", [P, CHUNK]) for c in range(2)]
    after_weights = m4.at
    o_hi = [m4(f"o_hi{c}", [P, OUT_K, CHUNK], F32R) for c in range(2)]
    o_lo = [m4(f"o_lo{c}", [P, OUT_K, CHUNK], F32R) for c in range(2)]
    assert m4.at <= nc.sbuf_usable_end, m4.at

    m3 = Plan(after_weights)
    od = [m3(f"od{c}", [P, 3, DIL_HEADS * STAT]) for c in range(2)]
    ob = [m3(f"ob{c}", [P, SWA_HEADS * HD]) for c in range(2)]
    wsum = m3("wsum", [P, 3, DIL_HEADS * HD])
    oa = m3("oa", [P, DIL_HEADS * HD])
    oT = [m3(f"oT{c}", [P, OUT_K, P]) for c in range(2)]
    nmin = m3("nmin", [P, DIL_HEADS])
    wg = m3("wg", [P, 3, DIL_HEADS])
    wden = m3("wden", [P, 3, DIL_HEADS])
    dsum = m3("dsum", [P, DIL_HEADS])
    assert m3.at <= nc.sbuf_usable_end, m3.at

    tables = Plan(after_hT - KD * SEQ * 4)
    pair_w = tables("pair_w", [P, TT, 2])
    scatter_idx = tables("scatter_idx", [P, MAX_BLOCKS + 1], I32)
    gather_idx = tables("gather_idx", [P, MAX_BLOCKS + 1], I32)
    expert_of = tables("expert_of", [1, MAX_BLOCKS + 1], I32)
    ends = tables("ends", [1, E], I32)

    m5 = Plan(tables.at)
    logits = m5("logits", [P, TT, GROUPS + E])
    wo_raw = [m5(f"wo_raw{c}", [P, D]) for c in range(4)]
    wo_hi = m5("wo_hi", [P, KD, D], F32R)
    wo_lo = m5("wo_lo", [P, KD, D], F32R)
    gt1b = m5("gt1b", [P, D])
    A2b = m5("A2b", [P, D])
    B2b = m5("B2b", [P, D])
    m_in = [m5(f"m_in{c}", [P, KD, P]) for c in range(2)]
    m_hi = [m5(f"m_hi{c}", [P, KD, P], F32R) for c in range(2)]
    m_lo = [m5(f"m_lo{c}", [P, KD, P], F32R) for c in range(2)]
    x_in = [m5(f"x_in{c}", [P, D]) for c in range(2)]
    x1 = [m5(f"x1{c}", [P, D]) for c in range(2)]
    h2 = [m5(f"h2{c}", [P, D]) for c in range(2)]
    h2T = m5("h2T", [P, KD, P])
    sq2 = m5("sq2", [P, D])
    zero_rows = m5("zero_rows", [PAD_ROWS // 2, D])
    w_rt = m5("w_rt", [P, KD, GROUPS + E])
    st2 = m5("st2", [P, 8])
    assert m5.at <= nc.sbuf_usable_end

    m6 = Plan(tables.at + TT * (GROUPS + E) * 4)
    ug = lambda name, n, dt=F32: m6(name, [P, TT, n], dt)
    r_bias = m6("r_bias", [P, GROUPS + E])
    iota_e = m6("iota_e", [P, TT, E])
    iota_r = m6("iota_r", [P, P])
    iota_b = m6("iota_b", [P, MAX_BLOCKS])
    flat_id = m6("flat_id", [P, TT, 2])
    pad_id = m6("pad_id", [P, 2])
    tri = m6("tri", [P, P], BF16)
    all_ones = m6("all_ones", [P, P], BF16)
    gmax = ug("gmax", 1)
    geq = ug("geq", GROUPS)
    gsel = ug("gsel", GROUPS)
    gex = ug("gex", GROUPS)
    gsum = ug("gsum", 1)
    gidx = ug("gidx", 1)
    el = ug("el", E)
    eeq = ug("eeq", E)
    oh = [ug(f"oh{k}", E) for k in range(2)]
    top = [ug(f"top{k}", 1) for k in range(2)]
    eidx = ug("eidx", 1)
    ratio = ug("ratio", 1)
    rinv = ug("rinv", 1)
    both = ug("both", E, BF16)
    posn = ug("posn", E)
    prod = ug("prod", E)
    slot_f = ug("slot_f", 2)
    slot_i = ug("slot_i", 2, I32)
    lane_i = ug("lane_i", 2, I32)
    blk_i = ug("blk_i", 2, I32)
    lane_f = ug("lane_f", 2)
    blk_f = ug("blk_f", 2)
    cnt = m6("cnt", [P, E])
    cnt_i = m6("cnt_i", [P, E], I32)
    nblk = m6("nblk", [P, E])
    pend = m6("pend", [P, E])
    pbase = m6("pbase", [P, E])
    cmp_e = m6("cmp_e", [P, MAX_BLOCKS, E])
    e_f = m6("e_f", [P, MAX_BLOCKS])
    lane_oh = [m6(f"lane_oh{k}", [P, P], F16) for k in range(2)]
    blk_oh = [m6(f"blk_oh{k}", [P, 2, MAX_BLOCKS], F16) for k in range(2)]
    tab = m6("tab", [P, 2, MAX_BLOCKS])
    idx_f = m6("idx_f", [P, MAX_BLOCKS])

    m8 = Plan(tables.at)
    xg = m8("xg", [P, D])
    x_hiT = m8("x_hiT", [P, KD, P], F32R)
    x_loT = m8("x_loT", [P, KD, P], F32R)
    hg = m8("hg", [P, DE])
    h_hiT = m8("h_hiT", [P, KE, P], F32R)
    h_loT = m8("h_loT", [P, KE, P], F32R)
    y_sb = m8("y_sb", [P, D])
    gi = m8("gi", [P, 1], I32)
    si = m8("si", [P, 1], I32)
    dn_hi = m8("dn_hi", [P, KE, D], F32R)
    dn_lo = m8("dn_lo", [P, KE, D], F32R)
    gu = m8("gu", [P, 4 * KD, 2 * DE], F32R)
    assert m8.at - 2 * KD * 2 * DE * 4 >= m6.at
    w_in = [m8(f"w_in{s}", [P, 2 * DE]) for s in range(RING)]
    assert m8.at <= nc.sbuf_usable_end, (m8.at, nc.sbuf_usable_end)
    m9 = Plan(tables.at)
    yp = [m9(f"yp{r}", [P, 2, D]) for r in range(ROUND)]
    xl = [m9(f"xl{r}", [P, D]) for r in range(ROUND)]
    acc = m9("acc", [P, 2 * ROUND, D])
    sq3 = m9("sq3", [P, D])
    gt2b = m9("gt2b", [P, D])
    gfb = m9("gfb", [P, D])
    ssq3 = m9("ssq3", [P, ROUND])
    ms3 = m9("ms3", [P, ROUND])
    rms3 = m9("rms3", [P, ROUND])
    rstd3 = m9("rstd3", [P, ROUND])

    bank = [ctx.enter_context(nc.psum_tensor(f"bank{i}", [P, 512], F32)) for i in range(3)]
    S_ps = ctx.enter_context(nc.psum_tensor("S_ps", [P, 2, 512], F32))
    E_ps = ctx.enter_context(nc.psum_tensor("E_ps", [P, 2, 512], F32))
    O_ps = ctx.enter_context(nc.psum_tensor("O_ps", [P, 512], F32))

    PS = [bank[0], bank[1], bank[2], S_ps[:, 0, :], S_ps[:, 1, :], E_ps[:, 0, :], E_ps[:, 1, :], O_ps]

    sems = {}

    def sem(name):
        if name not in sems:
            sems[name] = ctx.enter_context(nc.semaphore(name))
        return sems[name]

    inv_freq = (np.float32(THETA) ** (-np.arange(HALF, dtype=np.float32) * np.float32(2.0 / HD))).astype(np.float32)
    PI2 = two_pi_parts()
    MAGIC = 1.5 * 2.0 ** 23

    block = ctx.enter_context(nc.Block())

    def dilation(g):
        return DILATIONS[g] if g < 3 else 1

    def tile_of(T):
        return T % TT

    def first_token(g, t):
        d = dilation(g)
        per = TT // d
        return (t % per) * (P * d) + t // per

    def mask_index(g, t):
        if g == 2:
            return 3
        per = TT // dilation(g)
        m = t % per
        return (m + per - 1) // per + m // (per - 1)

    def unit(g, T, u):
        return T if g < 3 else 2 * T - SWA_T0 + u

    def units(g):
        return (0,) if g < 3 else (0, 1)

    def weight_row(n):
        return ((n // TT) % 2) * KD + (n % TT) // 2

    def gu_row(e, part, k):
        return ((e + 1) % 2 * 2 + part) * KD + k

    def ring_count(e, j):
        first = 2 if j % RING >= 2 * RING - KD else 1
        return 16 * (first + 2 * e + j // RING + 1)

    def group_of(T):
        return min(max(T, 0) // TILES_PER_GROUP, 3)

    def schedule(eng, step):
        def straight(T):
            gs = [group_of(x) if 0 <= x < STEPS else None for x in (T + 1, T, T - 1, T - 2, T - 3)]
            step(T, T % 2, gs, T < STEPS - TT)

        def looped(g, first, last, loads):
            with eng.Fori(first // 2, last // 2) as i:
                for c in range(2):
                    step(2 * i + c, c, [g] * 5, loads)

        for g in range(4):
            T0 = g * TILES_PER_GROUP
            for T in range(T0, T0 + 4):
                straight(T)
            end = T0 + TILES_PER_GROUP - 2
            if g < 3:
                looped(g, T0 + 4, end, True)
            else:
                looped(g, T0 + 4, STEPS - TT - 2, True)
                straight(STEPS - TT - 2)
                straight(STEPS - TT - 1)
                looped(g, STEPS - TT, end, False)
            for T in range(end, T0 + TILES_PER_GROUP):
                straight(T)
        for T in range(STEPS, STEPS + 3):
            straight(T)

    def acc_row(t):
        return acc[:, ds(t % (2 * ROUND), 1), :].rearrange("p a n -> p (a n)")

    def chunk_loops(eng, chunk):
        with eng.Fori(0, CHUNKS // 2 - 1) as i:
            for c in range(2):
                chunk(2 * i + c, c, True)
        for c in range(2):
            chunk(CHUNKS - 2 + c, c, c == 0)

    @block.sync
    def _(sp):
        sp.dma_start(c_col[:], A["c"].rearrange("a (k p) -> p (a k)", p=P), allow_slow_non_contiguous=True).then_inc(sem("c_in"), 16)
        wv = A["w_ada"].rearrange("a (k p) n -> p (a k) n", p=P)
        for j in range(N_MOD * D // CHUNK):
            wait(sp, sem("mod_mm"), j - 3)
            sp.dma_start(wada[j % 4][:], wv[:, :, j * CHUNK:(j + 1) * CHUNK]).then_inc(sem(f"slot_in{j % 4}"), 16)
            if j == 1:
                sp.dma_start(b_bc[:], A["b_ada"][0:1, :].broadcast_to([P, N_MOD * D])).then_inc(sem("g_in"), 16)
                for n, g in enumerate(("g_mix", "g_ffn", "g_final")):
                    src = A[g] if g != "g_final" else A[g].rearrange("(a n) -> a n", a=1)
                    sp.dma_start(g_bc[:, n, :], src[0:1, :].broadcast_to([P, D])).then_inc(sem("g_in"), 16)
        sp.wait_ge(sem("mod_rows_ready"), 1)
        for n, src in enumerate((mod[0:1, 2 * D:3 * D], mod[0:1, 5 * D:6 * D], mod[0:1, 4 * D:5 * D], mod[0:1, 3 * D:4 * D], g_bc[0:1, 2, :])):
            sp.dma_start(rows_d[n:n + 1, :], src).then_inc(sem("rows_out"), 16)
        sp.wait_ge(sem("rows_out"), 80)
        sp.wait_ge(sem("cols_ready"), 1)
        xv = A["x"].rearrange("a (t p) n -> p (a t) n", p=P)
        with sp.Fori(0, TT // 2) as i:
            for c in range(2):
                sp.wait_ge(sem(f"x_free{c}"), i + 1)
                sp.dma_start(xt[c][:], xv[:, ds(2 * i + c, 1), :].rearrange("p a n -> p (a n)")).then_inc(sem(f"x_in{c}"), 16)
        sp.wait_ge(sem("h_all"), TT + 1)
        pos = A["positions"]
        sp.dma_start(pos_i[:, 0:TT], pos.rearrange("a (t i) -> i (a t)", i=P), allow_slow_non_contiguous=True).then_inc(sem("pos_in"), 16)
        for r in range(4):
            sp.dma_start(pos_i[:, TT + 4 * r:TT + 4 * r + 4], pos.rearrange("a (b i r) -> r i (a b)", i=P, r=4)[r], allow_slow_non_contiguous=True).then_inc(sem("pos_in"), 16)
        sp.dma_start(pos_i[:, 2 * TT:3 * TT], pos.rearrange("a (i r) -> i (a r)", i=P)).then_inc(sem("pos_in"), 16)
        sp.dma_start(sink_bc[:], A["sink_logits"][0:1, :].broadcast_to([P, SWA_HEADS])).then_inc(sem("pos_in"), 16)

        wq = A["w_qkv"].rearrange("n (k p) m -> p n k m", p=P)

        def piece(n, c):
            wait(sp, sem("w_lo_ready"), n - 1)
            t = n % TT
            sp.dma_start(w_raw[c][:].rearrange("p (a b m) -> p a b m", a=1, b=1), wq[:, ds(n // TT, 1), ds(t // 2, 1), c * PIECE:(c + 1) * PIECE]).then_inc(sem(f"w_in{c}"), 16)

        for n in range(TT + 2):
            if n == 0:
                sp.wait_ge(sem("angles_ready"), 1)
            piece(n, n % 2)

        def step(T, c, gs, loads):
            g = gs[4]
            if g is not None:
                S = T - 3
                s, t = (S // TT) % 2, tile_of(S)
                tok = first_token(g, t)
                for u in units(g):
                    sp.wait_ge(sem("o_done"), unit(g, S, u) + 1)
                    if g < 3:
                        d = dilation(g)
                        dst = o_dil[g:g + 1, ds(tok, P, step=d), ds(s * (2 * STAT), 2 * STAT)]
                        src = o_row[1 - c][u][:].rearrange("p h m -> p (h m)")
                        dst = dst.rearrange("a p m -> (a p) m")
                    else:
                        dst = o_swa[ds(tok, P), ds(s * 256 + u * 128, 128)].rearrange("p (h m) -> p h m", h=2)
                        src = o_row[1 - c][u][:, :, 0:HD]
                    sp.dma_start(dst, src).then_inc(sem(f"o_out{1 - c}{u}"), 16)
            if loads and not (isinstance(T, int) and T + TT + 2 >= PASSES * TT):
                piece(T + TT + 2, c)

        schedule(sp, step)
        for c in range(2):
            sp.wait_ge(sem(f"o_out{c}0"), 16 * STEPS // 2)
            sp.wait_ge(sem(f"o_out{c}1"), 16 * TILES_PER_GROUP // 2)
        gv = A["w_gb"]

        def gate_piece(tile, j, last_use):
            wait(sp, sem("g_lo_ready"), last_use)
            cols = slice(j * (GATE_COLS // 2), (j + 1) * (GATE_COLS // 2))
            sp.dma_start(g_raw[j][:], gv[ds(tile, 1), :, cols].rearrange("a p m -> (a p) m")).then_inc(sem(f"g_in{j}"), 16)

        for j in range(2):
            gate_piece(0, j, 0)

        odv = o_dil.rearrange("g (t p) m -> p t g m", p=P)
        obv = o_swa.rearrange("(t p) m -> p t m", p=P)

        def merge_in(t, c):
            sp.dma_start(od[c][:], odv[:, ds(t, 1)].rearrange("p a g m -> p (a g) m")).then_inc(sem(f"od_in{c}"), 16)
            sp.dma_start(ob[c][:], obv[:, ds(t, 1)].rearrange("p a m -> p (a m)")).then_inc(sem(f"od_in{c}"), 16)

        def merge_out(t, c):
            sp.wait_ge(sem("oT_ready"), t + 2)
            sp.dma_start(oT_d[:, :, ds(t * P, P)], oT[c][:]).then_inc(sem(f"oT_out{c}"), 16)

        for c in range(2):
            sp.sem_inc(sem(f"oT_out{c}"), 16)
            merge_in(c, c)
        with sp.Fori(0, TT // 2 - 1) as i:
            for c in range(2):
                merge_out(2 * i + c, c)
                merge_in(2 * i + c + 2, c)
        for c in range(2):
            merge_out(TT - 2 + c, c)
        for c in range(2):
            sp.wait_ge(sem(f"oT_out{c}"), 16 * (TT // 2 + 1))

        def branch_inputs(q, cc):
            sp.dma_start(o_lo[cc][:].bitcast(F32), oT_d[:, :, ds(q * CHUNK, CHUNK)]).then_inc(sem("o_in"), 16)

        def chunk(q, cc, more):
            with sp.Fori(0, KD // 2) as i:
                for c in range(2):
                    for j in range(2):
                        gate_piece((2 * i + c + 1) % KD, j, 2 * (KD * q + 2 * i + c) + j + 1)
            if more:
                sp.wait_ge(sem("gates_done"), KD * q + 2)
                branch_inputs(q + 1, 1 - cc)

        branch_inputs(0, 0)
        chunk_loops(sp, chunk)

        wov = A["w_out"].rearrange("a (k p) n -> p (a k) n", p=P)
        sp.wait_ge(sem("merged"), CHUNKS * KD)
        sp.wait_ge(sem("g_lo_ready"), 2 * CHUNKS * KD + 2)
        for c in range(2):
            sp.wait_ge(sem(f"mT_out{c}"), 16 * (CHUNKS * KD // 2 + 1))
        def tile_in(t, c):
            sp.dma_start(m_in[c][:], mT_d[:, :, ds(t * P, P)]).then_inc(sem(f"m_in{c}"), 16)
            sp.dma_start(x_in[c][:], xv[:, ds(t, 1), :].rearrange("p a n -> p (a n)")).then_inc(sem(f"x_in{c}"), 16)

        for k in range(KD):
            wait(sp, sem("wo_lo_ready"), k - 3)
            sp.dma_start(wo_raw[k % 4][:], wov[:, k, :]).then_inc(sem(f"slot_in{k % 4}"), 16)
            if k == 3:
                tile_in(0, 0)
                for n, (t, row) in enumerate(((gt1b, 0), (A2b, 2), (B2b, 3))):
                    sp.dma_start(t[:], rows_d[row:row + 1, :].broadcast_to([P, D])).then_inc(sem("rows_in"), 16)
                sp.dma_start(w_rt[:], A["w_rt"].rearrange("(k p) n -> p k n", p=P)).then_inc(sem("rows_in"), 16)
                sp.wait_ge(sem("zero_rows"), 1)
                sp.dma_start(h2_d[SEQ:SEQ + PAD_ROWS // 2, :], zero_rows[:]).then_inc(sem("pads_out"), 16)

        def tile_out(t, c):
            sp.wait_ge(sem("h2_ready"), t + 1)
            sp.dma_start(x1_d[ds(t * P, P), :], x1[c][:]).then_inc(sem(f"x1_out{c}"), 16)
            sp.dma_start(h2_d[ds(t * P, P), :], h2[c][:]).then_inc(sem(f"x1_out{c}"), 16)

        tile_in(1, 1)
        with sp.Fori(0, TT // 2 - 1) as i:
            for c in range(2):
                tile_out(2 * i + c, c)
                tile_in(2 * i + c + 2, c)
        for c in range(2):
            tile_out(TT - 2 + c, c)
        for c in range(2):
            sp.wait_ge(sem(f"x1_out{c}"), 32 * (TT // 2))
        sp.wait_ge(sem("pads_out"), 16)
        sp.sem_inc(sem("h2_stored"), 1)

        sp.wait_ge(sem("logits_ready"), TT)
        sp.dma_start(r_bias[:], A["b_rt"][0:1, :].broadcast_to([P, GROUPS + E])).then_inc(sem("rows_in"), 16)
        wgu_v = A["w_gate_up"].rearrange("e (k p) n -> p e k n", p=P)
        wd_v = A["w_expert_down"].rearrange("a e (k p) n -> p (a e) k n", p=P)

        def gu_piece(e, k, slot):
            sp.dma_start(w_in[slot][:].rearrange("p (a n) -> p a n", a=1), wgu_v[:, ds(e, 1), k, :]).then_inc(sem(f"ring_in{slot}"), 16)

        def dn_piece(e, k, slot):
            sp.dma_start(w_in[slot][:].rearrange("p (a n) -> p a n", a=1), wd_v[:, ds(e, 1), k, :]).then_inc(sem(f"ring_in{slot}"), 16)

        for k in range(KD):
            slot = (k + 2 * RING - KD) % RING
            if k >= RING:
                sp.wait_ge(sem("gu_lo_ready"), k - RING + 1)
            gu_piece(0, k, slot)

        def expert_in(e):
            for j in range(PIECES):
                if j >= RING:
                    sp.wait_ge(sem("gu_lo_ready"), KD * (e + 1) + j - RING + 1)
                elif isinstance(e, int) and e == 0:
                    sp.wait_ge(sem("gu_lo_ready"), KD - RING + j + 1)
                elif j < RING - KE:
                    sp.wait_ge(sem("gu_lo_ready"), KD * e + RING + j + 1)
                else:
                    sp.wait_ge(sem("dn_lo_ready"), KE * e - RING + j + 1)
                if j < KD:
                    gu_piece(e + 1, j, j % RING)
                else:
                    dn_piece(e, j - KD, j % RING)

        expert_in(0)
        with sp.Fori(1, E - 1) as e:
            expert_in(e)
        for k in range(KE):
            sp.wait_ge(sem("dn_lo_ready"), KE * (E - 2) + k + 1)
            dn_piece(E - 1, k, (KD + k) % RING)

        sp.wait_ge(sem("experts_done"), 1)
        for n, (t, row) in enumerate(((gt2b, 1), (gfb, 4))):
            sp.dma_start(t[:], rows_d[row:row + 1, :].broadcast_to([P, D])).then_inc(sem("rows_in"), 16)
        yv = y_d[0:2 * SEQ, :].rearrange("(t p two) n -> p t two n", p=P, two=2)
        x1v = x1_d.rearrange("(t p) n -> p t n", p=P)
        ov = out.rearrange("a (t p) n -> p (a t) n", p=P)

        def last_in(t, r):
            sp.dma_start(yp[r][:], yv[:, ds(t, 1)].rearrange("p a two n -> p (a two) n")).then_inc(sem(f"slot_in{r}"), 16)
            sp.dma_start(xl[r][:], x1v[:, ds(t, 1)].rearrange("p a n -> p (a n)")).then_inc(sem(f"slot_in{r}"), 16)

        def last_out(t, r):
            sp.wait_ge(sem("out_ready"), t + 1)
            sp.dma_start(ov[:, ds(t, 1), :].rearrange("p a n -> p (a n)"), acc_row(t)).then_inc(sem(f"out_stored{r}"), 16)

        for r in range(ROUND):
            sp.sem_inc(sem(f"out_stored{r}"), 16)
            last_in(r, r)

        def last_round(q, more):
            for r in range(ROUND):
                t = ROUND * q + r
                if more:
                    sp.wait_ge(sem("acc_ready"), t + 1)
                    last_in(t + ROUND, r)
                if not isinstance(t, int) or t >= LAG:
                    last_out(t - LAG, (r - LAG) % ROUND)

        last_round(0, True)
        last_round(1, True)
        with sp.Fori(2, TT // ROUND - 1) as q:
            last_round(q, True)
        last_round(TT // ROUND - 1, False)
        for t in range(TT - LAG, TT):
            last_out(t, t % ROUND)
        for r in range(ROUND):
            sp.wait_ge(sem(f"out_stored{r}"), 16 * (TT // ROUND + 1))

    @block.gpsimd
    def _(pool):
        ch = Chain(pool, sem("pool_chain"))
        ch(nc.gpsimd.memset(ident[:], 0.0))
        ch(nc.gpsimd.memset(ones_row[:], 1.0))
        ch(nc.gpsimd.memset(ones[:], 1.0))
        ch.join()
        nc.gpsimd.affine_select(out=ident[:], in_=ident[:], compare_op=ALU.not_equal, fill=1.0, base=0,
                                pattern=[[-1, P]], channel_multiplier=1).then_inc(sem("ident_ready"), 1)
        pool.wait_ge(sem("h_all"), TT + 1)
        for k in range(HALF):
            last = nc.gpsimd.memset(invf[:, k:k + 1], float(inv_freq[k]))
        last.then_inc(sem("invf_ready"), 1)
        for q in qst:
            ch(nc.gpsimd.memset(q[:], 0.0))
        for t, lo, hi in ((kT_dil, 0, HD), (kT_dil, HD + SEQ, 2 * HD + SEQ), (kT_swa, 0, P), (kT_swa, P + SEQ, 2 * P + SEQ)):
            ch(nc.gpsimd.memset(t[:, lo:hi], 0.0))
        ch(nc.gpsimd.memset(v_dil[0:HD, 0, :], 0.0))
        ch.join()
        ch(nc.gpsimd.memset(v_dil[HD:P, TT, :], 0.0))
        ch.join()
        ch(nc.gpsimd.memset(v_swa[:, 0, :], 0.0))
        ch(nc.gpsimd.memset(v_swa[:, TT + 1, :], 0.0))
        for m, w, var in ((mask_dil, HD, 4), (mask_swa, P, 3)):
            n = P + 2 * w
            ch(nc.gpsimd.memset(m[:], 0.0))
            ch.join()
            for v in range(var):
                cuts = [(1, -1, 0), (-1, 1, 2 * w)]
                if v in (0, 3):
                    cuts.append((1, 0, -w))
                if v in (2, 3):
                    cuts.append((-1, 0, P + w - 1))
                for step_c, step_i, b in cuts:
                    ch(nc.gpsimd.affine_select(out=m[:, v, :], in_=m[:, v, :], compare_op=ALU.is_ge, fill=NEG, base=b,
                                               pattern=[[step_c, n]], channel_multiplier=step_i))
                    ch.join()
        nc.gpsimd.memset(mx[:], 0.0).then_inc(sem("attn_consts"), 1)

        def tile_src(g, T):
            tok = first_token(g, tile_of(T))
            return hT[:, :, ds(tok, P, step=dilation(g))]

        def lower_tile(T, c, g):
            pool.wait_ge(sem("h_hi_ready"), T + 1)
            nc.gpsimd.tensor_tensor(h_lo[c][:], tile_src(g, T), h_hi[c][:].bitcast(F32), ALU.subtract).then_inc(sem("h_lo_ready"), 1)

        def lower_piece(n, c):
            pool.wait_ge(sem("w_hi_ready"), n + 1)
            k = weight_row(n)
            cols = slice(c * PIECE, (c + 1) * PIECE)
            raw = w_raw[c][:].rearrange("p (a m) -> p a m", a=1)
            nc.gpsimd.tensor_tensor(w_lo[:, ds(k, 1), cols], raw, w_hi[:, ds(k, 1), cols].bitcast(F32), ALU.subtract).then_inc(sem("w_lo_ready"), 1)

        for n in range(TT):
            lower_piece(n, n % 2)
        lower_tile(0, 0, 0)

        def step(T, c, gs, loads):
            if gs[0] is not None:
                lower_tile(T + 1, 1 - c, gs[0])
            if loads and not (isinstance(T, int) and T + TT >= PASSES * TT):
                lower_piece(T + TT, c)

        schedule(pool, step)

        def lower_gate(n, c):
                for j in range(2):
                    pool.wait_ge(sem("g_hi_ready"), 2 * n + j + 1)
                    cols = slice(j * (GATE_COLS // 2), (j + 1) * (GATE_COLS // 2))
                    nc.gpsimd.tensor_tensor(g_lo[c][:, cols], g_raw[j][:], g_hi[c][:, cols].bitcast(F32), ALU.subtract).then_inc(sem("g_lo_ready"), 1)

        lower_gate(0, 0)
        with pool.Fori(0, CHUNKS * KD // 2) as i:
            for c in range(2):
                lower_gate(2 * i + c + 1, 1 - c)
        pool.wait_ge(sem("wo_hi_ready"), 1)
        nc.gpsimd.memset(zero_rows[:], 0.0).then_inc(sem("zero_rows"), 1)
        with pool.Fori(0, TT // 2) as i:
            for c in range(2):
                pool.wait_ge(sem("m_hi_ready"), 2 * i + c + 1)
                nc.gpsimd.tensor_tensor(m_lo[c][:], m_in[c][:], m_hi[c][:].bitcast(F32), ALU.subtract).then_inc(sem("m_lo_ready"), 1)

        pool.wait_ge(sem("logits_ready"), TT)
        exact = dict(allow_small_or_imprecise_dtypes=True)
        ch(nc.gpsimd.iota(iota_e[:], pattern=[[0, TT], [1, E]], base=0, channel_multiplier=0, **exact))
        ch(nc.gpsimd.iota(iota_r[:], pattern=[[1, P]], base=0, channel_multiplier=0, **exact))
        ch(nc.gpsimd.iota(iota_b[:], pattern=[[1, MAX_BLOCKS]], base=0, channel_multiplier=0, **exact))
        ch(nc.gpsimd.iota(flat_id[:], pattern=[[2 * P, TT], [1, 2]], base=-SEQ, channel_multiplier=2, **exact))
        ch(nc.gpsimd.iota(pad_id[:, 0:1], pattern=[[0, 1]], base=2 * SEQ, channel_multiplier=1, **exact))
        ch(nc.gpsimd.iota(pad_id[:, 1:2], pattern=[[0, 1]], base=SEQ - 2 * SEQ, channel_multiplier=-1, **exact))
        ch(nc.gpsimd.memset(all_ones[:], 1.0))
        ch(nc.gpsimd.memset(tri[:], 1.0))
        ch.join()
        nc.gpsimd.affine_select(out=tri[:], in_=tri[:], compare_op=ALU.is_gt, fill=0.0, base=0,
                                pattern=[[1, P]], channel_multiplier=-1).then_inc(sem("route_consts"), 1)

        pool.wait_ge(sem("tables_ready"), 1)
        pool.wait_ge(sem("h2_stored"), 1)
        total = pool.value_load(ends[0:1, E - 1:E], min_val=E, max_val=MAX_BLOCKS)

        def gather_block(g):
            nc.gpsimd.tensor_copy(gi[:], gather_idx[:, ds(g, 1)]).then_inc(sem("gi_ready"), 1)
            pool.wait_ge(sem("gi_ready"), g + 1)
            pool.sem_inc(sem("row_dmas"), 1)
            nc.gpsimd.indirect_dma_start(xg[:], None, h2_d, bass.IndirectOffsetOnAxis(ap=gi[:, 0:1], axis=0)).then_inc(sem("xg_in"), 16)

        def scatter_block(g):
            nc.gpsimd.tensor_copy(si[:], scatter_idx[:, ds(g, 1)]).then_inc(sem("si_ready"), 1)
            pool.wait_ge(sem("si_ready"), g + 1)
            pool.wait_ge(sem("y_ready"), g + 2)
            pool.sem_inc(sem("row_dmas"), 1)
            nc.gpsimd.indirect_dma_start(y_d, bass.IndirectOffsetOnAxis(ap=si[:, 0:1], axis=0), y_sb[:], None).then_inc(sem("y_out"), 16)

        pool.sem_inc(sem("y_free"), 1)
        gather_block(0)
        pool.wait_ge(sem("xgT_done"), 1)
        gather_block(1)
        with pool.Fori(1, total) as g:
            pool.wait_ge(sem("xgT_done"), g + 1)
            gather_block(g + 1)
            scatter_block(g - 1)
            pool.wait_ge(sem("y_out"), 16 * g)
            pool.sem_inc(sem("y_free"), 1)
        scatter_block(total - 1)
        pool.wait_ge(sem("y_out"), 16 * total)
        pool.sem_inc(sem("experts_done"), 1)

    @block.scalar
    def _(act):
        act.wait_ge(sem("c_in"), 16)
        nc.scalar.activation(c_sil[:], c_col[:], ACT.Silu).then_inc(sem("c_silu"), 1)
        act.sem_inc(sem("x_free0"), 1)
        act.sem_inc(sem("x_free1"), 1)
        with act.Fori(0, TT // 2) as i:
            for c in range(2):
                act.wait_ge(sem(f"x_in{c}"), 16 * (i + 1))
                nc.scalar.activation(sq[:], xt[c][:], ACT.Square, accum_out=stat1[:, 0:1]).then_inc(sem("sumsq"), 1)
                act.wait_ge(sem("meansq"), 2 * i + c + 1)
                nc.scalar.activation(stat1[:, 2:3], stat1[:, 1:2], ACT.Sqrt).then_inc(sem("rms"), 1)
                act.wait_ge(sem("rstd"), 2 * i + c + 1)
                act.wait_ge(sem("xn_used"), 2 * i + c + 1)
                nc.scalar.activation(xn[:], xt[c][:], ACT.Copy, scale=stat1[:, 3:4]).then_inc(sem("xn_ready"), 1)
                act.wait_ge(sem("xn_ready"), 2 * i + c + 1)
                act.sem_inc(sem(f"x_free{c}"), 1)
        act.wait_ge(sem("reduced"), 1)
        nc.scalar.activation(sin_t[:], ang[:], ACT.Sin)
        act.wait_ge(sem("reduced"), 2)
        nc.scalar.activation(cos_t[:], turn[:], ACT.Sin).then_inc(sem("angles_ready"), 1)

        def raise_tile(T, c, g):
            tok = first_token(g, tile_of(T))
            nc.scalar.activation(h_hi[c][:], hT[:, :, ds(tok, P, step=dilation(g))], ACT.Copy).then_inc(sem("h_hi_ready"), 1)

        def raise_piece(n, c):
            act.wait_ge(sem(f"w_in{c}"), 16 * (n // 2 + 1))
            k = weight_row(n)
            raw = w_raw[c][:].rearrange("p (a m) -> p a m", a=1)
            nc.scalar.activation(w_hi[:, ds(k, 1), c * PIECE:(c + 1) * PIECE], raw, ACT.Copy).then_inc(sem("w_hi_ready"), 1)

        act.wait_ge(sem("attn_consts"), 1)
        act.wait_ge(sem("angles_ready"), 1)
        for n in range(TT):
            raise_piece(n, n % 2)
        raise_tile(0, 0, 0)

        def step(T, c, gs, loads):
            g1 = gs[2]
            if g1 is not None:
                act.wait_ge(sem("proj_done"), T)
                wait(act, sem("rot_done"), T - 1)
                t = tile_of(T - 1)
                src = bank[1 - c]
                nq = 256 if g1 < 3 else 320
                nc.scalar.activation(qk_raw[:, 0:nq], src[:, 0:nq], ACT.Copy)
                if g1 < 3:
                    nc.scalar.activation(v_dil[HD:P, ds(t, 1), :], src[0:HD, 256:384].rearrange("p (a m) -> p a m", a=1), ACT.Copy)
                    last = nc.scalar.activation(v_dil[0:HD, ds(t + 1, 1), :], src[HD:P, 256:384].rearrange("p (a m) -> p a m", a=1), ACT.Copy)
                else:
                    last = nc.scalar.activation(v_swa[:, ds(t + 1, 1), :], src[:, 320:384].rearrange("p (a m) -> p a m", a=1), ACT.Copy)
                last.then_inc(sem("proj_evicted"), 1)
            if gs[0] is not None:
                raise_tile(T + 1, 1 - c, gs[0])
            if loads and not (isinstance(T, int) and T + TT >= PASSES * TT):
                raise_piece(T + TT, c)
            for u in (0, 1):
                g3, g2 = gs[4], gs[3]
                if g3 is not None and u in units(g3):
                    n = unit(g3, T - 3, u)
                    act.wait_ge(sem("eT_done"), n + 1)
                    w = 256 if g3 < 3 else 384
                    src = E_ps[:, 0, :] if g3 < 3 else E_ps[:, :, 0:384]
                    dst = eT[:, :, 0:w]
                    if g3 < 3:
                        src = src.rearrange("p (h w) -> p h w", h=2)
                    nc.scalar.activation(dst, src, ACT.Copy).then_inc(sem("eT_ready"), 1)
                if g2 is not None and u in units(g2):
                    n = unit(g2, T - 2, u)
                    act.wait_ge(sem("max_ready"), n + 1)
                    w = 256 if g2 < 3 else 384
                    row = o_row[c][u]
                    for h in range(2):
                        last = nc.scalar.activation(e_sb[u][:, h, 0:w], e_sb[u][:, h, 0:w], ACT.Exp, bias=row[:, h, HD:HD + 1],
                                                    scale=SCALE, accum_out=row[:, h, HD + 1:HD + 2])
                    if g2 == 3:
                        last = nc.scalar.activation(esk[c][u][:], snk[c][u][:], ACT.Exp)
                    last.then_inc(sem("exp_done"), 1)

        schedule(act, step)

        def raise_gate(n, c):
            act.wait_ge(sem("gates_done"), n + 1)
            for j in range(2):
                act.wait_ge(sem(f"g_in{j}"), 16 * (n + 1))
                cols = slice(j * (GATE_COLS // 2), (j + 1) * (GATE_COLS // 2))
                nc.scalar.activation(g_hi[c][:, cols], g_raw[j][:], ACT.Copy).then_inc(sem("g_hi_ready"), 1)

        def raise_chunk(q, k, cc):
            nc.scalar.activation(x_hi[cc][:, ds(k, 1), :], hT[:, ds(k, 1), ds(q * CHUNK, CHUNK)], ACT.Copy).then_inc(sem("x_hi_ready"), 1)

        act.wait_ge(sem("o_done"), SWA_T0 + 2 * TILES_PER_GROUP)
        raise_gate(0, 0)
        act.sem_inc(sem("oT_ready"), 1)
        with act.Fori(0, TT // 2) as i:
            for c in range(2):
                t = 2 * i + c
                act.wait_ge(sem("wg_in"), t + 1)
                nc.scalar.activation(wg[:], wg[:], ACT.Exp).then_inc(sem("wg_exp"), 1)
                if c == 0:
                    raise_chunk(0, i, 0)
                act.wait_ge(sem("oT_done"), t + 2)
                act.wait_ge(sem(f"oT_out{c}"), 16 * (i + 1))
                nc.scalar.activation(oT[c][:, 0:2, :], PS[0][:, 0:2 * P].rearrange("p (k s) -> p k s", k=2), ACT.Copy)
                nc.scalar.activation(oT[c][:, 2:OUT_K, :], PS[1][:, 0:4 * P].rearrange("p (k s) -> p k s", k=4), ACT.Copy).then_inc(sem("oT_ready"), 1)

        def gate_chunk(q, cc, more):
            act.wait_ge(sem("o_in"), 16 * (q + 1))
            nc.scalar.activation(o_hi[cc][:], o_lo[cc][:].bitcast(F32), ACT.Copy).then_inc(sem("o_hi_ready"), 1)
            with act.Fori(0, KD // 2) as i:
                for c in range(2):
                    n = KD * q + 2 * i + c
                    raise_gate(n + 1, 1 - c)
                    act.wait_ge(sem("gates_done"), n + 3)
                    for j in range(2):
                        last = nc.scalar.activation(sig[:, j, :], PS[4 * c + j][:], ACT.Sigmoid)
                    last.then_inc(sem("sig_ready"), 1)
                    if more:
                        raise_chunk(q + 1, 2 * i + c, 1 - cc)
                    act.wait_ge(sem("merged"), n + 1)
                    act.dma_start(mT_d[:, ds(2 * i + c, 1), ds(q * CHUNK, CHUNK)], mg[c][:].rearrange("p (a s) -> p a s", a=1)).then_inc(sem(f"mT_out{c}"), 16)

        for c in range(2):
            act.sem_inc(sem(f"mT_out{c}"), 16)
        chunk_loops(act, gate_chunk)

        def high_out(k):
            act.wait_ge(sem(f"slot_in{k % 4}"), 16 * (MOD_LOADS + k // 4 + 1))
            nc.scalar.activation(wo_hi[:, k, :], wo_raw[k % 4][:], ACT.Copy).then_inc(sem("wo_hi_ready"), 1)

        for k in range(4):
            high_out(k)

        def high_tile(t, c, i):
            act.wait_ge(sem(f"m_in{c}"), 16 * (i + 1))
            wait(act, sem("y_done"), t - 1)
            nc.scalar.activation(m_hi[c][:], m_in[c][:], ACT.Copy).then_inc(sem("m_hi_ready"), 1)

        def norm_tile(t, c):
            act.wait_ge(sem("x1_ready"), t + 1)
            nc.scalar.activation(sq2[:], x1[c][:], ACT.Square, accum_out=st2[:, 0:1]).then_inc(sem("sumsq"), 1)
            act.wait_ge(sem("meansq"), 1 * TT + t + 1)
            nc.scalar.activation(st2[:, 2:3], st2[:, 1:2], ACT.Sqrt).then_inc(sem("rms"), 1)

        def evict_tile(t):
            act.wait_ge(sem("h2T_done"), t + 1)
            for j in range(2):
                last = nc.scalar.activation(h2T[:, 4 * j:4 * j + 4, :], PS[4 + j][:].rearrange("p (k s) -> p k s", k=4), ACT.Copy)
            last.then_inc(sem("h2T_ready"), 1)

        high_tile(0, 0, 0)
        for k in range(4, KD):
            high_out(k)
        high_tile(1, 1, 0)
        norm_tile(0, 0)
        high_tile(2, 0, 1)
        evict_tile(0)
        norm_tile(1, 1)

        def out_pair(i, more):
            for c in range(2):
                t = 2 * i + c
                if c == 0 or more:
                    high_tile(t + 1, 1 - c, i + c)
                evict_tile(t - 1)
                norm_tile(t, c)

        with act.Fori(1, TT // 2 - 1) as i:
            out_pair(i, True)
        out_pair(TT // 2 - 1, False)
        evict_tile(TT - 1)

        for n, t in enumerate((gex, ratio)):
            act.wait_ge(sem("differences"), n + 1)
            nc.scalar.activation(t[:], t[:], ACT.Exp).then_inc(sem("exponentials"), 1)

        def gate_up_high(e, k, slot, count):
            act.wait_ge(sem(f"ring_in{slot}"), count)
            nc.scalar.activation(gu[:, ds(gu_row(e, 0, k), 1), :], w_in[slot][:].rearrange("p (a n) -> p a n", a=1), ACT.Copy).then_inc(sem("gu_hi_ready"), 1)

        def next_expert_high(g, e):
            wait(act, sem("gu_done"), g)
            for j in range(KD):
                gate_up_high(e + 1, j, j % RING, ring_count(e, j))

        def down_high(g, e, extra=0):
            wait(act, sem("down_done"), g)
            for k in range(KE):
                slot = (KD + k) % RING
                act.wait_ge(sem(f"ring_in{slot}"), ring_count(e, KD + k) - extra)
                nc.scalar.activation(dn_hi[:, k, :], w_in[slot][:], ACT.Copy).then_inc(sem("dn_hi_ready"), 1)

        def rows_T(g):
            act.wait_ge(sem("xgT_done"), g + 1)
            if not isinstance(g, int) or g > 0:
                act.wait_ge(sem("gu_done"), g)
            for j in range(2):
                last = nc.scalar.activation(x_hiT[:, 4 * j:4 * j + 4, :], PS[2 + j][:].rearrange("p (k s) -> p k s", k=4), ACT.Copy)
            last.then_inc(sem("xT_high"), 1)

        def rows_out(g):
            act.wait_ge(sem("down_done"), g + 1)
            act.wait_ge(sem("y_free"), g + 1)
            for j in range(2):
                last = nc.scalar.activation(y_sb[:, j * 512:(j + 1) * 512], PS[4 + j][:], ACT.Copy)
            last.then_inc(sem("y_ready"), 1)

        def block(g):
            act.wait_ge(sem("gu_done"), g + 1)
            wait(act, sem("hT_done"), g)
            nc.scalar.activation(hg[:], PS[0][:], ACT.Silu).then_inc(sem("silu_done"), 1)
            rows_T(g + 1)
            if not isinstance(g, int):
                rows_out(g - 1)
            act.wait_ge(sem("hT_done"), g + 1)
            nc.scalar.activation(h_hiT[:], PS[6][:].rearrange("p (k s) -> p k s", k=KE), ACT.Copy).then_inc(sem("hT_high"), 1)

        for k in range(KD):
            slot = (k + 2 * RING - KD) % RING
            gate_up_high(0, k, slot, 16 * (k // RING + 1))
        act.sem_inc(sem("y_ready"), 1)
        act.wait_ge(sem("tables_ready"), 1)
        total = act.value_load(ends[0:1, E - 1:E], min_val=E, max_val=MAX_BLOCKS)
        rows_T(0)
        next_expert_high(0, 0)
        block(0)
        down_high(0, 0)
        with act.Fori(1, total) as g:
            e = act.value_load(expert_of[0:1, ds(g, 1)], min_val=0, max_val=E - 1)
            e_was = act.value_load(expert_of[0:1, ds(g - 1, 1)], min_val=0, max_val=E - 1)
            with act.If(e_was < e):
                with act.If(e < E - 1):
                    next_expert_high(g, e)
            block(g)
            with act.If(e_was < e):
                with act.If(e < E - 1):
                    down_high(g, e)
                with act.Else():
                    down_high(g, e, 16)
        rows_out(total - 1)

        def weigh(q, r):
            t = ROUND * q + r
            act.wait_ge(sem(f"slot_in{r}"), 16 * (MOD_LOADS + OUT_LOADS) + 32 * (q + 1))
            wait(act, sem(f"out_stored{r}"), 16 * q)
            act.sem_inc(sem("last_waits"), 1)
            w0 = pair_w[:, ds(t, 1), 0:1].rearrange("p a b -> p (a b)")
            nc.scalar.activation(acc_row(t), yp[r][:, 0, :], ACT.Copy, scale=w0).then_inc(sem("first_weighed"), 1)

        def roots(q):
            act.wait_ge(sem("meansq"), 2 * TT + q + 1)
            nc.scalar.activation(rms3[:], ms3[:], ACT.Sqrt).then_inc(sem("rms"), 1)

        def last_round(q, more):
            for r in range(ROUND):
                if r < ROUND - 1:
                    weigh(q, r + 1)
                elif more:
                    weigh(q + 1, 0)
                if r == 0 and not (isinstance(q, int) and q == 0):
                    roots(q - 1)
                t = ROUND * q + r
                wait(act, sem("sumsq"), 2 * TT + t)
                act.wait_ge(sem("acc_ready"), t + 1)
                act.sem_inc(sem("last_waits"), 1)
                nc.scalar.activation(sq3[:], acc_row(t), ACT.Square, accum_out=ssq3[:, r:r + 1]).then_inc(sem("sumsq"), 1)

        weigh(0, 0)
        last_round(0, True)
        with act.Fori(1, TT // ROUND - 1) as q:
            last_round(q, True)
        last_round(TT // ROUND - 1, False)
        roots(TT // ROUND - 1)

    @block.vector
    def _(dve):
        ch = Chain(dve, sem("dve_chain"))
        dve.wait_ge(sem("ident_ready"), 1)
        dve.wait_ge(sem("c_silu"), 1)
        for k in range(KD):
            last = nc.vector.tensor_scalar(c_bc[:, k, :], ones[:], c_sil[:, k:k + 1], None, ALU.mult)
        last.then_inc(sem("c_bc_ready"), 1)
        dve.wait_ge(sem("g_in"), 64)
        for j in range(N_MOD * D // CHUNK):
            dve.wait_ge(sem("mod_mm"), j + 1)
            ch(nc.vector.tensor_tensor(mod[:, j * CHUNK:(j + 1) * CHUNK], bank[j % 2][:], b_bc[:, j * CHUNK:(j + 1) * CHUNK], ALU.add))
        ch.join()
        for n, g in ((1, 0), (4, 1)):
            ch(nc.vector.scalar_tensor_tensor(mod[:, n * D:(n + 1) * D], mod[:, n * D:(n + 1) * D], 1.0, g_bc[:, g, :], ALU.add, ALU.mult))
        ch.join()
        dve.sem_inc(sem("mod_rows_ready"), 1)
        dve.wait_ge(sem("cols_mm"), 1)
        nc.vector.tensor_copy(A1[:], bank[2][:, 0:KD])
        ch(nc.vector.tensor_copy(B1[:], bank[2][:, KD:2 * KD]))
        ch.join()
        dve.wait_ge(sem("rows_out"), 80)
        dve.sem_inc(sem("cols_ready"), 1)
        dve.sem_inc(sem("h_all"), 1)
        with dve.Fori(0, TT // 2) as i:
            for c in range(2):
                T = 2 * i + c
                dve.wait_ge(sem("sumsq"), T + 1)
                nc.vector.tensor_scalar(stat1[:, 1:2], stat1[:, 0:1], 1.0 / D, EPS, ALU.mult, ALU.add).then_inc(sem("meansq"), 1)
                dve.wait_ge(sem("rms"), T + 1)
                nc.vector.reciprocal(stat1[:, 3:4], stat1[:, 2:3]).then_inc(sem("rstd"), 1)
                dve.wait_ge(sem("xn_ready"), T + 1)
                dve.wait_ge(sem("xT_done"), T + 1)
                for k in range(KD):
                    src = bank[k // 4][:, (k % 4) * P:(k % 4 + 1) * P]
                    last = nc.vector.tensor_scalar(hT[:, k, ds(T * P, P)], src, A1[:, k:k + 1], B1[:, k:k + 1], ALU.mult, ALU.add)
                last.then_inc(sem("h_all"), 1)
        dve.wait_ge(sem("pos_in"), 112)
        dve.wait_ge(sem("invf_ready"), 1)
        link = lambda ins: (ch(ins), ch.join())
        link(nc.vector.tensor_copy(pos_f[:], pos_i[:]))
        pf = pos_f[:].rearrange("p (t a) -> p t a", a=1).broadcast_to([P, 3 * TT, HALF])
        fr = invf[:].rearrange("p (a f) -> p a f", a=1).broadcast_to([P, 3 * TT, HALF])
        link(nc.vector.tensor_tensor(ang[:], pf, fr, ALU.mult))
        link(nc.vector.tensor_scalar(turn[:], ang[:], float(1 / (2 * np.pi)), MAGIC, ALU.mult, ALU.add))
        link(nc.vector.tensor_scalar(turn[:], turn[:], -MAGIC, None, ALU.add))
        for part in PI2:
            link(nc.vector.scalar_tensor_tensor(ang[:], turn[:], -part, ang[:], ALU.mult, ALU.add))
        lim = 3.1415925
        nc.vector.tensor_scalar(ang[:], ang[:], lim, -lim, ALU.min, ALU.max).then_inc(sem("reduced"), 1)
        dve.wait_ge(sem("reduced"), 1)
        link(nc.vector.scalar_tensor_tensor(turn[:], ang[:], -1.0, ang[:], ALU.mult, ALU.max))
        nc.vector.tensor_scalar(turn[:], turn[:], -1.0, float(np.pi / 2), ALU.mult, ALU.add).then_inc(sem("reduced"), 1)
        dve.wait_ge(sem("attn_consts"), 1)
        link(nc.vector.tensor_scalar(nsink[:], sink_bc[:], -1.0, None, ALU.mult))
        dve.wait_ge(sem("angles_ready"), 1)

        def step(T, c, gs, loads):
            g1, g2, g3 = gs[2], gs[3], gs[4]
            if g1 is not None:
                S = T - 1
                row = tile_of(S) + (0 if g1 == 3 else TT * g1)
                nh = 4 if g1 < 3 else 5
                dve.wait_ge(sem("proj_evicted"), S + 1)
                wait(dve, sem("qkT_done"), S)
                cos_b = cos_t[:, ds(row, 1), :].broadcast_to([P, 2 * nh, HALF])
                sin_b = sin_t[:, ds(row, 1), :].broadcast_to([P, nh, HALF])
                raw = qk_raw[:, 0:nh * HD]
                r4 = raw.rearrange("p (h m) -> p h m", h=nh)
                tmp4 = qk_tmp[:, 0:nh * HD].rearrange("p (h m) -> p h m", h=nh)
                nc.vector.tensor_tensor(qk_rot[:, 0:nh * HD].rearrange("p (h m) -> p h m", m=HALF), raw.rearrange("p (h m) -> p h m", m=HALF), cos_b, ALU.mult)
                nc.vector.scalar_tensor_tensor(tmp4[:, :, 0:HALF], r4[:, :, HALF:HD], -1.0, sin_b, ALU.mult, ALU.mult)
                nc.vector.tensor_tensor(tmp4[:, :, HALF:HD], r4[:, :, 0:HALF], sin_b, ALU.mult).then_inc(sem("rot_parts"), 1)
                dve.wait_ge(sem("rot_parts"), S + 1)
                nc.vector.tensor_tensor(qk_rot[:, 0:nh * HD], qk_rot[:, 0:nh * HD], qk_tmp[:, 0:nh * HD], ALU.add).then_inc(sem("rot_done"), 1)
                dve.wait_ge(sem("qkT_done"), S + 1)
                t = tile_of(S)
                q = qst[1 - c]
                tb = bank[2]
                for pair in range(1 if g1 < 3 else 2):
                    nc.vector.tensor_copy(q[0:HD, 2 * pair, :], tb[0:HD, pair * P:(pair + 1) * P])
                    nc.vector.tensor_copy(q[HD:P, 2 * pair + 1, :], tb[HD:P, pair * P:(pair + 1) * P])
                if g1 < 3:
                    last = nc.vector.tensor_copy(kT_dil[:, ds(HD + t * P, P)], tb[:, P:2 * P])
                else:
                    nc.vector.tensor_copy(kT_swa[0:HD, ds(P + t * P, P)], tb[0:HD, 2 * P:3 * P])
                    last = nc.vector.tensor_copy(kT_swa[HD:P, ds(P + t * P, P)], tb[0:HD, 2 * P:3 * P])
                last.then_inc(sem("qk_ready"), 1)
            for u in (0, 1):
                if g2 is not None and u in units(g2):
                    S = T - 2
                    n = unit(g2, S, u)
                    dve.wait_ge(sem("s_done"), n + 1)
                    w = 256 if g2 < 3 else 384
                    e = e_sb[u][:, :, 0:w]
                    if g2 < 3:
                        src = S_ps[:, 0, :].rearrange("p (h w) -> p h w", h=2)
                        mk = mask_dil
                    else:
                        src, mk = S_ps[:, :, 0:384], mask_swa
                    m = mk[:, ds(mask_index(g2, tile_of(S)), 1), :].broadcast_to([P, 2, w])
                    nc.vector.tensor_tensor(e, src, m, ALU.add).then_inc(sem("masked"), 1)
                    dve.wait_ge(sem("masked"), n + 1)
                    wait(dve, sem("max_ready"), n)
                    nc.vector.tensor_reduce(mx[:], e, AX.X, ALU.max).then_inc(sem("maxed"), 1)
                    dve.wait_ge(sem("maxed"), n + 1)
                    wait(dve, sem(f"o_out{c}{u}"), 8 * (S - c) if u == 0 else 8 * (S - c) - 8 * SWA_T0)
                    negm = o_row[c][u][:, :, HD:HD + 1].rearrange("p h a -> p (h a)")
                    if g2 < 3:
                        nc.vector.tensor_scalar(negm, mx[:], -SCALE, None, ALU.mult).then_inc(sem("max_ready"), 1)
                    else:
                        head = ((S // TT) % 2) * 4 + 2 * u
                        nc.vector.tensor_scalar(nm[:], mx[:], -SCALE, None, ALU.mult).then_inc(sem("nm_step"), 1)
                        dve.wait_ge(sem("nm_step"), 2 * (n - SWA_T0) + 1)
                        nc.vector.tensor_tensor(negm, nm[:], nsink[:, ds(head, 2)], ALU.min).then_inc(sem("nm_step"), 1)
                        dve.wait_ge(sem("nm_step"), 2 * (n - SWA_T0) + 2)
                        nc.vector.tensor_tensor(snk[c][u][:], negm, sink_bc[:, ds(head, 2)], ALU.add).then_inc(sem("max_ready"), 1)
                if g3 is not None and u in units(g3):
                    S = T - 3
                    n = unit(g3, S, u)
                    row = o_row[1 - c][u]
                    dve.wait_ge(sem("pv_done"), n + 1)
                    src = O_ps[:, 0:P].rearrange("p (h m) -> p h m", h=2)
                    if g3 < 3:
                        nc.vector.tensor_copy(row[:, :, 0:HD], src).then_inc(sem("o_done"), 1)
                    else:
                        den = row[:, :, HD + 1:HD + 2].rearrange("p h a -> p (h a)")
                        nc.vector.tensor_tensor(rden[:], den, esk[1 - c][u][:], ALU.add).then_inc(sem("den_step"), 1)
                        dve.wait_ge(sem("den_step"), 2 * (n - SWA_T0) + 1)
                        nc.vector.reciprocal(rden[:], rden[:]).then_inc(sem("den_step"), 1)
                        dve.wait_ge(sem("den_step"), 2 * (n - SWA_T0) + 2)
                        rb = rden[:].rearrange("p (h a) -> p h a", a=1).broadcast_to([P, 2, HD])
                        nc.vector.tensor_tensor(row[:, :, 0:HD], src, rb, ALU.mult).then_inc(sem("o_done"), 1)

        schedule(dve, step)

        def lower_chunk(q, k, cc):
            dve.wait_ge(sem("x_hi_ready"), KD * q + k + 1)
            rows = hT[:, ds(k, 1), ds(q * CHUNK, CHUNK)]
            nc.vector.tensor_tensor(rows.bitcast(F32R), rows, x_hi[cc][:, ds(k, 1), :].bitcast(F32), ALU.subtract).then_inc(sem("x_lo_ready"), 1)

        with dve.Fori(0, TT // 2) as i:
            for c in range(2):
                t = 2 * i + c
                dve.wait_ge(sem(f"od_in{c}"), 32 * (i + 1))
                rows = od[c][:].rearrange("p g (h m) -> p g h m", m=STAT)
                negm = rows[:, :, :, HD:HD + 1].rearrange("p g h a -> p g (h a)")
                den = rows[:, :, :, HD + 1:HD + 2].rearrange("p g h a -> p g (h a)")
                flat = lambda t4: t4[:].rearrange("p g (h a) -> p (g h) a", a=1).broadcast_to([P, 3 * DIL_HEADS, HD])
                per_h = lambda t2: t2[:].rearrange("p (a h) -> p a h", a=1).broadcast_to([P, 3, DIL_HEADS])
                link_n = [0]

                def link5(ins, last=6):
                    link_n[0] += 1
                    ins.then_inc(sem("merge_step"), 1)
                    dve.wait_ge(sem("merge_step"), 8 * t + link_n[0])

                link5(nc.vector.tensor_tensor(nmin[:], negm[:, 0, :], negm[:, 1, :], ALU.min))
                link5(nc.vector.tensor_tensor(nmin[:], nmin[:], negm[:, 2, :], ALU.min))
                nc.vector.tensor_tensor(wg[:], per_h(nmin), negm, ALU.subtract).then_inc(sem("wg_in"), 1)
                if c == 0:
                    lower_chunk(0, i, 0)
                dve.wait_ge(sem("wg_exp"), t + 1)
                link5(nc.vector.tensor_tensor(wden[:], wg[:], den, ALU.mult))
                link5(nc.vector.tensor_reduce(dsum[:], wden[:].rearrange("p g h -> p h g"), AX.X, ALU.add))
                link5(nc.vector.reciprocal(dsum[:], dsum[:]))
                link5(nc.vector.tensor_tensor(wg[:], wg[:], per_h(dsum), ALU.mult))
                link5(nc.vector.tensor_tensor(wsum[:].rearrange("p g (h m) -> p (g h) m", m=HD), rows.rearrange("p g h m -> p (g h) m")[:, :, 0:HD], flat(wg), ALU.mult))
                link5(nc.vector.tensor_tensor(wsum[:, 0, :], wsum[:, 0, :], wsum[:, 1, :], ALU.add))
                dve.wait_ge(sem("oT_done"), t + 1)
                nc.vector.tensor_tensor(oa[:], wsum[:, 0, :], wsum[:, 2, :], ALU.add).then_inc(sem("oa_ready"), 1)

        dve.sem_inc(sem("gated"), 2)

        def gate_chunk(q, cc, more):
            dve.wait_ge(sem("o_hi_ready"), q + 1)
            nc.vector.tensor_tensor(o_lo[cc][:], o_lo[cc][:].bitcast(F32), o_hi[cc][:].bitcast(F32), ALU.subtract).then_inc(sem("o_lo_ready"), 1)
            with dve.Fori(0, KD // 2) as i:
                for c in range(2):
                    n = KD * q + 2 * i + c
                    dve.wait_ge(sem("sig_ready"), n + 1)
                    dve.wait_ge(sem(f"mT_out{c}"), 16 * ((KD // 2) * q + i + 1))
                    nc.vector.tensor_tensor(sig[:, 0, :], sig[:, 0, :], PS[4 * c + 2][:], ALU.mult)
                    nc.vector.tensor_tensor(sig[:, 1, :], sig[:, 1, :], PS[4 * c + 3][:], ALU.mult).then_inc(sem("gated"), 1)
                    dve.wait_ge(sem("gated"), n + 3)
                    nc.vector.tensor_tensor(mg[c][:], sig[:, 0, :], sig[:, 1, :], ALU.add).then_inc(sem("merged"), 1)
                    if more:
                        lower_chunk(q + 1, 2 * i + c, 1 - cc)

        chunk_loops(dve, gate_chunk)

        for k in range(KD):
            dve.wait_ge(sem("wo_hi_ready"), k + 1)
            nc.vector.tensor_tensor(wo_lo[:, k, :], wo_raw[k % 4][:], wo_hi[:, k, :].bitcast(F32), ALU.subtract).then_inc(sem("wo_lo_ready"), 1)
        dve.wait_ge(sem("rows_in"), 64)

        def residual(t, c, i):
            dve.wait_ge(sem("y_done"), t + 1)
            wait(dve, sem(f"x1_out{c}"), 32 * i)
            for j in range(2):
                last = nc.vector.tensor_tensor(x1[c][:, j * 512:(j + 1) * 512], PS[2 * c + j][:], gt1b[:, j * 512:(j + 1) * 512], ALU.mult)
            last.then_inc(sem("y_evicted"), 1)
            dve.wait_ge(sem("y_evicted"), t + 1)
            dve.wait_ge(sem(f"x_in{c}"), 16 * (TT // 2 + i + 1))
            nc.vector.tensor_tensor(x1[c][:], x1[c][:], x_in[c][:], ALU.add).then_inc(sem("x1_ready"), 1)
            dve.wait_ge(sem("sumsq"), 1 * TT + t + 1)
            nc.vector.tensor_scalar(st2[:, 1:2], st2[:, 0:1], 1.0 / D, EPS, ALU.mult, ALU.add).then_inc(sem("meansq"), 1)
            dve.wait_ge(sem("rms"), 1 * TT + t + 1)
            nc.vector.reciprocal(st2[:, 3:4], st2[:, 2:3]).then_inc(sem("rstd"), 1)
            dve.wait_ge(sem("rstd"), 1 * TT + t + 1)
            nc.vector.scalar_tensor_tensor(h2[c][:], x1[c][:], st2[:, 3:4], A2b[:], ALU.mult, ALU.mult).then_inc(sem("h2_scaled"), 1)
            dve.wait_ge(sem("h2_scaled"), t + 1)
            nc.vector.tensor_tensor(h2[c][:], h2[c][:], B2b[:], ALU.add).then_inc(sem("h2_ready"), 1)

        def take_logits(t):
            dve.wait_ge(sem("logits_done"), t + 1)
            nc.vector.tensor_copy(logits[:, ds(t, 1), :], PS[6][:, 0:GROUPS + E].rearrange("p (a n) -> p a n", a=1)).then_inc(sem("logits_ready"), 1)

        residual(0, 0, 0)
        residual(1, 1, 0)
        take_logits(0)
        with dve.Fori(1, TT // 2) as i:
            for c in range(2):
                residual(2 * i + c, c, i)
                take_logits(2 * i + c - 1)
        take_logits(TT - 1)

        dve.wait_ge(sem("rows_in"), 80)
        dve.wait_ge(sem("route_consts"), 1)
        dve.wait_ge(sem("dve_chain"), ch.n)
        rb = r_bias[:].rearrange("p (a n) -> p a n", a=1).broadcast_to([P, TT, GROUPS + E])
        link(nc.vector.tensor_tensor(logits[:], logits[:], rb, ALU.add))
        gl = logits[:, :, 0:GROUPS]

        def wide(ap, n):
            return ap[:].broadcast_to([P, TT, n])

        def first_best(vals, n, best, eq, idx, oh_out):
            link(nc.vector.tensor_reduce(best[:].rearrange("p t a -> p (t a)"), vals, AX.X, ALU.max))
            link(nc.vector.tensor_tensor(eq[:], vals, wide(best, n), ALU.is_equal))
            link(nc.vector.scalar_tensor_tensor(eq[:], eq[:], -float(n), iota_e[:, :, 0:n], ALU.mult, ALU.add))
            link(nc.vector.tensor_reduce(idx[:].rearrange("p t a -> p (t a)"), eq[:], AX.X, ALU.min))
            link(nc.vector.tensor_tensor(oh_out[:], eq[:], wide(idx, n), ALU.is_equal))

        first_best(gl, GROUPS, gmax, geq, gidx, gsel)
        nc.vector.tensor_tensor(gex[:], gl, wide(gmax, GROUPS), ALU.subtract).then_inc(sem("differences"), 1)
        link(nc.vector.tensor_scalar(gsel[:], gsel[:], -NEG, NEG, ALU.mult, ALU.add))
        pen = gsel[:].rearrange("p t (g a) -> p (t g) a", a=1).broadcast_to([P, TT * GROUPS, PER_GROUP])
        link(nc.vector.tensor_copy(el[:], logits[:, :, GROUPS:]))
        el3 = el[:].rearrange("p t (g a) -> p (t g) a", a=PER_GROUP)
        link(nc.vector.tensor_tensor(el3, el3, pen, ALU.add))
        first_best(el[:], E, top[0], eeq, eidx, oh[0])
        link(nc.vector.scalar_tensor_tensor(el[:], oh[0][:], 2 * NEG, el[:], ALU.mult, ALU.add))
        first_best(el[:], E, top[1], eeq, eidx, oh[1])
        nc.vector.tensor_tensor(ratio[:], top[1][:], top[0][:], ALU.subtract).then_inc(sem("differences"), 1)
        nc.vector.tensor_tensor(both[:], oh[0][:], oh[1][:], ALU.add).then_inc(sem("both_ready"), 1)
        dve.wait_ge(sem("exponentials"), 1)
        link(nc.vector.tensor_reduce(gsum[:].rearrange("p t a -> p (t a)"), gex[:], AX.X, ALU.add))
        dve.wait_ge(sem("exponentials"), 2)
        link(nc.vector.tensor_scalar(rinv[:], ratio[:], 1.0, None, ALU.add))
        link(nc.vector.tensor_tensor(rinv[:], rinv[:], gsum[:], ALU.mult))
        link(nc.vector.reciprocal(pair_w[:, :, 0:1], rinv[:]))
        link(nc.vector.tensor_tensor(pair_w[:, :, 1:2], pair_w[:, :, 0:1], ratio[:], ALU.mult))
        dve.wait_ge(sem("ranks_done"), 1)
        link(nc.vector.tensor_scalar(cnt_i[:], PS[1][:, 0:E], float(BLK - 1), None, ALU.add))
        link(nc.vector.tensor_scalar(cnt_i[:], cnt_i[:], 7, None, ALU.logical_shift_right))
        link(nc.vector.tensor_copy(nblk[:], cnt_i[:]))
        link(nc.vector.tensor_scalar(nblk[:], nblk[:], 1.0, None, ALU.max))
        link(nc.vector.memset(cnt[:], 1.0))
        link(nc.vector.tensor_tensor_scan(pend[:], cnt[:], nblk[:], 0.0, ALU.mult, ALU.add))
        link(nc.vector.tensor_copy(ends[:], pend[0:1, :]))
        link(nc.vector.tensor_tensor(pbase[:], pend[:], nblk[:], ALU.subtract))
        link(nc.vector.tensor_scalar(pbase[:], pbase[:], float(BLK), None, ALU.mult))
        pe_b = pend[:].rearrange("p (a e) -> p a e", a=1).broadcast_to([P, MAX_BLOCKS, E])
        ib_b = iota_b[:].rearrange("p (b a) -> p b a", a=1).broadcast_to([P, MAX_BLOCKS, E])
        link(nc.vector.tensor_tensor(cmp_e[:], pe_b, ib_b, ALU.is_le))
        link(nc.vector.tensor_reduce(e_f[:], cmp_e[:], AX.X, ALU.add))
        link(nc.vector.tensor_scalar(e_f[:], e_f[:], float(E - 1), None, ALU.min))
        link(nc.vector.tensor_copy(expert_of[0:1, 0:MAX_BLOCKS], e_f[0:1, :]))
        rk = PS[0][:, 0:TT * E].rearrange("p (t e) -> p t e", e=E)
        pb = pbase[:].rearrange("p (a e) -> p a e", a=1).broadcast_to([P, TT, E])
        link(nc.vector.tensor_tensor(posn[:], rk, pb, ALU.add))
        for k in range(2):
            link(nc.vector.tensor_tensor(prod[:], posn[:], oh[k][:], ALU.mult))
            link(nc.vector.tensor_reduce(slot_f[:, :, k:k + 1].rearrange("p t a -> p (t a)"), prod[:], AX.X, ALU.add))
        link(nc.vector.tensor_copy(slot_i[:], slot_f[:]))
        link(nc.vector.tensor_scalar(lane_i[:], slot_i[:], BLK - 1, None, ALU.bitwise_and))
        link(nc.vector.tensor_scalar(blk_i[:], slot_i[:], 7, None, ALU.logical_shift_right))
        link(nc.vector.tensor_copy(lane_f[:], lane_i[:]))
        link(nc.vector.tensor_copy(blk_f[:], blk_i[:]))
        with dve.Fori(0, TT) as t:
            for k in range(2):
                dve.wait_ge(sem("oh_free"), 2 * t + k + 1)
                lane = lane_f[:, ds(t, 1), k:k + 1].rearrange("p a b -> p (a b)")
                blk = blk_f[:, ds(t, 1), k:k + 1].rearrange("p a b -> p (a b)")
                ident_k = flat_id[:, ds(t, 1), k:k + 1].rearrange("p a b -> p (a b)")
                nc.vector.tensor_scalar(lane_oh[k][:], iota_r[:], lane, None, ALU.is_equal)
                nc.vector.tensor_scalar(blk_oh[k][:, 0, :], iota_b[:], blk, ident_k, ALU.is_equal, ALU.mult)
                nc.vector.tensor_scalar(blk_oh[k][:, 1, :], iota_b[:], blk, None, ALU.is_equal).then_inc(sem("oh_ready"), 1)
        dve.wait_ge(sem("oh_free"), 2 * TT + 2)
        link(nc.vector.tensor_copy(tab[:], PS[2][:, 0:2 * MAX_BLOCKS].rearrange("p (a b) -> p a b", a=2)))
        link(nc.vector.scalar_tensor_tensor(idx_f[:], tab[:, 1, :], pad_id[:, 1:2], tab[:, 0, :], ALU.mult, ALU.add))
        link(nc.vector.tensor_scalar(idx_f[:], idx_f[:], pad_id[:, 0:1], None, ALU.add))
        link(nc.vector.tensor_copy(scatter_idx[:, 0:MAX_BLOCKS], idx_f[:]))
        link(nc.vector.tensor_copy(scatter_idx[:, MAX_BLOCKS:], pad_id[:, 0:1]))
        link(nc.vector.tensor_scalar(gather_idx[:], scatter_idx[:], 1, None, ALU.logical_shift_right))
        dve.sem_inc(sem("tables_ready"), 1)

        def gate_up_low(e, k, slot, count):
            dve.wait_ge(sem("gu_hi_ready"), count)
            raw = w_in[slot][:].rearrange("p (a n) -> p a n", a=1)
            nc.vector.tensor_tensor(gu[:, ds(gu_row(e, 1, k), 1), :], raw, gu[:, ds(gu_row(e, 0, k), 1), :].bitcast(F32), ALU.subtract).then_inc(sem("gu_lo_ready"), 1)

        def next_expert_low(e):
            for j in range(KD):
                gate_up_low(e + 1, j, j % RING, KD * (e + 1) + j + 1)

        def down_low(e):
            for k in range(KE):
                dve.wait_ge(sem("dn_hi_ready"), KE * e + k + 1)
                nc.vector.tensor_tensor(dn_lo[:, k, :], w_in[(KD + k) % RING][:], dn_hi[:, k, :].bitcast(F32), ALU.subtract).then_inc(sem("dn_lo_ready"), 1)

        def rows_low(g):
            dve.wait_ge(sem("xT_high"), g + 1)
            for j in range(2):
                last = nc.vector.tensor_tensor(x_loT[:, 4 * j:4 * j + 4, :], PS[2 + j][:].rearrange("p (k s) -> p k s", k=4), x_hiT[:, 4 * j:4 * j + 4, :].bitcast(F32), ALU.subtract)
            last.then_inc(sem("xT_ready"), 1)

        def block(g):
            dve.wait_ge(sem("silu_done"), g + 1)
            nc.vector.tensor_tensor(hg[:], hg[:], PS[1][:], ALU.mult).then_inc(sem("h_ready"), 1)
            rows_low(g + 1)
            dve.wait_ge(sem("hT_high"), g + 1)
            nc.vector.tensor_tensor(h_loT[:], PS[6][:].rearrange("p (k s) -> p k s", k=KE), h_hiT[:].bitcast(F32), ALU.subtract).then_inc(sem("hT_ready"), 1)

        for k in range(KD):
            gate_up_low(0, k, (k + 2 * RING - KD) % RING, k + 1)
        dve.wait_ge(sem("tables_ready"), 1)
        total = dve.value_load(ends[0:1, E - 1:E], min_val=E, max_val=MAX_BLOCKS)
        rows_low(0)
        next_expert_low(0)
        block(0)
        down_low(0)
        with dve.Fori(1, total) as g:
            e = dve.value_load(expert_of[0:1, ds(g, 1)], min_val=0, max_val=E - 1)
            e_was = dve.value_load(expert_of[0:1, ds(g - 1, 1)], min_val=0, max_val=E - 1)
            with dve.If(e_was < e):
                with dve.If(e < E - 1):
                    next_expert_low(e)
            block(g)
            with dve.If(e_was < e):
                down_low(e)

        dve.wait_ge(sem("rows_in"), 112)

        def total_row(q, r):
            t = ROUND * q + r
            steps_done = [0]

            def link3(ins):
                steps_done[0] += 1
                ins.then_inc(sem("last_step"), 1)
                dve.wait_ge(sem("last_step"), 2 * t + steps_done[0])

            w1 = pair_w[:, ds(t, 1), 1:2].rearrange("p a b -> p (a b)")
            row = acc_row(t)
            dve.wait_ge(sem("first_weighed"), t + 1)
            link3(nc.vector.scalar_tensor_tensor(row, yp[r][:, 1, :], w1, row, ALU.mult, ALU.add))
            link3(nc.vector.tensor_tensor(row, row, gt2b[:], ALU.mult))
            nc.vector.tensor_tensor(row, row, xl[r][:], ALU.add).then_inc(sem("acc_ready"), 1)

        def means(q):
            dve.wait_ge(sem("sumsq"), 2 * TT + ROUND * (q + 1))
            nc.vector.tensor_scalar(ms3[:], ssq3[:], 1.0 / D, EPS, ALU.mult, ALU.add).then_inc(sem("meansq"), 1)

        def inverse_roots(q):
            dve.wait_ge(sem("rms"), 2 * TT + q + 1)
            nc.vector.reciprocal(rstd3[:], rms3[:]).then_inc(sem("rstd"), 1)
            dve.wait_ge(sem("rstd"), 2 * TT + q + 1)

        def finish(t, r):
            nc.vector.scalar_tensor_tensor(acc_row(t), acc_row(t), rstd3[:, r:r + 1], gfb[:], ALU.mult, ALU.mult).then_inc(sem("out_ready"), 1)

        def last_round(q):
            for r in range(ROUND):
                t = ROUND * q + r
                total_row(q, r)
                if not isinstance(q, int) or t >= ROUND:
                    if r == 0:
                        if not isinstance(q, int) or q > 1:
                            finish(t - LAG, ROUND - 1)
                        means(q - 1)
                    else:
                        if r == 1:
                            inverse_roots(q - 1)
                        finish(t - LAG, r - 1)

        last_round(0)
        last_round(1)
        with dve.Fori(2, TT // ROUND) as q:
            last_round(q)
        finish(TT - LAG, ROUND - 1)
        means(TT // ROUND - 1)
        inverse_roots(TT // ROUND - 1)
        for r in range(ROUND):
            finish(TT - ROUND + r, r)

    @block.tensor
    def _(pe):
        pe.wait_ge(sem("ident_ready"), 1)
        pe.wait_ge(sem("c_bc_ready"), 1)
        for j in range(N_MOD * D // CHUNK):
            pe.wait_ge(sem(f"slot_in{j % 4}"), 16 * (j // 4 + 1))
            wait(pe, sem("dve_chain"), j - 1)
            for k in range(KD):
                last = nc.tensor.matmul(bank[j % 2][:], c_bc[:, k, :], wada[j % 4][:, k, :], start=(k == 0), stop=(k == KD - 1))
            last.then_inc(sem("mod_mm"), 1)
        pe.wait_ge(sem("mod_rows_ready"), 1)
        for col in range(2 * KD):
            k = col % KD
            src = mod[0:1, D + k * P:D + (k + 1) * P] if col < KD else mod[0:1, k * P:(k + 1) * P]
            last = nc.tensor.matmul(bank[2][:, col:col + 1], src, ones_row[0:1, 0:1], start=True, stop=True)
        last.then_inc(sem("cols_mm"), 1)
        pe.sem_inc(sem("xn_used"), 1)
        with pe.Fori(0, TT // 2) as i:
            for c in range(2):
                T = 2 * i + c
                pe.wait_ge(sem("xn_ready"), T + 1)
                pe.wait_ge(sem("h_all"), T + 1)
                for k in range(KD):
                    last = nc.tensor.transpose(bank[k // 4][:, (k % 4) * P:(k % 4 + 1) * P], xn[:, k * P:(k + 1) * P], ident[:])
                last.then_inc(sem("xT_done"), 1)
                pe.wait_ge(sem("xT_done"), T + 1)
                pe.sem_inc(sem("xn_used"), 1)

        def project(T, c, g, ks):
            row = ((T // TT) % 2) * KD
            for k in ks:
                for a, (x, w) in enumerate(((h_hi, w_hi), (h_hi, w_lo), (h_lo, w_hi))):
                    last = nc.tensor.matmul(bank[c][:, 0:PASS_COLS].rearrange("p (a m) -> p a m", a=1), x[c][:, k, :], w[:, ds(row + k, 1), :], start=(k == 0 and a == 0), stop=(k == KD - 1 and a == 2))
            if ks[-1] == KD - 1:
                last.then_inc(sem("proj_done"), 1)

        def step(T, c, gs, loads):
            g, g1, g2, g3 = gs[1], gs[2], gs[3], gs[4]
            if g is not None:
                pe.wait_ge(sem("h_lo_ready"), T + 1)
                pe.wait_ge(sem("w_lo_ready"), TT * (T // TT) + TT)
                wait(pe, sem("proj_evicted"), T - 1)
                project(T, c, g, (0, 1, 2, 3))
            if g1 is not None:
                pe.wait_ge(sem("rot_done"), T)
                tb = bank[2]
                if g1 < 3:
                    nc.tensor.transpose(tb[:, 0:P], qk_rot[:, 0:P], ident[:])
                    last = nc.tensor.transpose(tb[:, P:2 * P], qk_rot[:, P:2 * P], ident[:])
                else:
                    nc.tensor.transpose(tb[:, 0:P], qk_rot[:, 0:P], ident[:])
                    nc.tensor.transpose(tb[:, P:2 * P], qk_rot[:, P:2 * P], ident[:])
                    last = nc.tensor.transpose(tb[0:HD, 2 * P:3 * P], qk_rot[:, 2 * P:2 * P + HD], ident[:])
                last.then_inc(sem("qkT_done"), 1)
            if g is not None:
                project(T, c, g, (4, 5))
            two = (g2 == 3 or g3 == 3)
            for u in (0, 1):
                if g3 is not None and u in units(g3):
                    n = unit(g3, T - 3, u)
                    pe.wait_ge(sem("exp_done"), n + 1)
                    for h in range(2):
                        for j in range(2 if g3 < 3 else 3):
                            dst = E_ps[:, 0, (2 * h + j) * P:(2 * h + j + 1) * P] if g3 < 3 else E_ps[:, h, j * P:(j + 1) * P]
                            last = nc.tensor.transpose(dst, e_sb[u][:, h, j * P:(j + 1) * P], ident[:])
                    last.then_inc(sem("eT_done"), 1)
                if g2 is not None and u in units(g2):
                    S = T - 2
                    n = unit(g2, S, u)
                    if isinstance(T, int) and T - 1 >= STEPS:
                        pe.wait_ge(sem("qk_ready"), STEPS)
                    else:
                        pe.wait_ge(sem("qk_ready"), T)
                    wait(pe, sem("masked"), n)
                    t = tile_of(S)
                    for h in range(2):
                        if g2 < 3:
                            last = nc.tensor.matmul(S_ps[:, 0, h * 256:(h + 1) * 256], qst[c][:, h, :], kT_dil[:, ds(t * P, 256)], start=True, stop=True)
                        else:
                            last = nc.tensor.matmul(S_ps[:, h, 0:384], qst[c][:, 2 * u + h, :], kT_swa[:, ds(t * P, 384)], start=True, stop=True)
                    last.then_inc(sem("s_done"), 1)
                if g is not None:
                    if u == 0:
                        project(T, c, g, (6,) if two else (6, 7))
                    elif two:
                        project(T, c, g, (7,))
                if g3 is not None and u in units(g3):
                    S = T - 3
                    n = unit(g3, S, u)
                    pe.wait_ge(sem("eT_ready"), n + 1)
                    wait(pe, sem("o_done"), n)
                    t = tile_of(S)
                    nj = 2 if g3 < 3 else 3
                    for h in range(2):
                        for j in range(nj):
                            v = v_dil[:, ds(t + j, 1), h * HD:(h + 1) * HD] if g3 < 3 else v_swa[:, ds(t + j, 1), :]
                            last = nc.tensor.matmul(O_ps[:, h * HD:(h + 1) * HD].rearrange("p (a m) -> p a m", a=1), eT[:, h, j * P:(j + 1) * P], v,
                                                    start=(j == 0), stop=(j == nj - 1))
                    last.then_inc(sem("pv_done"), 1)

        schedule(pe, step)

        pe.sem_inc(sem("oT_done"), 1)
        pe.sem_inc(sem("gates_done"), 2)
        with pe.Fori(0, TT // 2) as i:
            for c in range(2):
                t = 2 * i + c
                pe.wait_ge(sem("oa_ready"), t + 1)
                pe.wait_ge(sem("oT_ready"), t + 1)
                for k in range(2):
                    nc.tensor.transpose(PS[0][:, k * P:(k + 1) * P], oa[:, k * P:(k + 1) * P], ident[:])
                for k in range(4):
                    last = nc.tensor.transpose(PS[1][:, k * P:(k + 1) * P], ob[c][:, k * P:(k + 1) * P], ident[:])
                last.then_inc(sem("oT_done"), 1)

        parts = lambda w, x: ((w[0], x[0]), (w[0], x[1]), (w[1], x[0]))

        pe.wait_ge(sem("oT_ready"), TT + 1)
        def gate_chunk(q, cc, more):
            with pe.Fori(0, KD // 2) as i:
                for c in range(2):
                    n = KD * q + 2 * i + c
                    pe.wait_ge(sem("x_lo_ready"), KD * (q + 1))
                    pe.wait_ge(sem("g_lo_ready"), 2 * n + 2)
                    pe.wait_ge(sem("gated"), n + 1)
                    gw = (g_hi[c], g_lo[c])
                    off = KD * 2 * P
                    x_k = lambda k: (x_hi[cc][:, k:k + 1, :], hT[:, k:k + 1, ds(q * CHUNK, CHUNK)].bitcast(F32R))
                    o_k = lambda k: (o_hi[cc][:, k:k + 1, :], o_lo[cc][:, k:k + 1, :])
                    jobs = [(0, k, k * 2 * P, k == 0, k == KD - 1, x_k) for k in range(KD)]
                    jobs += [(1, k, k * 2 * P + P, k == 0, k == KD - 1, x_k) for k in range(KD)]
                    jobs += [(2, k, off + k * P, k == 0, k == 1, o_k) for k in range(2)]
                    jobs += [(3, k, off + k * P, k == 2, k == OUT_K - 1, o_k) for k in range(2, OUT_K)]
                    for dst, k, col, first, last_k, xs in jobs:
                        if dst == 2 and k == 0:
                            pe.wait_ge(sem("o_lo_ready"), q + 1)
                        for a, (w, x) in enumerate(parts(gw, xs(k))):
                            last = nc.tensor.matmul(PS[4 * c + dst][:].rearrange("p (a n) -> p a n", a=1), w[:, col:col + P], x,
                                                    start=first and a == 0, stop=last_k and a == 2)
                    last.then_inc(sem("gates_done"), 1)

        chunk_loops(pe, gate_chunk)

        def out_tile(t, c, halves):
            for j in halves:
                for k in range(KD):
                    if isinstance(t, int) and t == 0 and j == 0:
                        pe.wait_ge(sem("wo_lo_ready"), k + 1)
                    for a, (x, w) in enumerate(((m_hi, wo_hi), (m_hi, wo_lo), (m_lo, wo_hi))):
                        last = nc.tensor.matmul(PS[2 * c + j][:], x[c][:, k, :], w[:, k, j * 512:(j + 1) * 512],
                                                start=(k == 0 and a == 0), stop=(k == KD - 1 and a == 2))
            if halves[-1] == 1:
                last.then_inc(sem("y_done"), 1)

        def turn_tile(t, c):
            pe.wait_ge(sem("h2_ready"), t + 1)
            wait(pe, sem("h2T_ready"), t)
            for k in range(KD):
                last = nc.tensor.transpose(PS[4 + k // 4][:, (k % 4) * P:(k % 4 + 1) * P], h2[c][:, k * P:(k + 1) * P], ident[:])
            last.then_inc(sem("h2T_done"), 1)

        def route_tile(t):
            pe.wait_ge(sem("h2T_ready"), t + 1)
            wait(pe, sem("logits_ready"), t)
            for k in range(KD):
                last = nc.tensor.matmul(PS[6][:, 0:GROUPS + E], h2T[:, k, :], w_rt[:, k, :], start=(k == 0), stop=(k == KD - 1))
            last.then_inc(sem("logits_done"), 1)

        pe.wait_ge(sem("rows_in"), 64)
        pe.wait_ge(sem("m_lo_ready"), 1)
        out_tile(0, 0, (0, 1))
        pe.wait_ge(sem("m_lo_ready"), 2)
        out_tile(1, 1, (0,))
        turn_tile(0, 0)
        out_tile(1, 1, (1,))
        route_tile(0)
        with pe.Fori(1, TT // 2) as i:
            for c in range(2):
                t = 2 * i + c
                pe.wait_ge(sem("m_lo_ready"), t + 1)
                pe.wait_ge(sem("y_evicted"), t - 1)
                out_tile(t, c, (0,))
                turn_tile(t - 1, 1 - c)
                out_tile(t, c, (1,))
                route_tile(t - 1)
        turn_tile(TT - 1, 1)
        route_tile(TT - 1)

        pe.wait_ge(sem("both_ready"), 1)
        M = both[:].rearrange("p t e -> p (t e)")
        nc.tensor.matmul(PS[0][:, 0:TT * E], tri[:], M, start=True, stop=False)
        for back in range(1, TT):
            nc.tensor.matmul(PS[0][:, back * E:TT * E], all_ones[:], M[:, 0:(TT - back) * E], start=False, stop=(back == TT - 1))
        for t in range(TT):
            last = nc.tensor.matmul(PS[1][:, 0:E], all_ones[:], M[:, t * E:(t + 1) * E], start=(t == 0), stop=(t == TT - 1))
        last.then_inc(sem("ranks_done"), 1)
        pe.sem_inc(sem("oh_free"), 2)

        def place(t):
            for k in range(2):
                pe.wait_ge(sem("oh_ready"), 2 * t + k + 1)
                edge = isinstance(t, int)
                nc.tensor.matmul(PS[2][:, 0:2 * MAX_BLOCKS], lane_oh[k][:], blk_oh[k][:].rearrange("p a b -> p (a b)"),
                                 start=(edge and t == 0 and k == 0), stop=(edge and t == TT - 1 and k == 1)).then_inc(sem("oh_free"), 1)

        place(0)
        with pe.Fori(1, TT - 1) as t:
            place(t)
        place(TT - 1)

        pe.wait_ge(sem("tables_ready"), 1)
        total = pe.value_load(ends[0:1, E - 1:E], min_val=E, max_val=MAX_BLOCKS)

        def turn_rows(g):
            pe.wait_ge(sem("xg_in"), 16 * (g + 1))
            wait(pe, sem("xT_ready"), g)
            for k in range(KD):
                last = nc.tensor.transpose(PS[2 + k // 4][:, (k % 4) * P:(k % 4 + 1) * P], xg[:, k * P:(k + 1) * P], ident[:])
            last.then_inc(sem("xgT_done"), 1)

        def gate_up(g, e):
            pe.wait_ge(sem("xT_ready"), g + 1)
            pe.wait_ge(sem("gu_lo_ready"), KD * (e + 1))
            wait(pe, sem("h_ready"), g)
            for k in range(KD):
                for j in range(2):
                    for a, (x, part) in enumerate(((x_hiT, 0), (x_hiT, 1), (x_loT, 0))):
                        last = nc.tensor.matmul(PS[j][:].rearrange("p (a n) -> p a n", a=1), x[:, k, :], gu[:, ds(gu_row(e, part, k), 1), j * DE:(j + 1) * DE],
                                                start=(k == 0 and a == 0), stop=(k == KD - 1 and a == 2))
            last.then_inc(sem("gu_done"), 1)

        def down(g, e):
            pe.wait_ge(sem("hT_ready"), g + 1)
            pe.wait_ge(sem("dn_lo_ready"), KE * (e + 1))
            pe.wait_ge(sem("y_ready"), g + 1)
            for k in range(KE):
                for j in range(2):
                    for a, (x, w) in enumerate(((h_hiT, dn_hi), (h_hiT, dn_lo), (h_loT, dn_hi))):
                        last = nc.tensor.matmul(PS[4 + j][:], x[:, k, :], w[:, k, j * 512:(j + 1) * 512],
                                                start=(k == 0 and a == 0), stop=(k == KE - 1 and a == 2))
            last.then_inc(sem("down_done"), 1)

        def turn_hidden(g):
            pe.wait_ge(sem("h_ready"), g + 1)
            for k in range(KE):
                last = nc.tensor.transpose(PS[6][:, k * P:(k + 1) * P], hg[:, k * P:(k + 1) * P], ident[:])
            last.then_inc(sem("hT_done"), 1)

        turn_rows(0)
        gate_up(0, 0)
        turn_rows(1)
        turn_hidden(0)
        with pe.Fori(1, total) as g:
            e = pe.value_load(expert_of[0:1, ds(g, 1)], min_val=0, max_val=E - 1)
            e_was = pe.value_load(expert_of[0:1, ds(g - 1, 1)], min_val=0, max_val=E - 1)
            gate_up(g, e)
            turn_rows(g + 1)
            down(g - 1, e_was)
            turn_hidden(g)
        down(total - 1, E - 1)


def kernel(**inputs):
    import numpy as _np
    import concourse.bacc as _bacc
    from concourse import mybir as _mybir
    from concourse.bass_utils import run_bass_kernel_spmd as _run

    a = {n: _np.asarray(v) for n, v in inputs.items()}
    w = a["w_in"][0]
    dil, qw, kvw = DIL_HEADS * HD, SWA_HEADS * HD, 2 * HD
    q0, k0, v0 = 0, 3 * dil, 6 * dil
    qb, kb, vb, gates = 9 * dil, 9 * dil + qw, 9 * dil + qw + kvw, 9 * dil + qw + 2 * kvw

    def columns(*runs):
        return _np.concatenate([w[:, at:at + n] for at, n in runs], axis=1)

    passes = [columns((q0 + p * P, P), (k0 + p * P, P), (v0 + p * P, P)) for p in range(6)]
    passes += [columns((qb + p * 4 * HD, 4 * HD), (kb + p * HD, HD), (vb + p * HD, HD)) for p in range(2)]
    gate = w[:, gates:].reshape(KD, P, 2, KD, P).transpose(3, 1, 0, 2, 4).reshape(KD, P, KD * 2 * P)
    branch = _np.concatenate([a["w_branch_a"][0], a["w_branch_b"][0]], axis=0)
    branch = branch.reshape(OUT_K, P, KD, P).transpose(2, 1, 0, 3).reshape(KD, P, OUT_K * P)
    laid = {n: a[n] for n in ("x", "c", "positions", "w_ada", "b_ada", "g_mix", "g_ffn", "g_final", "sink_logits", "w_out",
                              "w_expert_down")}
    laid["w_gate_up"] = _np.concatenate([a["w_expert_gate"][0], a["w_expert_up"][0]], axis=2)
    laid["w_qkv"] = _np.stack(passes)
    laid["w_gb"] = _np.concatenate([gate, branch], axis=2)
    laid["w_rt"] = _np.concatenate([a["w_group"][0], a["w_route"][0]], axis=1)
    laid["b_rt"] = _np.concatenate([a["b_group"], a["b_route"]], axis=1)

    nc = _bacc.Bacc("TRN2", target_bir_lowering=False, num_devices=1)
    arrays, A = {}, {}
    for n, v in laid.items():
        arrays[f"in_{n}"] = v = _np.ascontiguousarray(v)
        A[n] = nc.dram_tensor(f"in_{n}", v.shape, _mybir.dt.from_np(v.dtype), kind="ExternalInput").ap()
    out = nc.dram_tensor("out_0", (1, SEQ, D), _mybir.dt.float32, kind="ExternalOutput").ap()
    build(nc, A, out)
    r = _run(nc, [arrays], core_ids=[0])
    return r.results[0]["out_0"]
```

```python
import numpy as np
import concourse.bass as bass
from concourse import mybir
from contextlib import ExitStack

F32 = mybir.dt.float32
F32R = mybir.dt.float32r
BF16 = mybir.dt.bfloat16
F16 = mybir.dt.float16
I32 = mybir.dt.int32
ALU = mybir.AluOpType
ACT = mybir.ActivationFunctionType
AX = mybir.AxisListType
ds = bass.ds

P = 128
SEQ = 2048
D = 1024
KD = D // P
TT = SEQ // P
HD = 64
HALF = HD // 2
DILATIONS = (1, 4, 16)
DIL_HEADS = 4
SWA_HEADS = 8
SCALE = HD ** -0.5
EPS = 1e-6
NEG = -1e30
THETA = 10000.0
N_MOD = 6
E = 32
GROUPS = 4
PER_GROUP = E // GROUPS
DE = 512
KE = DE // P
BLK = 128
MAX_BLOCKS = SEQ * 2 // BLK + E
CHUNK = 512
PAD_ROWS = P
ROUND = 4
ROUNDS = SEQ // P // ROUND
NORM_FROM = 4
assert 2 * (N_MOD * D // CHUNK - NORM_FROM) == TT
LAG = ROUND + 1
RING = 6
PIECES = KD + KE
assert PIECES == 2 * RING

MOD_CHUNKS = N_MOD * D // CHUNK
MOD_HALVES = 2 * MOD_CHUNKS
MOD_LOADS = MOD_HALVES // 4
OUT_LOADS = KD // 4

PASSES = 8
PASS_COLS = 384
TILES_PER_GROUP = 2 * TT
PIECE = PASS_COLS // 2
SWA_T0 = 3 * TILES_PER_GROUP
STEPS = 4 * TILES_PER_GROUP
STAT = HD + 2

OUT_K = 6
GATE_COLS = KD * 2 * P + OUT_K * P
CHUNKS = SEQ // CHUNK


def wait(eng, sem, n):
    if not (isinstance(n, int) and n <= 0):
        eng.wait_ge(sem, n)


class Chain:

    def __init__(self, eng, sem):
        self.eng, self.sem, self.n = eng, sem, 0

    def __call__(self, ins):
        ins.then_inc(self.sem, 1)
        self.n = self.n + 1
        return ins

    def join(self):
        wait(self.eng, self.sem, self.n)


def two_pi_parts():
    rest, parts = 2 * np.pi, []
    for bits in (8, 10, 24):
        scale = 2.0 ** (bits - 1 - np.floor(np.log2(rest)))
        parts.append(float(np.float32(np.floor(rest * scale) / scale)))
        rest -= parts[-1]
    return parts


def build(nc, A, out, debug=False):
    ctx = ExitStack()
    with ctx:
        body(nc, A, out, ctx, debug)


def body(nc, A, out, ctx, debug):
    kind = "ExternalOutput" if debug else "Internal"

    def dram(name, shape, dt=F32):
        return nc.dram_tensor(name, shape, dt, kind=kind).ap()

    o_dil = dram("o_dil", [3, SEQ, DIL_HEADS * STAT])
    o_swa = dram("o_swa", [SEQ, SWA_HEADS * HD])
    rows_d = dram("mod_rows", [N_MOD, D])
    oT_d = dram("oT_d", [P, OUT_K, SEQ])
    mT_d = dram("mT_d", [P, KD, SEQ])
    x1_d = dram("x1_d", [SEQ, D])
    h2_d = dram("h2_d", [SEQ + PAD_ROWS // 2, D])
    y_d = dram("y_d", [2 * SEQ + PAD_ROWS, D])

    class Plan:
        def __init__(self, at):
            self.at = at

        def __call__(self, name, shape, dt=F32):
            size = int(np.prod(shape[1:])) * {F32: 4, F32R: 4, I32: 4, BF16: 2, F16: 2}[dt]
            t = nc.alloc_sbuf_tensor_at("sb_" + name, shape, dt, offset=self.at)
            self.at += (size + 31) // 32 * 32
            return t

    base = nc.sbuf_base
    base = (base + 31) // 32 * 32
    keep = Plan(base)
    ident = keep("ident", [P, P])
    ones_row = keep("ones_row", [1, 2])
    A1 = keep("A1", [P, KD])
    B1 = keep("B1", [P, KD])
    hT = keep("hT", [P, KD, SEQ])
    after_hT = keep.at

    top_size = (2 * 3 * TT * HALF * 4 + 4 * 256 * 2 + 3 * 384 * 2 + 2 * SWA_HEADS * 4
                + 2 * 3 * TT * 4 + HALF * 4)
    top = Plan((nc.sbuf_usable_end - top_size - 64) // 32 * 32)
    top_start = top.at
    cos_t = top("cos_t", [P, 3 * TT, HALF])
    sin_t = top("sin_t", [P, 3 * TT, HALF])
    mask_dil = top("mask_dil", [P, 4, 256], BF16)
    mask_swa = top("mask_swa", [P, 3, 384], BF16)
    sink_bc = top("sink_bc", [P, SWA_HEADS])
    nsink = top("nsink", [P, SWA_HEADS])
    pos_i = top("pos_i", [P, 3 * TT], I32)
    pos_f = top("pos_f", [P, 3 * TT])
    invf = top("invf", [P, HALF])
    ang, turn = sin_t, cos_t

    m2 = Plan(after_hT)
    w_raw = [m2(f"w_raw{c}", [P, PIECE]) for c in range(2)]
    w_hi = m2("w_hi", [P, 2 * KD, PASS_COLS], F32R)
    first_pass_end = m2.at + KD * PASS_COLS * 4
    w_lo = m2("w_lo", [P, 2 * KD, PASS_COLS], F32R)
    h_hi = [m2(f"h_hi{c}", [P, KD, P], F32R) for c in range(2)]
    h_lo = [m2(f"h_lo{c}", [P, KD, P], F32R) for c in range(2)]
    kT_dil = m2("kT_dil", [P, SEQ + 2 * HD])
    v_dil = m2("v_dil", [P, TT + 1, P])
    kT_swa = m2("kT_swa", [P, SEQ + 2 * P])
    v_swa = m2("v_swa", [P, TT + 2, HD])
    qk_raw = m2("qk_raw", [P, 320])
    qk_tmp = m2("qk_tmp", [P, 320])
    qk_rot = m2("qk_rot", [P, 320])
    qst = [m2(f"qst{c}", [P, 4, P]) for c in range(2)]
    e_sb = [m2(f"e_sb{u}", [P, 2, 384]) for u in range(2)]
    eT = m2("eT", [P, 2, 384])
    o_row = [[m2(f"o_row{c}{u}", [P, 2, STAT]) for u in range(2)] for c in range(2)]
    mx = m2("mx", [P, 2])
    snk = [[m2(f"snk{c}{u}", [P, 2]) for u in range(2)] for c in range(2)]
    esk = [[m2(f"esk{c}{u}", [P, 2]) for u in range(2)] for c in range(2)]
    rden = m2("rden", [P, 2])
    assert m2.at <= top_start, (m2.at, top_start)

    m0 = Plan(first_pass_end)
    c_col = m0("c_col", [P, KD])
    c_sil = m0("c_sil", [P, KD])
    bias_rows = m0("bias_rows", [MOD_CHUNKS, CHUNK])
    gain = m0("gain", [1, D])
    mod_row = [m0(f"mod_row{r}", [1, CHUNK]) for r in range(4)]
    wada = [m0(f"wada{r}", [P, KD // 2, CHUNK]) for r in range(4)]
    x_round = [m0(f"x_round{c}", [P, ROUND, D]) for c in range(2)]
    xn = [m0(f"xn{c}", [P, D]) for c in range(2)]
    ssq1 = m0("ssq1", [P, ROUND])
    ms1 = m0("ms1", [P, ROUND])
    rms1 = m0("rms1", [P, ROUND])
    rstd1 = m0("rstd1", [P, ROUND])
    assert m0.at <= top_start, (m0.at, top_start)

    m4 = Plan(after_hT)
    hT_lo = Plan(after_hT - KD * SEQ * 4)("hT_lo", [P, KD, SEQ], F32R)
    x_hi = [m4(f"x_hi{c}", [P, KD, CHUNK], F32R) for c in range(2)]
    g_raw = [m4(f"g_raw{j}", [P, GATE_COLS // 2]) for j in range(2)]
    g_hi = [m4(f"g_hi{c}", [P, GATE_COLS], F32R) for c in range(2)]
    g_lo = [m4(f"g_lo{c}", [P, GATE_COLS], F32R) for c in range(2)]
    sig = m4("sig", [P, 2, CHUNK])
    mg = [m4(f"mg{c}", [P, CHUNK]) for c in range(2)]
    after_weights = m4.at
    o_hi = [m4(f"o_hi{c}", [P, OUT_K, CHUNK], F32R) for c in range(2)]
    same_place = Plan(m4.at)
    o_in = [same_place(f"o_in{c}", [P, OUT_K, CHUNK]) for c in range(2)]
    o_lo = [m4(f"o_lo{c}", [P, OUT_K, CHUNK], F32R) for c in range(2)]
    assert m4.at <= nc.sbuf_usable_end, m4.at

    m3 = Plan(after_weights)
    od = [m3(f"od{c}", [P, 2, 3, DIL_HEADS * STAT]) for c in range(2)]
    ob = [m3(f"ob{c}", [P, 2, SWA_HEADS * HD]) for c in range(2)]
    wsum = m3("wsum", [P, 2, 3, DIL_HEADS * HD])
    oa = m3("oa", [P, 2, DIL_HEADS * HD])
    oT = [m3(f"oT{c}", [P, OUT_K, 2 * P]) for c in range(2)]
    nmin = m3("nmin", [P, 2, DIL_HEADS])
    wg = m3("wg", [P, 2, 3, DIL_HEADS])
    wden = m3("wden", [P, 2, 3, DIL_HEADS])
    dsum = m3("dsum", [P, 2, DIL_HEADS])
    assert m3.at <= nc.sbuf_usable_end, m3.at

    tables = Plan(after_hT - KD * SEQ * 4)
    pair_w = tables("pair_w", [P, TT, 2])
    scatter_idx = tables("scatter_idx", [P, MAX_BLOCKS + 1], I32)
    gather_idx = tables("gather_idx", [P, MAX_BLOCKS + 1], I32)
    expert_of = tables("expert_of", [1, MAX_BLOCKS + 1], I32)
    ends = tables("ends", [1, E], I32)

    m5 = Plan(tables.at)
    logits = m5("logits", [P, TT, GROUPS + E])
    wo_raw = [m5(f"wo_raw{c}", [P, D]) for c in range(4)]
    wo_hi = m5("wo_hi", [P, KD, D], F32R)
    wo_lo = m5("wo_lo", [P, KD, D], F32R)
    gt1b = m5("gt1b", [P, D])
    A2b = m5("A2b", [P, D])
    B2b = m5("B2b", [P, D])
    m_in = [m5(f"m_in{c}", [P, KD, P]) for c in range(2)]
    m_hi = [m5(f"m_hi{c}", [P, KD, P], F32R) for c in range(2)]
    m_lo = [m5(f"m_lo{c}", [P, KD, P], F32R) for c in range(2)]
    x_in = [m5(f"x_in{c}", [P, D]) for c in range(2)]
    x1 = [m5(f"x1{c}", [P, D]) for c in range(2)]
    h2 = [m5(f"h2{c}", [P, D]) for c in range(2)]
    h2T = m5("h2T", [P, KD, P])
    sq2 = m5("sq2", [P, D])
    zero_rows = m5("zero_rows", [PAD_ROWS // 2, D])
    w_rt = m5("w_rt", [P, KD, GROUPS + E])
    st2 = m5("st2", [P, 8])
    assert m5.at <= nc.sbuf_usable_end

    m6 = Plan(tables.at + TT * (GROUPS + E) * 4)
    ug = lambda name, n, dt=F32: m6(name, [P, TT, n], dt)
    r_bias = m6("r_bias", [P, GROUPS + E])
    iota_e = m6("iota_e", [P, TT, E])
    iota_r = m6("iota_r", [P, P])
    iota_b = m6("iota_b", [P, MAX_BLOCKS])
    flat_id = m6("flat_id", [P, TT, 2])
    pad_id = m6("pad_id", [P, 2])
    tri = m6("tri", [P, P], BF16)
    all_ones = m6("all_ones", [P, P], BF16)
    gmax = ug("gmax", 1)
    geq = ug("geq", GROUPS)
    gsel = ug("gsel", GROUPS)
    gex = ug("gex", GROUPS)
    gsum = ug("gsum", 1)
    gidx = ug("gidx", 1)
    el = ug("el", E)
    eeq = ug("eeq", E)
    oh = [ug(f"oh{k}", E) for k in range(2)]
    top = [ug(f"top{k}", 1) for k in range(2)]
    eidx = ug("eidx", 1)
    ratio = ug("ratio", 1)
    rinv = ug("rinv", 1)
    both = ug("both", E, BF16)
    posn = ug("posn", E)
    prod = ug("prod", E)
    slot_f = ug("slot_f", 2)
    slot_i = ug("slot_i", 2, I32)
    lane_i = ug("lane_i", 2, I32)
    blk_i = ug("blk_i", 2, I32)
    lane_f = ug("lane_f", 2)
    blk_f = ug("blk_f", 2)
    cnt = m6("cnt", [P, E])
    cnt_i = m6("cnt_i", [P, E], I32)
    nblk = m6("nblk", [P, E])
    pend = m6("pend", [P, E])
    pbase = m6("pbase", [P, E])
    cmp_e = m6("cmp_e", [P, MAX_BLOCKS, E])
    e_f = m6("e_f", [P, MAX_BLOCKS])
    lane_oh = [m6(f"lane_oh{k}", [P, P], F16) for k in range(2)]
    blk_oh = [m6(f"blk_oh{k}", [P, 2, MAX_BLOCKS], F16) for k in range(2)]
    tab = m6("tab", [P, 2, MAX_BLOCKS])
    idx_f = m6("idx_f", [P, MAX_BLOCKS])

    m8 = Plan(tables.at)
    xg = m8("xg", [P, D])
    x_hiT = m8("x_hiT", [P, KD, P], F32R)
    x_loT = m8("x_loT", [P, KD, P], F32R)
    hg = m8("hg", [P, DE])
    h_hiT = m8("h_hiT", [P, KE, P], F32R)
    h_loT = m8("h_loT", [P, KE, P], F32R)
    y_sb = m8("y_sb", [P, D])
    gi = m8("gi", [P, 1], I32)
    si = m8("si", [P, 1], I32)
    dn_hi = m8("dn_hi", [P, KE, D], F32R)
    dn_lo = m8("dn_lo", [P, KE, D], F32R)
    gu = m8("gu", [P, 4 * KD, 2 * DE], F32R)
    assert m8.at - 2 * KD * 2 * DE * 4 >= m6.at
    ring_at = m8.at
    w_in = [m8(f"w_in{s}", [P, 2 * DE]) for s in range(RING)]
    assert m8.at <= nc.sbuf_usable_end, (m8.at, nc.sbuf_usable_end)
    m9 = Plan(tables.at)
    yp = [m9(f"yp{r}", [P, 2, D]) for r in range(ROUND)]
    acc = m9("acc", [P, 2 * ROUND, D])
    sq3 = m9("sq3", [P, D])
    ssq3 = m9("ssq3", [P, ROUND])
    ms3 = m9("ms3", [P, ROUND])
    rms3 = m9("rms3", [P, ROUND])
    rstd3 = m9("rstd3", [P, ROUND])

    assert m9.at <= ring_at
    early = Plan(ring_at)
    gt2b = early("gt2b", [P, D])
    gfb = early("gfb", [P, D])
    xl = [early(f"xl{r}", [P, D]) for r in range(ROUND)]

    bank = [ctx.enter_context(nc.psum_tensor(f"bank{i}", [P, 512], F32)) for i in range(3)]
    S_ps = ctx.enter_context(nc.psum_tensor("S_ps", [P, 2, 512], F32))
    E_ps = ctx.enter_context(nc.psum_tensor("E_ps", [P, 2, 512], F32))
    O_ps = ctx.enter_context(nc.psum_tensor("O_ps", [P, 512], F32))

    PS = [bank[0], bank[1], bank[2], S_ps[:, 0, :], S_ps[:, 1, :], E_ps[:, 0, :], E_ps[:, 1, :], O_ps]

    sems = {}

    def sem(name):
        if name not in sems:
            sems[name] = ctx.enter_context(nc.semaphore(name))
        return sems[name]

    inv_freq = (np.float32(THETA) ** (-np.arange(HALF, dtype=np.float32) * np.float32(2.0 / HD))).astype(np.float32)
    PI2 = two_pi_parts()
    MAGIC = 1.5 * 2.0 ** 23

    block = ctx.enter_context(nc.Block())

    def dilation(g):
        return DILATIONS[g] if g < 3 else 1

    def tile_of(T):
        return T % TT

    def first_token(g, t):
        d = dilation(g)
        per = TT // d
        return (t % per) * (P * d) + t // per

    def mask_index(g, t):
        if g == 2:
            return 3
        per = TT // dilation(g)
        m = t % per
        return (m + per - 1) // per + m // (per - 1)

    def unit(g, T, u):
        return T if g < 3 else 2 * T - SWA_T0 + u

    def units(g):
        return (0,) if g < 3 else (0, 1)

    def weight_row(n):
        return ((n // TT) % 2) * KD + (n % TT) // 2

    def gu_row(e, part, k):
        return ((e + 1) % 2 * 2 + part) * KD + k

    def ring_count(e, j):
        first = 2 if j % RING >= 2 * RING - KD else 1
        return 16 * (first + 2 * e + j // RING + 1)

    def group_of(T):
        return min(max(T, 0) // TILES_PER_GROUP, 3)

    def schedule(eng, step):
        def straight(T):
            gs = [group_of(x) if 0 <= x < STEPS else None for x in (T + 1, T, T - 1, T - 2, T - 3)]
            step(T, T % 2, gs, T < STEPS - TT)

        def looped(g, first, last, loads):
            with eng.Fori(first // 2, last // 2) as i:
                for c in range(2):
                    step(2 * i + c, c, [g] * 5, loads)

        for g in range(4):
            T0 = g * TILES_PER_GROUP
            for T in range(T0, T0 + 4):
                straight(T)
            end = T0 + TILES_PER_GROUP - 2
            if g < 3:
                looped(g, T0 + 4, end, True)
            else:
                looped(g, T0 + 4, STEPS - TT - 2, True)
                straight(STEPS - TT - 2)
                straight(STEPS - TT - 1)
                looped(g, STEPS - TT, end, False)
            for T in range(end, T0 + TILES_PER_GROUP):
                straight(T)
        for T in range(STEPS, STEPS + 3):
            straight(T)

    def acc_row(t):
        return acc[:, ds(t % (2 * ROUND), 1), :].rearrange("p a n -> p (a n)")

    def chunk_loops(eng, chunk):
        with eng.Fori(0, CHUNKS // 2 - 1) as i:
            for c in range(2):
                chunk(2 * i + c, c, True)
        for c in range(2):
            chunk(CHUNKS - 2 + c, c, c == 0)

    @block.sync
    def _(sp):
        xv = A["x"].rearrange("a (t p) n -> p (a t) n", p=P)
        wq = A["w_qkv"].rearrange("n (k p) m -> p n k m", p=P)
        wv = A["w_ada"].rearrange("a (k p) n -> p (a k) n", p=P)

        def ada_half(n):
            j, h = n // 2, n % 2
            wait(sp, sem("mod_mm"), n - 3)
            sp.dma_start(wada[n % 4][:], wv[:, h * (KD // 2):(h + 1) * (KD // 2), j * CHUNK:(j + 1) * CHUNK]).then_inc(sem(f"slot_in{n % 4}"), 16)

        def x_in_round(q):
            wait(sp, sem("xn_ready"), ROUND * (q - 1))
            sp.dma_start(x_round[q % 2][:], xv[:, ROUND * q:ROUND * (q + 1), :]).then_inc(sem(f"x_in{q % 2}"), 16)

        def row_out(j):
            sp.wait_ge(sem("mod_row"), j + 1)
            sp.dma_start(rows_d[j // 2:j // 2 + 1, (j % 2) * CHUNK:(j % 2 + 1) * CHUNK], mod_row[j % 4][:]).then_inc(sem("rows_out"), 16)

        def piece(n, c):
            wait(sp, sem("w_lo_ready"), n - 1)
            t = n % TT
            sp.dma_start(w_raw[c][:].rearrange("p (a b m) -> p a b m", a=1, b=1), wq[:, ds(n // TT, 1), ds(t // 2, 1), c * PIECE:(c + 1) * PIECE]).then_inc(sem(f"w_in{c}"), 16)

        sp.dma_start(c_col[:], A["c"].rearrange("a (k p) -> p (a k)", p=P), allow_slow_non_contiguous=True).then_inc(sem("c_in"), 16)
        for j in range(MOD_CHUNKS):
            for h in range(2):
                ada_half(2 * j + h)
            if j == 0:
                sp.dma_start(bias_rows[:], A["b_ada"].rearrange("a (j n) -> (a j) n", n=CHUNK)).then_inc(sem("g_in"), 16)
                sp.dma_start(gain[:], A["g_mix"][0:1, :]).then_inc(sem("g_in"), 16)
                pos = A["positions"]
                sp.dma_start(pos_i[:, 0:TT], pos.rearrange("a (t i) -> i (a t)", i=P), allow_slow_non_contiguous=True).then_inc(sem("pos_in"), 16)
                for r in range(4):
                    sp.dma_start(pos_i[:, TT + 4 * r:TT + 4 * r + 4], pos.rearrange("a (b i r) -> r i (a b)", i=P, r=4)[r], allow_slow_non_contiguous=True).then_inc(sem("pos_in"), 16)
                sp.dma_start(pos_i[:, 2 * TT:3 * TT], pos.rearrange("a (i r) -> i (a r)", i=P)).then_inc(sem("pos_in"), 16)
                sp.dma_start(sink_bc[:], A["sink_logits"][0:1, :].broadcast_to([P, SWA_HEADS])).then_inc(sem("pos_in"), 16)
            if j % 2 == 1 and j > 0 and (j - 1) // 2 in (0, 1):
                x_in_round((j - 1) // 2)
            if j in (7, 9):
                x_in_round((j - 3) // 2)
            if j >= NORM_FROM:
                for n in (2 * (j - NORM_FROM), 2 * (j - NORM_FROM) + 1):
                    piece(n, n % 2)
            if j > NORM_FROM:
                row_out(j - 1)
            if j == NORM_FROM + 1:
                sp.dma_start(gain[:], A["g_ffn"][0:1, :]).then_inc(sem("g_in"), 16)
        row_out(MOD_CHUNKS - 1)
        for n in range(TT, TT + 2):
            piece(n, n % 2)

        def step(T, c, gs, loads):
            g = gs[4]
            if g is not None:
                S = T - 3
                s, t = (S // TT) % 2, tile_of(S)
                tok = first_token(g, t)
                for u in units(g):
                    sp.wait_ge(sem("o_done"), unit(g, S, u) + 1)
                    if g < 3:
                        d = dilation(g)
                        dst = o_dil[g:g + 1, ds(tok, P, step=d), ds(s * (2 * STAT), 2 * STAT)]
                        src = o_row[1 - c][u][:].rearrange("p h m -> p (h m)")
                        dst = dst.rearrange("a p m -> (a p) m")
                    else:
                        dst = o_swa[ds(tok, P), ds(s * 256 + u * 128, 128)].rearrange("p (h m) -> p h m", h=2)
                        src = o_row[1 - c][u][:, :, 0:HD]
                    sp.dma_start(dst, src).then_inc(sem(f"o_out{1 - c}{u}"), 16)
            if loads and not (isinstance(T, int) and T + TT + 2 >= PASSES * TT):
                piece(T + TT + 2, c)

        schedule(sp, step)
        for c in range(2):
            sp.wait_ge(sem(f"o_out{c}0"), 16 * STEPS // 2)
            sp.wait_ge(sem(f"o_out{c}1"), 16 * TILES_PER_GROUP // 2)
        gv = A["w_gb"]

        def gate_piece(tile, j, last_use):
            wait(sp, sem("g_lo_ready"), last_use)
            cols = slice(j * (GATE_COLS // 2), (j + 1) * (GATE_COLS // 2))
            sp.dma_start(g_raw[j][:], gv[ds(tile, 1), :, cols].rearrange("a p m -> (a p) m")).then_inc(sem(f"g_in{j}"), 16)

        for j in range(2):
            gate_piece(0, j, 0)

        odv = o_dil.rearrange("g (t p) m -> p t g m", p=P)
        obv = o_swa.rearrange("(i u p) m -> p i u m", p=P, u=2)

        def dilated_in(i, c):
            for u in range(2):
                sp.dma_start(od[c][:, u], odv[:, ds(2 * i + u, 1)].rearrange("p a g m -> p (a g) m")).then_inc(sem(f"od_in{c}"), 16)

        def windowed_in(i, c):
            sp.dma_start(ob[c][:], obv[:, ds(i, 1)].rearrange("p a u m -> p (a u) m")).then_inc(sem(f"od_in{c}"), 16)

        def merge_out(i, c):
            sp.wait_ge(sem("oT_ready"), 2 * i + 4)
            sp.dma_start(oT_d[:, :, ds(i * 2 * P, 2 * P)], oT[c][:]).then_inc(sem(f"oT_out{c}"), 16)

        for c in range(2):
            sp.sem_inc(sem(f"oT_out{c}"), 16)
            dilated_in(c, c)
            windowed_in(c, c)
        with sp.Fori(0, TT // 4 - 1) as i:
            for c in range(2):
                pair = 2 * i + c
                sp.wait_ge(sem("oa_ready"), pair + 1)
                dilated_in(pair + 2, c)
                sp.wait_ge(sem("oT_done"), 2 * pair + 3)
                windowed_in(pair + 2, c)
                merge_out(pair, c)
        for c in range(2):
            merge_out(TT // 2 - 2 + c, c)
        for c in range(2):
            sp.wait_ge(sem(f"oT_out{c}"), 16 * (TT // 4 + 1))

        def branch_inputs(q, cc):
            sp.dma_start(o_in[cc][:], oT_d[:, :, ds(q * CHUNK, CHUNK)]).then_inc(sem("o_in"), 16)

        def chunk(q, cc, more):
            with sp.Fori(0, KD // 2) as i:
                for c in range(2):
                    for j in range(2):
                        gate_piece((2 * i + c + 1) % KD, j, 2 * (KD * q + 2 * i + c) + j + 1)
            if more:
                sp.wait_ge(sem("gates_done"), KD * q + 2)
                branch_inputs(q + 1, 1 - cc)

        branch_inputs(0, 0)
        chunk_loops(sp, chunk)

        wov = A["w_out"].rearrange("a (k p) n -> p (a k) n", p=P)
        sp.wait_ge(sem("merged"), CHUNKS * KD)
        sp.wait_ge(sem("g_lo_ready"), 2 * CHUNKS * KD + 2)
        def tile_in(t, c):
            sp.dma_start(m_in[c][:], mT_d[:, :, ds(t * P, P)]).then_inc(sem(f"m_in{c}"), 16)
            sp.dma_start(x_in[c][:], xv[:, ds(t, 1), :].rearrange("p a n -> p (a n)")).then_inc(sem(f"x_in{c}"), 16)

        for k in range(KD):
            wait(sp, sem("wo_lo_ready"), k - 3)
            sp.dma_start(wo_raw[k % 4][:], wov[:, k, :]).then_inc(sem(f"slot_in{k % 4}"), 16)
            if k == 0:
                for c in range(2):
                    sp.wait_ge(sem(f"mT_out{c}"), 16 * (CHUNKS * KD // 2 + 1))
                tile_in(0, 0)
            if k == 3:
                for n, (t, row) in enumerate(((gt1b, 2), (A2b, 4), (B2b, 3))):
                    sp.dma_start(t[:], rows_d[row:row + 1, :].broadcast_to([P, D])).then_inc(sem("rows_in"), 16)
                sp.dma_start(w_rt[:], A["w_rt"].rearrange("(k p) n -> p k n", p=P)).then_inc(sem("rows_in"), 16)
                sp.wait_ge(sem("zero_rows"), 1)
                sp.dma_start(h2_d[SEQ:SEQ + PAD_ROWS // 2, :], zero_rows[:]).then_inc(sem("pads_out"), 16)

        def tile_out(t, c):
            sp.wait_ge(sem("h2_ready"), t + 1)
            sp.dma_start(x1_d[ds(t * P, P), :], x1[c][:]).then_inc(sem(f"x1_out{c}"), 16)
            sp.dma_start(h2_d[ds(t * P, P), :], h2[c][:]).then_inc(sem(f"x1_out{c}"), 16)

        tile_in(1, 1)
        with sp.Fori(0, TT // 2 - 1) as i:
            for c in range(2):
                t = 2 * i + c
                sp.wait_ge(sem("m_lo_ready"), t + 1)
                sp.wait_ge(sem("x1_ready"), t + 1)
                tile_in(t + 2, c)
                tile_out(t, c)
        for c in range(2):
            tile_out(TT - 2 + c, c)
        for c in range(2):
            sp.wait_ge(sem(f"x1_out{c}"), 32 * (TT // 2))
        sp.wait_ge(sem("pads_out"), 16)
        sp.sem_inc(sem("h2_stored"), 1)

        sp.wait_ge(sem("logits_ready"), TT)
        sp.dma_start(r_bias[:], A["b_rt"][0:1, :].broadcast_to([P, GROUPS + E])).then_inc(sem("rows_in"), 16)
        wgu_v = A["w_gate_up"].rearrange("e (k p) n -> p e k n", p=P)
        wd_v = A["w_expert_down"].rearrange("a e (k p) n -> p (a e) k n", p=P)

        def gu_piece(e, k, slot):
            sp.dma_start(w_in[slot][:].rearrange("p (a n) -> p a n", a=1), wgu_v[:, ds(e, 1), k, :]).then_inc(sem(f"ring_in{slot}"), 16)

        def dn_piece(e, k, slot):
            sp.dma_start(w_in[slot][:].rearrange("p (a n) -> p a n", a=1), wd_v[:, ds(e, 1), k, :]).then_inc(sem(f"ring_in{slot}"), 16)

        for k in range(KD):
            slot = (k + 2 * RING - KD) % RING
            if k >= RING:
                sp.wait_ge(sem("gu_lo_ready"), k - RING + 1)
            gu_piece(0, k, slot)

        def expert_in(e):
            for j in range(PIECES):
                if j >= RING:
                    sp.wait_ge(sem("gu_lo_ready"), KD * (e + 1) + j - RING + 1)
                elif isinstance(e, int) and e == 0:
                    sp.wait_ge(sem("gu_lo_ready"), KD - RING + j + 1)
                elif j < RING - KE:
                    sp.wait_ge(sem("gu_lo_ready"), KD * e + RING + j + 1)
                else:
                    sp.wait_ge(sem("dn_lo_ready"), KE * e - RING + j + 1)
                if j < KD:
                    gu_piece(e + 1, j, j % RING)
                else:
                    dn_piece(e, j - KD, j % RING)

        expert_in(0)
        with sp.Fori(1, E - 1) as e:
            expert_in(e)
        for k in range(KE):
            sp.wait_ge(sem("dn_lo_ready"), KE * (E - 2) + k + 1)
            dn_piece(E - 1, k, (KD + k) % RING)

        sp.wait_ge(sem("dn_lo_ready"), KE * E)
        for t, row in ((gt2b, rows_d[5:6, :]), (gfb, A["g_final"].rearrange("(a n) -> a n", a=1))):
            sp.dma_start(t[:], row.broadcast_to([P, D])).then_inc(sem("rows_in"), 16)
        yv = y_d[0:2 * SEQ, :].rearrange("(t p two) n -> p t two n", p=P, two=2)
        x1v = x1_d.rearrange("(t p) n -> p t n", p=P)
        ov = out.rearrange("a (t p) n -> p (a t) n", p=P)

        def x1_in(t, r):
            sp.dma_start(xl[r][:], x1v[:, ds(t, 1)].rearrange("p a n -> p (a n)")).then_inc(sem(f"slot_in{r}"), 16)

        def outputs_in(t, r):
            sp.dma_start(yp[r][:], yv[:, ds(t, 1)].rearrange("p a two n -> p (a two) n")).then_inc(sem(f"slot_in{r}"), 16)

        def last_out(t, r):
            sp.wait_ge(sem("out_ready"), t + 1)
            sp.dma_start(ov[:, ds(t, 1), :].rearrange("p a n -> p (a n)"), acc_row(t)).then_inc(sem(f"out_stored{r}"), 16)

        for r in range(ROUND):
            sp.sem_inc(sem(f"out_stored{r}"), 16)
            x1_in(r, r)
        sp.wait_ge(sem("experts_done"), 1)
        for r in range(ROUND):
            outputs_in(r, r)

        def last_round(q, more):
            for r in range(ROUND):
                t = ROUND * q + r
                if more:
                    sp.wait_ge(sem("acc_ready"), t + 1)
                    outputs_in(t + ROUND, r)
                    x1_in(t + ROUND, r)
                if not isinstance(t, int) or t >= LAG:
                    last_out(t - LAG, (r - LAG) % ROUND)

        last_round(0, True)
        last_round(1, True)
        with sp.Fori(2, TT // ROUND - 1) as q:
            last_round(q, True)
        last_round(TT // ROUND - 1, False)
        for t in range(TT - LAG, TT):
            last_out(t, t % ROUND)
        for r in range(ROUND):
            sp.wait_ge(sem(f"out_stored{r}"), 16 * (TT // ROUND + 1))

    @block.gpsimd
    def _(pool):
        ch = Chain(pool, sem("pool_chain"))
        ch(nc.gpsimd.memset(ident[:], 0.0))
        ch(nc.gpsimd.memset(ones_row[:], 1.0))
        ch.join()
        nc.gpsimd.affine_select(out=ident[:], in_=ident[:], compare_op=ALU.not_equal, fill=1.0, base=0,
                                pattern=[[-1, P]], channel_multiplier=1).then_inc(sem("ident_ready"), 1)
        for k in range(HALF):
            last = nc.gpsimd.memset(invf[:, k:k + 1], float(inv_freq[k]))
        last.then_inc(sem("invf_ready"), 1)
        for m, w, var in ((mask_dil, HD, 4), (mask_swa, P, 3)):
            n = P + 2 * w
            ch(nc.gpsimd.memset(m[:], 0.0))
            ch.join()
            for v in range(var):
                cuts = [(1, -1, 0), (-1, 1, 2 * w)]
                if v in (0, 3):
                    cuts.append((1, 0, -w))
                if v in (2, 3):
                    cuts.append((-1, 0, P + w - 1))
                for step_c, step_i, b in cuts:
                    ch(nc.gpsimd.affine_select(out=m[:, v, :], in_=m[:, v, :], compare_op=ALU.is_ge, fill=NEG, base=b,
                                               pattern=[[step_c, n]], channel_multiplier=step_i))
                    ch.join()
        def tile_src(g, T):
            tok = first_token(g, tile_of(T))
            return hT[:, :, ds(tok, P, step=dilation(g))]

        def lower_tile(T, c, g):
            pool.wait_ge(sem("h_hi_ready"), T + 1)
            nc.gpsimd.tensor_tensor(h_lo[c][:], tile_src(g, T), h_hi[c][:].bitcast(F32), ALU.subtract).then_inc(sem("h_lo_ready"), 1)

        def lower_piece(n, c):
            pool.wait_ge(sem("w_hi_ready"), n + 1)
            k = weight_row(n)
            cols = slice(c * PIECE, (c + 1) * PIECE)
            raw = w_raw[c][:].rearrange("p (a m) -> p a m", a=1)
            nc.gpsimd.tensor_tensor(w_lo[:, ds(k, 1), cols], raw, w_hi[:, ds(k, 1), cols].bitcast(F32), ALU.subtract).then_inc(sem("w_lo_ready"), 1)

        for n in range(TT):
            lower_piece(n, n % 2)
        pool.wait_ge(sem("h_all"), TT)
        pool.wait_ge(sem("rows_out"), 16 * (MOD_CHUNKS - NORM_FROM))
        for q in qst:
            ch(nc.gpsimd.memset(q[:], 0.0))
        for t, lo, hi in ((kT_dil, 0, HD), (kT_dil, HD + SEQ, 2 * HD + SEQ), (kT_swa, 0, P), (kT_swa, P + SEQ, 2 * P + SEQ)):
            ch(nc.gpsimd.memset(t[:, lo:hi], 0.0))
        ch(nc.gpsimd.memset(v_dil[0:HD, 0, :], 0.0))
        ch.join()
        ch(nc.gpsimd.memset(v_dil[HD:P, TT, :], 0.0))
        ch.join()
        ch(nc.gpsimd.memset(v_swa[:, 0, :], 0.0))
        nc.gpsimd.memset(v_swa[:, TT + 1, :], 0.0).then_inc(sem("attn_consts"), 1)
        lower_tile(0, 0, 0)

        def step(T, c, gs, loads):
            if gs[0] is not None:
                lower_tile(T + 1, 1 - c, gs[0])
            if loads and not (isinstance(T, int) and T + TT >= PASSES * TT):
                lower_piece(T + TT, c)

        schedule(pool, step)

        def lower_gate(n, c):
                for j in range(2):
                    pool.wait_ge(sem("g_hi_ready"), 2 * n + j + 1)
                    cols = slice(j * (GATE_COLS // 2), (j + 1) * (GATE_COLS // 2))
                    nc.gpsimd.tensor_tensor(g_lo[c][:, cols], g_raw[j][:], g_hi[c][:, cols].bitcast(F32), ALU.subtract).then_inc(sem("g_lo_ready"), 1)

        lower_gate(0, 0)
        with pool.Fori(0, CHUNKS * KD // 2) as i:
            for c in range(2):
                lower_gate(2 * i + c + 1, 1 - c)
        pool.wait_ge(sem("wo_hi_ready"), 2)
        nc.gpsimd.memset(zero_rows[:], 0.0).then_inc(sem("zero_rows"), 1)
        with pool.Fori(0, TT // 2) as i:
            for c in range(2):
                pool.wait_ge(sem("m_hi_ready"), 2 * i + c + 1)
                nc.gpsimd.tensor_tensor(m_lo[c][:], m_in[c][:], m_hi[c][:].bitcast(F32), ALU.subtract).then_inc(sem("m_lo_ready"), 1)

        pool.wait_ge(sem("logits_ready"), TT)
        exact = dict(allow_small_or_imprecise_dtypes=True)
        ch(nc.gpsimd.iota(iota_e[:], pattern=[[0, TT], [1, E]], base=0, channel_multiplier=0, **exact))
        ch(nc.gpsimd.iota(iota_r[:], pattern=[[1, P]], base=0, channel_multiplier=0, **exact))
        ch(nc.gpsimd.iota(iota_b[:], pattern=[[1, MAX_BLOCKS]], base=0, channel_multiplier=0, **exact))
        ch(nc.gpsimd.iota(flat_id[:], pattern=[[2 * P, TT], [1, 2]], base=-SEQ, channel_multiplier=2, **exact))
        ch(nc.gpsimd.iota(pad_id[:, 0:1], pattern=[[0, 1]], base=2 * SEQ, channel_multiplier=1, **exact))
        ch(nc.gpsimd.iota(pad_id[:, 1:2], pattern=[[0, 1]], base=SEQ - 2 * SEQ, channel_multiplier=-1, **exact))
        ch(nc.gpsimd.memset(all_ones[:], 1.0))
        ch(nc.gpsimd.memset(tri[:], 1.0))
        ch.join()
        nc.gpsimd.affine_select(out=tri[:], in_=tri[:], compare_op=ALU.is_gt, fill=0.0, base=0,
                                pattern=[[1, P]], channel_multiplier=-1).then_inc(sem("route_consts"), 1)

        pool.wait_ge(sem("tables_ready"), 1)
        pool.wait_ge(sem("h2_stored"), 1)
        total = pool.value_load(ends[0:1, E - 1:E], min_val=E, max_val=MAX_BLOCKS)

        def gather_block(g):
            nc.gpsimd.tensor_copy(gi[:], gather_idx[:, ds(g, 1)]).then_inc(sem("gi_ready"), 1)
            pool.wait_ge(sem("gi_ready"), g + 1)
            pool.sem_inc(sem("row_dmas"), 1)
            nc.gpsimd.indirect_dma_start(xg[:], None, h2_d, bass.IndirectOffsetOnAxis(ap=gi[:, 0:1], axis=0)).then_inc(sem("xg_in"), 16)

        def scatter_block(g):
            nc.gpsimd.tensor_copy(si[:], scatter_idx[:, ds(g, 1)]).then_inc(sem("si_ready"), 1)
            pool.wait_ge(sem("si_ready"), g + 1)
            pool.wait_ge(sem("y_ready"), g + 2)
            pool.sem_inc(sem("row_dmas"), 1)
            nc.gpsimd.indirect_dma_start(y_d, bass.IndirectOffsetOnAxis(ap=si[:, 0:1], axis=0), y_sb[:], None).then_inc(sem("y_out"), 16)

        pool.sem_inc(sem("y_free"), 1)
        gather_block(0)
        pool.wait_ge(sem("xgT_done"), 1)
        gather_block(1)
        with pool.Fori(1, total) as g:
            pool.wait_ge(sem("xgT_done"), g + 1)
            gather_block(g + 1)
            scatter_block(g - 1)
            pool.wait_ge(sem("y_out"), 16 * g)
            pool.sem_inc(sem("y_free"), 1)
        scatter_block(total - 1)
        pool.wait_ge(sem("y_out"), 16 * total)
        pool.sem_inc(sem("experts_done"), 1)

    @block.scalar
    def _(act):
        act.wait_ge(sem("c_in"), 16)
        nc.scalar.activation(c_sil[:], c_col[:], ACT.Silu).then_inc(sem("c_silu"), 1)
        def raise_tile(T, c, g):
            tok = first_token(g, tile_of(T))
            nc.scalar.activation(h_hi[c][:], hT[:, :, ds(tok, P, step=dilation(g))], ACT.Copy).then_inc(sem("h_hi_ready"), 1)

        def raise_piece(n, c):
            act.wait_ge(sem(f"w_in{c}"), 16 * (n // 2 + 1))
            k = weight_row(n)
            raw = w_raw[c][:].rearrange("p (a m) -> p a m", a=1)
            nc.scalar.activation(w_hi[:, ds(k, 1), c * PIECE:(c + 1) * PIECE], raw, ACT.Copy).then_inc(sem("w_hi_ready"), 1)

        def squares(q):
            act.wait_ge(sem(f"x_in{q % 2}"), 16 * (q // 2 + 1))
            wait(act, sem("xT_done"), ROUND * q)
            for r in range(ROUND):
                wait(act, sem("sumsq"), ROUND * q + r)
                nc.scalar.activation(xn[0][:], x_round[q % 2][:, r, :], ACT.Square, accum_out=ssq1[:, r:r + 1]).then_inc(sem("sumsq"), 1)
            act.wait_ge(sem("meansq"), q + 1)
            nc.scalar.activation(rms1[:], ms1[:], ACT.Sqrt).then_inc(sem("rms"), 1)

        def scale_row(t):
            act.wait_ge(sem("rstd"), t // ROUND + 1)
            wait(act, sem("xT_done"), t - 1)
            nc.scalar.activation(xn[t % 2][:], x_round[t // ROUND % 2][:, t % ROUND, :], ACT.Copy, scale=rstd1[:, t % ROUND:t % ROUND + 1]).then_inc(sem("xn_ready"), 1)

        squares(0)
        act.wait_ge(sem("reduced"), 2)
        nc.scalar.activation(sin_t[:], ang[:], ACT.Sin).then_inc(sem("angles_ready"), 1)
        nc.scalar.activation(cos_t[:], turn[:], ACT.Sin).then_inc(sem("angles_ready"), 1)
        for j in range(TT // 2):
            scale_row(2 * j)
            scale_row(2 * j + 1)
            for n in (2 * j, 2 * j + 1):
                raise_piece(n, n % 2)
            if j % 2 == 1 and (j + 1) // 2 < ROUNDS:
                squares((j + 1) // 2)
        act.wait_ge(sem("h_all"), TT)
        act.wait_ge(sem("rows_out"), 16 * (MOD_CHUNKS - NORM_FROM))
        raise_tile(0, 0, 0)
        act.wait_ge(sem("attn_consts"), 1)

        def take_projection(T, c, g):
            act.wait_ge(sem("proj_done"), T + 1)
            wait(act, sem("rot_done"), T)
            t = tile_of(T)
            src = bank[c]
            nq = 256 if g < 3 else 320
            nc.scalar.activation(qk_raw[:, 0:nq], src[:, 0:nq], ACT.Copy)
            if g < 3:
                nc.scalar.activation(v_dil[HD:P, ds(t, 1), :], src[0:HD, 256:384].rearrange("p (a m) -> p a m", a=1), ACT.Copy)
                last = nc.scalar.activation(v_dil[0:HD, ds(t + 1, 1), :], src[HD:P, 256:384].rearrange("p (a m) -> p a m", a=1), ACT.Copy)
            else:
                last = nc.scalar.activation(v_swa[:, ds(t + 1, 1), :], src[:, 320:384].rearrange("p (a m) -> p a m", a=1), ACT.Copy)
            last.then_inc(sem("proj_evicted"), 1)

        def step(T, c, gs, loads):
            if gs[0] is not None:
                raise_tile(T + 1, 1 - c, gs[0])
            if loads and not (isinstance(T, int) and T + TT >= PASSES * TT):
                raise_piece(T + TT, c)
            g2, g3 = gs[3], gs[4]

            def probs_T(u):
                n = unit(g3, T - 3, u)
                act.wait_ge(sem("eT_done"), n + 1)
                w = 256 if g3 < 3 else 384
                src = E_ps[:, 0, :] if g3 < 3 else E_ps[:, :, 0:384]
                if g3 < 3:
                    src = src.rearrange("p (h w) -> p h w", h=2)
                nc.scalar.activation(eT[:, :, 0:w], src, ACT.Copy).then_inc(sem("eT_ready"), 1)

            def exponentials(u):
                n = unit(g2, T - 2, u)
                act.wait_ge(sem("max_ready"), n + 1)
                w = 256 if g2 < 3 else 384
                row = o_row[c][u]
                for h in range(2):
                    last = nc.scalar.activation(e_sb[u][:, h, 0:w], e_sb[u][:, h, 0:w], ACT.Exp, bias=row[:, h, HD:HD + 1],
                                                scale=SCALE, accum_out=row[:, h, HD + 1:HD + 2])
                if g2 == 3:
                    last = nc.scalar.activation(esk[c][u][:], snk[c][u][:], ACT.Exp)
                last.then_inc(sem("exp_done"), 1)

            if g3 is not None:
                probs_T(0)
            if g3 == 3:
                probs_T(1)
            if gs[1] is not None:
                take_projection(T, c, gs[1])
            if g2 is not None:
                for u in units(g2):
                    exponentials(u)

        schedule(act, step)

        def raise_gate(n, c):
            act.wait_ge(sem("gates_done"), n + 1)
            for j in range(2):
                act.wait_ge(sem(f"g_in{j}"), 16 * (n + 1))
                cols = slice(j * (GATE_COLS // 2), (j + 1) * (GATE_COLS // 2))
                nc.scalar.activation(g_hi[c][:, cols], g_raw[j][:], ACT.Copy).then_inc(sem("g_hi_ready"), 1)

        def raise_chunk(q, k, cc):
            nc.scalar.activation(x_hi[cc][:, ds(k, 1), :], hT[:, ds(k, 1), ds(q * CHUNK, CHUNK)], ACT.Copy).then_inc(sem("x_hi_ready"), 1)

        act.wait_ge(sem("o_done"), SWA_T0 + 2 * TILES_PER_GROUP)
        raise_gate(0, 0)
        act.sem_inc(sem("oT_ready"), 2)
        with act.Fori(0, TT // 4) as i:
            for c in range(2):
                pair = 2 * i + c
                act.wait_ge(sem("wg_in"), pair + 1)
                nc.scalar.activation(wg[:], wg[:], ACT.Exp).then_inc(sem("wg_exp"), 1)
                raise_chunk(0, pair, 0)
                act.wait_ge(sem(f"oT_out{c}"), 16 * (i + 1))
                for u in range(2):
                    act.wait_ge(sem("oT_done"), 2 * pair + u + 2)
                    cols = slice(u * P, (u + 1) * P)
                    nc.scalar.activation(oT[c][:, 0:2, cols], PS[2 * u][:, 0:2 * P].rearrange("p (k s) -> p k s", k=2), ACT.Copy)
                    nc.scalar.activation(oT[c][:, 2:OUT_K, cols], PS[2 * u + 1][:, 0:4 * P].rearrange("p (k s) -> p k s", k=4), ACT.Copy).then_inc(sem("oT_ready"), 1)

        def gate_chunk(q, cc, more):
            act.wait_ge(sem("o_in"), 16 * (q + 1))
            nc.scalar.activation(o_hi[cc][:], o_in[cc][:], ACT.Copy).then_inc(sem("o_hi_ready"), 1)
            with act.Fori(0, KD // 2) as i:
                for c in range(2):
                    n = KD * q + 2 * i + c
                    raise_gate(n + 1, 1 - c)
                    act.wait_ge(sem("gates_done"), n + 3)
                    for j in range(2):
                        last = nc.scalar.activation(sig[:, j, :], PS[4 * c + j][:], ACT.Sigmoid)
                    last.then_inc(sem("sig_ready"), 1)
                    if more:
                        raise_chunk(q + 1, 2 * i + c, 1 - cc)
                    act.wait_ge(sem("merged"), n + 1)
                    act.dma_start(mT_d[:, ds(2 * i + c, 1), ds(q * CHUNK, CHUNK)], mg[c][:].rearrange("p (a s) -> p a s", a=1)).then_inc(sem(f"mT_out{c}"), 16)

        for c in range(2):
            act.sem_inc(sem(f"mT_out{c}"), 16)
        chunk_loops(act, gate_chunk)

        def high_out(k):
            act.wait_ge(sem(f"slot_in{k % 4}"), 16 * (MOD_LOADS + k // 4 + 1))
            nc.scalar.activation(wo_hi[:, k, :], wo_raw[k % 4][:], ACT.Copy).then_inc(sem("wo_hi_ready"), 1)

        high_out(0)

        def high_tile(t, c, i):
            act.wait_ge(sem(f"m_in{c}"), 16 * (i + 1))
            wait(act, sem("y_done"), t - 1)
            nc.scalar.activation(m_hi[c][:], m_in[c][:], ACT.Copy).then_inc(sem("m_hi_ready"), 1)

        def norm_tile(t, c):
            act.wait_ge(sem("x1_ready"), t + 1)
            nc.scalar.activation(sq2[:], x1[c][:], ACT.Square, accum_out=st2[:, 0:1]).then_inc(sem("sumsq"), 1)
            act.wait_ge(sem("meansq"), ROUNDS + t + 1)
            nc.scalar.activation(st2[:, 2:3], st2[:, 1:2], ACT.Sqrt).then_inc(sem("rms"), 1)

        def evict_tile(t):
            act.wait_ge(sem("h2T_done"), t + 1)
            for j in range(2):
                last = nc.scalar.activation(h2T[:, 4 * j:4 * j + 4, :], PS[4 + j][:].rearrange("p (k s) -> p k s", k=4), ACT.Copy)
            last.then_inc(sem("h2T_ready"), 1)

        high_tile(0, 0, 0)
        for k in range(1, KD):
            high_out(k)
        high_tile(1, 1, 0)
        norm_tile(0, 0)
        high_tile(2, 0, 1)
        evict_tile(0)
        norm_tile(1, 1)

        def out_pair(i, more):
            for c in range(2):
                t = 2 * i + c
                if c == 0 or more:
                    high_tile(t + 1, 1 - c, i + c)
                evict_tile(t - 1)
                norm_tile(t, c)

        with act.Fori(1, TT // 2 - 1) as i:
            out_pair(i, True)
        out_pair(TT // 2 - 1, False)
        evict_tile(TT - 1)

        for n, t in enumerate((gex, ratio)):
            act.wait_ge(sem("differences"), n + 1)
            nc.scalar.activation(t[:], t[:], ACT.Exp).then_inc(sem("exponentials"), 1)

        def gate_up_high(e, k, slot, count):
            act.wait_ge(sem(f"ring_in{slot}"), count)
            nc.scalar.activation(gu[:, ds(gu_row(e, 0, k), 1), :], w_in[slot][:].rearrange("p (a n) -> p a n", a=1), ACT.Copy).then_inc(sem("gu_hi_ready"), 1)

        def next_expert_high(g, e):
            wait(act, sem("gu_done"), g)
            for j in range(KD):
                gate_up_high(e + 1, j, j % RING, ring_count(e, j))

        def down_high(g, e, extra=0):
            wait(act, sem("down_done"), g)
            for k in range(KE):
                slot = (KD + k) % RING
                act.wait_ge(sem(f"ring_in{slot}"), ring_count(e, KD + k) - extra)
                nc.scalar.activation(dn_hi[:, k, :], w_in[slot][:], ACT.Copy).then_inc(sem("dn_hi_ready"), 1)

        def rows_T(g):
            act.wait_ge(sem("xgT_done"), g + 1)
            if not isinstance(g, int) or g > 0:
                act.wait_ge(sem("gu_done"), g)
            for j in range(2):
                last = nc.scalar.activation(x_hiT[:, 4 * j:4 * j + 4, :], PS[2 + j][:].rearrange("p (k s) -> p k s", k=4), ACT.Copy)
            last.then_inc(sem("xT_high"), 1)

        def rows_out(g):
            act.wait_ge(sem("down_done"), g + 1)
            act.wait_ge(sem("y_free"), g + 1)
            for j in range(2):
                last = nc.scalar.activation(y_sb[:, j * 512:(j + 1) * 512], PS[4 + j][:], ACT.Copy)
            last.then_inc(sem("y_ready"), 1)

        def block(g):
            act.wait_ge(sem("gu_done"), g + 1)
            wait(act, sem("hT_done"), g)
            nc.scalar.activation(hg[:], PS[0][:], ACT.Silu).then_inc(sem("silu_done"), 1)
            rows_T(g + 1)
            if not isinstance(g, int):
                rows_out(g - 1)
            act.wait_ge(sem("hT_done"), g + 1)
            nc.scalar.activation(h_hiT[:], PS[6][:].rearrange("p (k s) -> p k s", k=KE), ACT.Copy).then_inc(sem("hT_high"), 1)

        for k in range(KD):
            slot = (k + 2 * RING - KD) % RING
            gate_up_high(0, k, slot, 16 * (k // RING + 1))
        act.sem_inc(sem("y_ready"), 1)
        act.wait_ge(sem("tables_ready"), 1)
        total = act.value_load(ends[0:1, E - 1:E], min_val=E, max_val=MAX_BLOCKS)
        rows_T(0)
        next_expert_high(0, 0)
        block(0)
        down_high(0, 0)
        with act.Fori(1, total) as g:
            e = act.value_load(expert_of[0:1, ds(g, 1)], min_val=0, max_val=E - 1)
            e_was = act.value_load(expert_of[0:1, ds(g - 1, 1)], min_val=0, max_val=E - 1)
            with act.If(e_was < e):
                with act.If(e < E - 1):
                    next_expert_high(g, e)
            block(g)
            with act.If(e_was < e):
                with act.If(e < E - 1):
                    down_high(g, e)
                with act.Else():
                    down_high(g, e, 16)
        rows_out(total - 1)

        def weigh(q, r):
            t = ROUND * q + r
            act.wait_ge(sem(f"slot_in{r}"), 16 * (MOD_LOADS + OUT_LOADS) + 32 * (q + 1))
            wait(act, sem(f"out_stored{r}"), 16 * q)
            act.sem_inc(sem("last_waits"), 1)
            w0 = pair_w[:, ds(t, 1), 0:1].rearrange("p a b -> p (a b)")
            nc.scalar.activation(acc_row(t), yp[r][:, 0, :], ACT.Copy, scale=w0).then_inc(sem("first_weighed"), 1)

        def roots(q):
            act.wait_ge(sem("meansq"), ROUNDS + TT + q + 1)
            nc.scalar.activation(rms3[:], ms3[:], ACT.Sqrt).then_inc(sem("rms"), 1)

        def last_round(q, more):
            for r in range(ROUND):
                if r < ROUND - 1:
                    weigh(q, r + 1)
                elif more:
                    weigh(q + 1, 0)
                if r == 0 and not (isinstance(q, int) and q == 0):
                    roots(q - 1)
                t = ROUND * q + r
                wait(act, sem("sumsq"), 2 * TT + t)
                act.wait_ge(sem("acc_ready"), t + 1)
                act.sem_inc(sem("last_waits"), 1)
                nc.scalar.activation(sq3[:], acc_row(t), ACT.Square, accum_out=ssq3[:, r:r + 1]).then_inc(sem("sumsq"), 1)

        weigh(0, 0)
        last_round(0, True)
        with act.Fori(1, TT // ROUND - 1) as q:
            last_round(q, True)
        last_round(TT // ROUND - 1, False)
        roots(TT // ROUND - 1)

    @block.vector
    def _(dve):
        ch = Chain(dve, sem("dve_chain"))
        link = lambda ins: (ch(ins), ch.join())

        def take_row(j):
            dve.wait_ge(sem("mod_mm"), 2 * (j + 1))
            if j == NORM_FROM:
                dve.wait_ge(sem("cols_mm"), 1)
                ch(nc.vector.tensor_copy(A1[:], bank[2][:, 0:KD]))
                ch(nc.vector.tensor_copy(B1[:], bank[2][:, KD:2 * KD]))
            if j == 2 * NORM_FROM:
                dve.wait_ge(sem("rows_out"), 16 * NORM_FROM)
            src, n = bank[j % 2][0:1, :], j // 2
            if n in (1, 4):
                dve.wait_ge(sem("g_in"), 32 if n == 1 else 48)
                half = gain[:, (j % 2) * CHUNK:(j % 2 + 1) * CHUNK]
                nc.vector.scalar_tensor_tensor(mod_row[j % 4][:], src, 1.0, half, ALU.add, ALU.mult).then_inc(sem("mod_row"), 1)
            else:
                nc.vector.tensor_copy(mod_row[j % 4][:], src).then_inc(sem("mod_row"), 1)

        def row_stats(q):
            dve.wait_ge(sem("sumsq"), ROUND * (q + 1))
            nc.vector.tensor_scalar(ms1[:], ssq1[:], 1.0 / D, EPS, ALU.mult, ALU.add).then_inc(sem("meansq"), 1)
            dve.wait_ge(sem("rms"), q + 1)
            wait(dve, sem("xn_ready"), ROUND * q)
            nc.vector.reciprocal(rstd1[:], rms1[:]).then_inc(sem("rstd"), 1)

        def take_tile(t):
            dve.wait_ge(sem("xT_done"), t + 1)
            for k in range(KD):
                src = PS[3 + 2 * (t % 2) + k // 4][:, (k % 4) * P:(k % 4 + 1) * P]
                last = nc.vector.tensor_scalar(hT[:, k, t * P:(t + 1) * P], src, A1[:, k:k + 1], B1[:, k:k + 1], ALU.mult, ALU.add)
            last.then_inc(sem("h_all"), 1)

        take_row(0)
        dve.wait_ge(sem("pos_in"), 112)
        dve.wait_ge(sem("invf_ready"), 1)
        link(nc.vector.tensor_copy(pos_f[:], pos_i[:]))
        pf = pos_f[:].rearrange("p (t a) -> p t a", a=1).broadcast_to([P, 3 * TT, HALF])
        fr = invf[:].rearrange("p (a f) -> p a f", a=1).broadcast_to([P, 3 * TT, HALF])
        link(nc.vector.tensor_tensor(ang[:], pf, fr, ALU.mult))
        link(nc.vector.tensor_scalar(turn[:], ang[:], float(1 / (2 * np.pi)), MAGIC, ALU.mult, ALU.add))
        take_row(1)
        link(nc.vector.tensor_scalar(turn[:], turn[:], -MAGIC, None, ALU.add))
        for part in PI2:
            link(nc.vector.scalar_tensor_tensor(ang[:], turn[:], -part, ang[:], ALU.mult, ALU.add))
        take_row(2)
        row_stats(0)
        lim = 3.1415925
        nc.vector.tensor_scalar(ang[:], ang[:], lim, -lim, ALU.min, ALU.max).then_inc(sem("reduced"), 1)
        dve.wait_ge(sem("reduced"), 1)
        link(nc.vector.scalar_tensor_tensor(turn[:], ang[:], -1.0, ang[:], ALU.mult, ALU.max))
        nc.vector.tensor_scalar(turn[:], turn[:], -1.0, float(np.pi / 2), ALU.mult, ALU.add).then_inc(sem("reduced"), 1)
        link(nc.vector.tensor_scalar(nsink[:], sink_bc[:], -1.0, None, ALU.mult))
        take_row(3)
        for j in range(NORM_FROM, MOD_CHUNKS):
            take_row(j)
            ch.join()
            t = 2 * (j - NORM_FROM)
            take_tile(t)
            take_tile(t + 1)
            if t % ROUND == 2 and t + 2 < TT:
                row_stats(t // ROUND + 1)
        dve.wait_ge(sem("attn_consts"), 1)
        dve.wait_ge(sem("angles_ready"), 2)

        def rotary(S, g):
            row = tile_of(S) + (0 if g == 3 else TT * g)
            nh = 4 if g < 3 else 5
            dve.wait_ge(sem("proj_evicted"), S + 1)
            wait(dve, sem("qkT_done"), S)
            cos_b = cos_t[:, ds(row, 1), :].broadcast_to([P, 2 * nh, HALF])
            sin_b = sin_t[:, ds(row, 1), :].broadcast_to([P, nh, HALF])
            raw = qk_raw[:, 0:nh * HD]
            r4 = raw.rearrange("p (h m) -> p h m", h=nh)
            tmp4 = qk_tmp[:, 0:nh * HD].rearrange("p (h m) -> p h m", h=nh)
            nc.vector.tensor_tensor(qk_rot[:, 0:nh * HD].rearrange("p (h m) -> p h m", m=HALF), raw.rearrange("p (h m) -> p h m", m=HALF), cos_b, ALU.mult)
            nc.vector.scalar_tensor_tensor(tmp4[:, :, 0:HALF], r4[:, :, HALF:HD], -1.0, sin_b, ALU.mult, ALU.mult)
            nc.vector.tensor_tensor(tmp4[:, :, HALF:HD], r4[:, :, 0:HALF], sin_b, ALU.mult).then_inc(sem("rot_parts"), 1)
            dve.wait_ge(sem("rot_parts"), S + 1)
            nc.vector.tensor_tensor(qk_rot[:, 0:nh * HD], qk_rot[:, 0:nh * HD], qk_tmp[:, 0:nh * HD], ALU.add).then_inc(sem("rot_done"), 1)

        def step(T, c, gs, loads):
            g1, g2, g3 = gs[2], gs[3], gs[4]
            if g1 is not None:
                S = T - 1
                if g1 < 3:
                    rotary(S, g1)
                dve.wait_ge(sem("qkT_done"), S + 1)
                t = tile_of(S)
                q = qst[1 - c]
                tb = bank[2]
                for pair in range(1 if g1 < 3 else 2):
                    nc.vector.tensor_copy(q[0:HD, 2 * pair, :], tb[0:HD, pair * P:(pair + 1) * P])
                    nc.vector.tensor_copy(q[HD:P, 2 * pair + 1, :], tb[HD:P, pair * P:(pair + 1) * P])
                if g1 < 3:
                    last = nc.vector.tensor_copy(kT_dil[:, ds(HD + t * P, P)], tb[:, P:2 * P])
                else:
                    nc.vector.tensor_copy(kT_swa[0:HD, ds(P + t * P, P)], tb[0:HD, 2 * P:3 * P])
                    last = nc.vector.tensor_copy(kT_swa[HD:P, ds(P + t * P, P)], tb[0:HD, 2 * P:3 * P])
                last.then_inc(sem("qk_ready"), 1)
            for u in (0, 1):
                if g2 is not None and u in units(g2):
                    S = T - 2
                    n = unit(g2, S, u)
                    dve.wait_ge(sem("s_done"), n + 1)
                    w = 256 if g2 < 3 else 384
                    e = e_sb[u][:, :, 0:w]
                    if g2 < 3:
                        src = S_ps[:, 0, :].rearrange("p (h w) -> p h w", h=2)
                        mk = mask_dil
                    else:
                        src, mk = S_ps[:, :, 0:384], mask_swa
                    m = mk[:, ds(mask_index(g2, tile_of(S)), 1), :].broadcast_to([P, 2, w])
                    nc.vector.tensor_tensor(e, src, m, ALU.add).then_inc(sem("masked"), 1)
                    if g2 == 3 and u == 1 and gs[1] is not None:
                        rotary(T, 3)
                    dve.wait_ge(sem("masked"), n + 1)
                    wait(dve, sem("max_ready"), n)
                    nc.vector.tensor_reduce(mx[:], e, AX.X, ALU.max).then_inc(sem("maxed"), 1)
                    dve.wait_ge(sem("maxed"), n + 1)
                    wait(dve, sem(f"o_out{c}{u}"), 8 * (S - c) if u == 0 else 8 * (S - c) - 8 * SWA_T0)
                    negm = o_row[c][u][:, :, HD:HD + 1].rearrange("p h a -> p (h a)")
                    if g2 < 3:
                        nc.vector.tensor_scalar(negm, mx[:], -SCALE, None, ALU.mult).then_inc(sem("max_ready"), 1)
                    else:
                        head = ((S // TT) % 2) * 4 + 2 * u
                        nc.vector.scalar_tensor_tensor(negm, mx[:], -SCALE, nsink[:, ds(head, 2)], ALU.mult, ALU.min).then_inc(sem("nm_step"), 1)
                        dve.wait_ge(sem("nm_step"), n - SWA_T0 + 1)
                        nc.vector.tensor_tensor(snk[c][u][:], negm, sink_bc[:, ds(head, 2)], ALU.add).then_inc(sem("max_ready"), 1)
                if g3 is not None and u in units(g3):
                    S = T - 3
                    n = unit(g3, S, u)
                    row = o_row[1 - c][u]
                    dve.wait_ge(sem("pv_done"), n + 1)
                    src = O_ps[:, 0:P].rearrange("p (h m) -> p h m", h=2)
                    if g3 < 3:
                        nc.vector.tensor_copy(row[:, :, 0:HD], src).then_inc(sem("o_done"), 1)
                    else:
                        den = row[:, :, HD + 1:HD + 2].rearrange("p h a -> p (h a)")
                        nc.vector.tensor_tensor(rden[:], den, esk[1 - c][u][:], ALU.add).then_inc(sem("den_step"), 1)
                        dve.wait_ge(sem("den_step"), 2 * (n - SWA_T0) + 1)
                        nc.vector.reciprocal(rden[:], rden[:]).then_inc(sem("den_step"), 1)
                        dve.wait_ge(sem("den_step"), 2 * (n - SWA_T0) + 2)
                        rb = rden[:].rearrange("p (h a) -> p h a", a=1).broadcast_to([P, 2, HD])
                        nc.vector.tensor_tensor(row[:, :, 0:HD], src, rb, ALU.mult).then_inc(sem("o_done"), 1)

            if gs[1] == 3 and g2 != 3:
                rotary(T, 3)

        schedule(dve, step)

        def lower_chunk(q, k, cc):
            dve.wait_ge(sem("x_hi_ready"), KD * q + k + 1)
            at = (slice(None), ds(k, 1), ds(q * CHUNK, CHUNK))
            nc.vector.tensor_tensor(hT_lo[at], hT[at], x_hi[cc][:, ds(k, 1), :].bitcast(F32), ALU.subtract).then_inc(sem("x_lo_ready"), 1)

        with dve.Fori(0, TT // 4) as i:
            for c in range(2):
                pair = 2 * i + c
                dve.wait_ge(sem(f"od_in{c}"), 48 * (i + 1))
                rows = od[c][:].rearrange("p u g (h m) -> p u g h m", m=STAT)
                negm = rows[:, :, :, :, HD:HD + 1].rearrange("p u g h a -> p u g (h a)")
                den = rows[:, :, :, :, HD + 1:HD + 2].rearrange("p u g h a -> p u g (h a)")
                per_h = lambda t3: t3[:].rearrange("p u (a h) -> p u a h", a=1).broadcast_to([P, 2, 3, DIL_HEADS])
                link_n = [0]

                def link5(ins):
                    link_n[0] += 1
                    ins.then_inc(sem("merge_step"), 1)
                    dve.wait_ge(sem("merge_step"), 8 * pair + link_n[0])

                link5(nc.vector.tensor_tensor(nmin[:], negm[:, :, 0, :], negm[:, :, 1, :], ALU.min))
                link5(nc.vector.tensor_tensor(nmin[:], nmin[:], negm[:, :, 2, :], ALU.min))
                nc.vector.tensor_tensor(wg[:], per_h(nmin), negm, ALU.subtract).then_inc(sem("wg_in"), 1)
                lower_chunk(0, pair, 0)
                dve.wait_ge(sem("wg_exp"), pair + 1)
                link5(nc.vector.tensor_tensor(wden[:], wg[:], den, ALU.mult))
                link5(nc.vector.tensor_reduce(dsum[:], wden[:].rearrange("p u g h -> p u h g"), AX.X, ALU.add))
                link5(nc.vector.reciprocal(dsum[:], dsum[:]))
                link5(nc.vector.tensor_tensor(wg[:], wg[:], per_h(dsum), ALU.mult))
                flat_wg = wg[:].rearrange("p u g (h a) -> p (u g h) a", a=1).broadcast_to([P, 2 * 3 * DIL_HEADS, HD])
                link5(nc.vector.tensor_tensor(wsum[:].rearrange("p u g (h m) -> p (u g h) m", m=HD), rows.rearrange("p u g h m -> p (u g h) m")[:, :, 0:HD], flat_wg, ALU.mult))
                link5(nc.vector.tensor_tensor(wsum[:, :, 0, :], wsum[:, :, 0, :], wsum[:, :, 1, :], ALU.add))
                dve.wait_ge(sem("oT_done"), 2 * pair + 1)
                nc.vector.tensor_tensor(oa[:], wsum[:, :, 0, :], wsum[:, :, 2, :], ALU.add).then_inc(sem("oa_ready"), 1)

        dve.sem_inc(sem("gated"), 2)

        def gate_chunk(q, cc, more):
            dve.wait_ge(sem("o_hi_ready"), q + 1)
            nc.vector.tensor_tensor(o_lo[cc][:], o_in[cc][:], o_hi[cc][:].bitcast(F32), ALU.subtract).then_inc(sem("o_lo_ready"), 1)
            with dve.Fori(0, KD // 2) as i:
                for c in range(2):
                    n = KD * q + 2 * i + c
                    dve.wait_ge(sem("sig_ready"), n + 1)
                    dve.wait_ge(sem(f"mT_out{c}"), 16 * ((KD // 2) * q + i + 1))
                    nc.vector.tensor_tensor(sig[:, 0, :], sig[:, 0, :], PS[4 * c + 2][:], ALU.mult)
                    nc.vector.tensor_tensor(sig[:, 1, :], sig[:, 1, :], PS[4 * c + 3][:], ALU.mult).then_inc(sem("gated"), 1)
                    dve.wait_ge(sem("gated"), n + 3)
                    nc.vector.tensor_tensor(mg[c][:], sig[:, 0, :], sig[:, 1, :], ALU.add).then_inc(sem("merged"), 1)
                    if more:
                        lower_chunk(q + 1, 2 * i + c, 1 - cc)

        chunk_loops(dve, gate_chunk)

        for k in range(KD):
            dve.wait_ge(sem("wo_hi_ready"), k + 1)
            nc.vector.tensor_tensor(wo_lo[:, k, :], wo_raw[k % 4][:], wo_hi[:, k, :].bitcast(F32), ALU.subtract).then_inc(sem("wo_lo_ready"), 1)
        dve.wait_ge(sem("rows_in"), 64)

        def residual(t, c, i):
            dve.wait_ge(sem("y_done"), t + 1)
            wait(dve, sem(f"x1_out{c}"), 32 * i)
            for j in range(2):
                last = nc.vector.tensor_tensor(x1[c][:, j * 512:(j + 1) * 512], PS[2 * c + j][:], gt1b[:, j * 512:(j + 1) * 512], ALU.mult)
            last.then_inc(sem("y_evicted"), 1)
            dve.wait_ge(sem("y_evicted"), t + 1)
            dve.wait_ge(sem(f"x_in{c}"), 16 * (ROUNDS // 2 + i + 1))
            nc.vector.tensor_tensor(x1[c][:], x1[c][:], x_in[c][:], ALU.add).then_inc(sem("x1_ready"), 1)
            dve.wait_ge(sem("sumsq"), 1 * TT + t + 1)
            nc.vector.tensor_scalar(st2[:, 1:2], st2[:, 0:1], 1.0 / D, EPS, ALU.mult, ALU.add).then_inc(sem("meansq"), 1)
            dve.wait_ge(sem("rms"), ROUNDS + t + 1)
            nc.vector.reciprocal(st2[:, 3:4], st2[:, 2:3]).then_inc(sem("rstd"), 1)
            dve.wait_ge(sem("rstd"), ROUNDS + t + 1)
            nc.vector.scalar_tensor_tensor(h2[c][:], x1[c][:], st2[:, 3:4], A2b[:], ALU.mult, ALU.mult).then_inc(sem("h2_scaled"), 1)
            dve.wait_ge(sem("h2_scaled"), t + 1)
            nc.vector.tensor_tensor(h2[c][:], h2[c][:], B2b[:], ALU.add).then_inc(sem("h2_ready"), 1)

        def take_logits(t):
            dve.wait_ge(sem("logits_done"), t + 1)
            nc.vector.tensor_copy(logits[:, ds(t, 1), :], PS[6][:, 0:GROUPS + E].rearrange("p (a n) -> p a n", a=1)).then_inc(sem("logits_ready"), 1)

        residual(0, 0, 0)
        residual(1, 1, 0)
        with dve.Fori(1, TT // 2) as i:
            for c in range(2):
                take_logits(2 * i + c - 2)
                residual(2 * i + c, c, i)
        take_logits(TT - 2)
        take_logits(TT - 1)

        dve.wait_ge(sem("rows_in"), 80)
        dve.wait_ge(sem("route_consts"), 1)
        dve.wait_ge(sem("dve_chain"), ch.n)
        rb = r_bias[:].rearrange("p (a n) -> p a n", a=1).broadcast_to([P, TT, GROUPS + E])
        link(nc.vector.tensor_tensor(logits[:], logits[:], rb, ALU.add))
        gl = logits[:, :, 0:GROUPS]

        def wide(ap, n):
            return ap[:].broadcast_to([P, TT, n])

        def first_best(vals, n, best, eq, idx, oh_out):
            link(nc.vector.tensor_reduce(best[:].rearrange("p t a -> p (t a)"), vals, AX.X, ALU.max))
            link(nc.vector.tensor_tensor(eq[:], vals, wide(best, n), ALU.is_equal))
            link(nc.vector.scalar_tensor_tensor(eq[:], eq[:], -float(n), iota_e[:, :, 0:n], ALU.mult, ALU.add))
            link(nc.vector.tensor_reduce(idx[:].rearrange("p t a -> p (t a)"), eq[:], AX.X, ALU.min))
            link(nc.vector.tensor_tensor(oh_out[:], eq[:], wide(idx, n), ALU.is_equal))

        first_best(gl, GROUPS, gmax, geq, gidx, gsel)
        nc.vector.tensor_tensor(gex[:], gl, wide(gmax, GROUPS), ALU.subtract).then_inc(sem("differences"), 1)
        link(nc.vector.tensor_scalar(gsel[:], gsel[:], -NEG, NEG, ALU.mult, ALU.add))
        pen = gsel[:].rearrange("p t (g a) -> p (t g) a", a=1).broadcast_to([P, TT * GROUPS, PER_GROUP])
        link(nc.vector.tensor_copy(el[:], logits[:, :, GROUPS:]))
        el3 = el[:].rearrange("p t (g a) -> p (t g) a", a=PER_GROUP)
        link(nc.vector.tensor_tensor(el3, el3, pen, ALU.add))
        first_best(el[:], E, top[0], eeq, eidx, oh[0])
        link(nc.vector.scalar_tensor_tensor(el[:], oh[0][:], 2 * NEG, el[:], ALU.mult, ALU.add))
        first_best(el[:], E, top[1], eeq, eidx, oh[1])
        nc.vector.tensor_tensor(ratio[:], top[1][:], top[0][:], ALU.subtract).then_inc(sem("differences"), 1)
        nc.vector.tensor_tensor(both[:], oh[0][:], oh[1][:], ALU.add).then_inc(sem("both_ready"), 1)
        dve.wait_ge(sem("exponentials"), 1)
        link(nc.vector.tensor_reduce(gsum[:].rearrange("p t a -> p (t a)"), gex[:], AX.X, ALU.add))
        dve.wait_ge(sem("exponentials"), 2)
        link(nc.vector.tensor_scalar(rinv[:], ratio[:], 1.0, None, ALU.add))
        link(nc.vector.tensor_tensor(rinv[:], rinv[:], gsum[:], ALU.mult))
        link(nc.vector.reciprocal(pair_w[:, :, 0:1], rinv[:]))
        link(nc.vector.tensor_tensor(pair_w[:, :, 1:2], pair_w[:, :, 0:1], ratio[:], ALU.mult))
        dve.wait_ge(sem("ranks_done"), 1)
        link(nc.vector.tensor_scalar(cnt_i[:], PS[1][:, 0:E], float(BLK - 1), None, ALU.add))
        link(nc.vector.tensor_scalar(cnt_i[:], cnt_i[:], 7, None, ALU.logical_shift_right))
        link(nc.vector.tensor_copy(nblk[:], cnt_i[:]))
        link(nc.vector.tensor_scalar(nblk[:], nblk[:], 1.0, None, ALU.max))
        link(nc.vector.memset(cnt[:], 1.0))
        link(nc.vector.tensor_tensor_scan(pend[:], cnt[:], nblk[:], 0.0, ALU.mult, ALU.add))
        link(nc.vector.tensor_copy(ends[:], pend[0:1, :]))
        link(nc.vector.tensor_tensor(pbase[:], pend[:], nblk[:], ALU.subtract))
        link(nc.vector.tensor_scalar(pbase[:], pbase[:], float(BLK), None, ALU.mult))
        pe_b = pend[:].rearrange("p (a e) -> p a e", a=1).broadcast_to([P, MAX_BLOCKS, E])
        ib_b = iota_b[:].rearrange("p (b a) -> p b a", a=1).broadcast_to([P, MAX_BLOCKS, E])
        link(nc.vector.tensor_tensor(cmp_e[:], pe_b, ib_b, ALU.is_le))
        link(nc.vector.tensor_reduce(e_f[:], cmp_e[:], AX.X, ALU.add))
        link(nc.vector.tensor_scalar(e_f[:], e_f[:], float(E - 1), None, ALU.min))
        link(nc.vector.tensor_copy(expert_of[0:1, 0:MAX_BLOCKS], e_f[0:1, :]))
        rk = PS[0][:, 0:TT * E].rearrange("p (t e) -> p t e", e=E)
        pb = pbase[:].rearrange("p (a e) -> p a e", a=1).broadcast_to([P, TT, E])
        link(nc.vector.tensor_tensor(posn[:], rk, pb, ALU.add))
        for k in range(2):
            link(nc.vector.tensor_tensor(prod[:], posn[:], oh[k][:], ALU.mult))
            link(nc.vector.tensor_reduce(slot_f[:, :, k:k + 1].rearrange("p t a -> p (t a)"), prod[:], AX.X, ALU.add))
        link(nc.vector.tensor_copy(slot_i[:], slot_f[:]))
        link(nc.vector.tensor_scalar(lane_i[:], slot_i[:], BLK - 1, None, ALU.bitwise_and))
        link(nc.vector.tensor_scalar(blk_i[:], slot_i[:], 7, None, ALU.logical_shift_right))
        link(nc.vector.tensor_copy(lane_f[:], lane_i[:]))
        link(nc.vector.tensor_copy(blk_f[:], blk_i[:]))
        with dve.Fori(0, TT) as t:
            for k in range(2):
                dve.wait_ge(sem("oh_free"), 2 * t + k + 1)
                lane = lane_f[:, ds(t, 1), k:k + 1].rearrange("p a b -> p (a b)")
                blk = blk_f[:, ds(t, 1), k:k + 1].rearrange("p a b -> p (a b)")
                ident_k = flat_id[:, ds(t, 1), k:k + 1].rearrange("p a b -> p (a b)")
                nc.vector.tensor_scalar(lane_oh[k][:], iota_r[:], lane, None, ALU.is_equal)
                nc.vector.tensor_scalar(blk_oh[k][:, 0, :], iota_b[:], blk, ident_k, ALU.is_equal, ALU.mult)
                nc.vector.tensor_scalar(blk_oh[k][:, 1, :], iota_b[:], blk, None, ALU.is_equal).then_inc(sem("oh_ready"), 1)
        dve.wait_ge(sem("oh_free"), 2 * TT + 2)
        link(nc.vector.tensor_copy(tab[:], PS[2][:, 0:2 * MAX_BLOCKS].rearrange("p (a b) -> p a b", a=2)))
        link(nc.vector.scalar_tensor_tensor(idx_f[:], tab[:, 1, :], pad_id[:, 1:2], tab[:, 0, :], ALU.mult, ALU.add))
        link(nc.vector.tensor_scalar(idx_f[:], idx_f[:], pad_id[:, 0:1], None, ALU.add))
        link(nc.vector.tensor_copy(scatter_idx[:, 0:MAX_BLOCKS], idx_f[:]))
        link(nc.vector.tensor_copy(scatter_idx[:, MAX_BLOCKS:], pad_id[:, 0:1]))
        link(nc.vector.tensor_scalar(gather_idx[:], scatter_idx[:], 1, None, ALU.logical_shift_right))
        dve.sem_inc(sem("tables_ready"), 1)

        def gate_up_low(e, k, slot, count):
            dve.wait_ge(sem("gu_hi_ready"), count)
            raw = w_in[slot][:].rearrange("p (a n) -> p a n", a=1)
            nc.vector.tensor_tensor(gu[:, ds(gu_row(e, 1, k), 1), :], raw, gu[:, ds(gu_row(e, 0, k), 1), :].bitcast(F32), ALU.subtract).then_inc(sem("gu_lo_ready"), 1)

        def next_expert_low(e):
            for j in range(KD):
                gate_up_low(e + 1, j, j % RING, KD * (e + 1) + j + 1)

        def down_low(e):
            for k in range(KE):
                dve.wait_ge(sem("dn_hi_ready"), KE * e + k + 1)
                nc.vector.tensor_tensor(dn_lo[:, k, :], w_in[(KD + k) % RING][:], dn_hi[:, k, :].bitcast(F32), ALU.subtract).then_inc(sem("dn_lo_ready"), 1)

        def rows_low(g):
            dve.wait_ge(sem("xT_high"), g + 1)
            for j in range(2):
                last = nc.vector.tensor_tensor(x_loT[:, 4 * j:4 * j + 4, :], PS[2 + j][:].rearrange("p (k s) -> p k s", k=4), x_hiT[:, 4 * j:4 * j + 4, :].bitcast(F32), ALU.subtract)
            last.then_inc(sem("xT_ready"), 1)

        def block(g):
            dve.wait_ge(sem("silu_done"), g + 1)
            nc.vector.tensor_tensor(hg[:], hg[:], PS[1][:], ALU.mult).then_inc(sem("h_ready"), 1)
            rows_low(g + 1)
            dve.wait_ge(sem("hT_high"), g + 1)
            nc.vector.tensor_tensor(h_loT[:], PS[6][:].rearrange("p (k s) -> p k s", k=KE), h_hiT[:].bitcast(F32), ALU.subtract).then_inc(sem("hT_ready"), 1)

        for k in range(KD):
            gate_up_low(0, k, (k + 2 * RING - KD) % RING, k + 1)
        dve.wait_ge(sem("tables_ready"), 1)
        total = dve.value_load(ends[0:1, E - 1:E], min_val=E, max_val=MAX_BLOCKS)
        rows_low(0)
        next_expert_low(0)
        block(0)
        down_low(0)
        with dve.Fori(1, total) as g:
            e = dve.value_load(expert_of[0:1, ds(g, 1)], min_val=0, max_val=E - 1)
            e_was = dve.value_load(expert_of[0:1, ds(g - 1, 1)], min_val=0, max_val=E - 1)
            with dve.If(e_was < e):
                with dve.If(e < E - 1):
                    next_expert_low(e)
            block(g)
            with dve.If(e_was < e):
                down_low(e)

        dve.wait_ge(sem("rows_in"), 112)

        def total_row(q, r):
            t = ROUND * q + r
            steps_done = [0]

            def link3(ins):
                steps_done[0] += 1
                ins.then_inc(sem("last_step"), 1)
                dve.wait_ge(sem("last_step"), 2 * t + steps_done[0])

            w1 = pair_w[:, ds(t, 1), 1:2].rearrange("p a b -> p (a b)")
            row = acc_row(t)
            dve.wait_ge(sem("first_weighed"), t + 1)
            link3(nc.vector.scalar_tensor_tensor(row, yp[r][:, 1, :], w1, row, ALU.mult, ALU.add))
            link3(nc.vector.tensor_tensor(row, row, gt2b[:], ALU.mult))
            nc.vector.tensor_tensor(row, row, xl[r][:], ALU.add).then_inc(sem("acc_ready"), 1)

        def means(q):
            dve.wait_ge(sem("sumsq"), 2 * TT + ROUND * (q + 1))
            nc.vector.tensor_scalar(ms3[:], ssq3[:], 1.0 / D, EPS, ALU.mult, ALU.add).then_inc(sem("meansq"), 1)

        def inverse_roots(q):
            dve.wait_ge(sem("rms"), ROUNDS + TT + q + 1)
            nc.vector.reciprocal(rstd3[:], rms3[:]).then_inc(sem("rstd"), 1)
            dve.wait_ge(sem("rstd"), ROUNDS + TT + q + 1)

        def finish(t, r):
            nc.vector.scalar_tensor_tensor(acc_row(t), acc_row(t), rstd3[:, r:r + 1], gfb[:], ALU.mult, ALU.mult).then_inc(sem("out_ready"), 1)

        def last_round(q):
            for r in range(ROUND):
                t = ROUND * q + r
                total_row(q, r)
                if not isinstance(q, int) or t >= ROUND:
                    if r == 0:
                        if not isinstance(q, int) or q > 1:
                            finish(t - LAG, ROUND - 1)
                        means(q - 1)
                    else:
                        if r == 1:
                            inverse_roots(q - 1)
                        finish(t - LAG, r - 1)

        last_round(0)
        last_round(1)
        with dve.Fori(2, TT // ROUND) as q:
            last_round(q)
        finish(TT - LAG, ROUND - 1)
        means(TT // ROUND - 1)
        inverse_roots(TT // ROUND - 1)
        for r in range(ROUND):
            finish(TT - ROUND + r, r)

    @block.tensor
    def _(pe):
        pe.wait_ge(sem("ident_ready"), 1)
        pe.wait_ge(sem("c_silu"), 1)

        def mod_chunk(j):
            wait(pe, sem("mod_row"), j - 1)
            out_row = bank[j % 2][0:1, :]
            for k in range(KD):
                n = 2 * j + k // (KD // 2)
                if k % (KD // 2) == 0:
                    pe.wait_ge(sem(f"slot_in{n % 4}"), 16 * (n // 4 + 1))
                last = nc.tensor.matmul(out_row, c_sil[:, k:k + 1], wada[n % 4][:, k % (KD // 2), :], start=(k == 0), stop=False)
                if k == KD // 2 - 1:
                    last.then_inc(sem("mod_mm"), 1)
            if j == 0:
                pe.wait_ge(sem("g_in"), 32)
            nc.tensor.matmul(out_row, ident[0:MOD_CHUNKS, j:j + 1], bias_rows[:], start=False, stop=True).then_inc(sem("mod_mm"), 1)

        def turn_tile_1(t):
            pe.wait_ge(sem("xn_ready"), t + 1)
            wait(pe, sem("h_all"), t - 1)
            for k in range(KD):
                last = nc.tensor.transpose(PS[3 + 2 * (t % 2) + k // 4][:, (k % 4) * P:(k % 4 + 1) * P], xn[t % 2][:, k * P:(k + 1) * P], ident[:])
            last.then_inc(sem("xT_done"), 1)

        for j in range(MOD_CHUNKS):
            mod_chunk(j)
            if j == NORM_FROM:
                pe.wait_ge(sem("mod_row"), NORM_FROM)
                for col in range(2 * KD):
                    row = 2 * (1 - col // KD) + col % KD // 4
                    last = nc.tensor.matmul(bank[2][:, col:col + 1], mod_row[row][0:1, (col % 4) * P:(col % 4 + 1) * P], ones_row[0:1, 0:1], start=True, stop=True)
                last.then_inc(sem("cols_mm"), 1)
            if j >= NORM_FROM:
                turn_tile_1(2 * (j - NORM_FROM))
                turn_tile_1(2 * (j - NORM_FROM) + 1)
        pe.wait_ge(sem("h_all"), TT)

        def project(T, c, g, ks):
            row = ((T // TT) % 2) * KD
            for k in ks:
                for a, (x, w) in enumerate(((h_hi, w_hi), (h_hi, w_lo), (h_lo, w_hi))):
                    last = nc.tensor.matmul(bank[c][:, 0:PASS_COLS].rearrange("p (a m) -> p a m", a=1), x[c][:, k, :], w[:, ds(row + k, 1), :], start=(k == 0 and a == 0), stop=(k == KD - 1 and a == 2))
            if ks[-1] == KD - 1:
                last.then_inc(sem("proj_done"), 1)

        def step(T, c, gs, loads):
            g, g1, g2, g3 = gs[1], gs[2], gs[3], gs[4]
            if g is not None:
                pe.wait_ge(sem("h_lo_ready"), T + 1)
                pe.wait_ge(sem("w_lo_ready"), TT * (T // TT) + TT)
                wait(pe, sem("proj_evicted"), T - 1)
                project(T, c, g, (0, 1, 2, 3))
            if g1 is not None:
                pe.wait_ge(sem("rot_done"), T)
                tb = bank[2]
                if g1 < 3:
                    nc.tensor.transpose(tb[:, 0:P], qk_rot[:, 0:P], ident[:])
                    last = nc.tensor.transpose(tb[:, P:2 * P], qk_rot[:, P:2 * P], ident[:])
                else:
                    nc.tensor.transpose(tb[:, 0:P], qk_rot[:, 0:P], ident[:])
                    nc.tensor.transpose(tb[:, P:2 * P], qk_rot[:, P:2 * P], ident[:])
                    last = nc.tensor.transpose(tb[0:HD, 2 * P:3 * P], qk_rot[:, 2 * P:2 * P + HD], ident[:])
                last.then_inc(sem("qkT_done"), 1)
            if g is not None:
                project(T, c, g, (4, 5))
            two = (g2 == 3 or g3 == 3)
            for u in (0, 1):
                if g3 is not None and u in units(g3):
                    n = unit(g3, T - 3, u)
                    pe.wait_ge(sem("exp_done"), n + 1)
                    for h in range(2):
                        for j in range(2 if g3 < 3 else 3):
                            dst = E_ps[:, 0, (2 * h + j) * P:(2 * h + j + 1) * P] if g3 < 3 else E_ps[:, h, j * P:(j + 1) * P]
                            last = nc.tensor.transpose(dst, e_sb[u][:, h, j * P:(j + 1) * P], ident[:])
                    last.then_inc(sem("eT_done"), 1)
                if g2 is not None and u in units(g2):
                    S = T - 2
                    n = unit(g2, S, u)
                    if isinstance(T, int) and T - 1 >= STEPS:
                        pe.wait_ge(sem("qk_ready"), STEPS)
                    else:
                        pe.wait_ge(sem("qk_ready"), T)
                    wait(pe, sem("masked"), n)
                    t = tile_of(S)
                    for h in range(2):
                        if g2 < 3:
                            last = nc.tensor.matmul(S_ps[:, 0, h * 256:(h + 1) * 256], qst[c][:, h, :], kT_dil[:, ds(t * P, 256)], start=True, stop=True)
                        else:
                            last = nc.tensor.matmul(S_ps[:, h, 0:384], qst[c][:, 2 * u + h, :], kT_swa[:, ds(t * P, 384)], start=True, stop=True)
                    last.then_inc(sem("s_done"), 1)
                if g is not None:
                    if u == 0:
                        project(T, c, g, (6,) if two else (6, 7))
                    elif two:
                        project(T, c, g, (7,))
                if g3 is not None and u in units(g3):
                    S = T - 3
                    n = unit(g3, S, u)
                    pe.wait_ge(sem("eT_ready"), n + 1)
                    wait(pe, sem("o_done"), n)
                    t = tile_of(S)
                    nj = 2 if g3 < 3 else 3
                    for h in range(2):
                        for j in range(nj):
                            v = v_dil[:, ds(t + j, 1), h * HD:(h + 1) * HD] if g3 < 3 else v_swa[:, ds(t + j, 1), :]
                            last = nc.tensor.matmul(O_ps[:, h * HD:(h + 1) * HD].rearrange("p (a m) -> p a m", a=1), eT[:, h, j * P:(j + 1) * P], v,
                                                    start=(j == 0), stop=(j == nj - 1))
                    last.then_inc(sem("pv_done"), 1)

        schedule(pe, step)

        pe.sem_inc(sem("oT_done"), 1)
        pe.sem_inc(sem("gates_done"), 2)
        with pe.Fori(0, TT // 4) as i:
            for c in range(2):
                for u in range(2):
                    pair = 2 * i + c
                    pe.wait_ge(sem("oa_ready"), pair + 1)
                    pe.wait_ge(sem("oT_ready"), 2 * pair + u + 1)
                    for k in range(2):
                        nc.tensor.transpose(PS[2 * u][:, k * P:(k + 1) * P], oa[:, u, k * P:(k + 1) * P], ident[:])
                    for k in range(4):
                        last = nc.tensor.transpose(PS[2 * u + 1][:, k * P:(k + 1) * P], ob[c][:, u, k * P:(k + 1) * P], ident[:])
                    last.then_inc(sem("oT_done"), 1)

        parts = lambda w, x: ((w[0], x[0]), (w[0], x[1]), (w[1], x[0]))

        pe.wait_ge(sem("oT_ready"), TT + 2)
        def gate_chunk(q, cc, more):
            with pe.Fori(0, KD // 2) as i:
                for c in range(2):
                    n = KD * q + 2 * i + c
                    pe.wait_ge(sem("x_lo_ready"), KD * (q + 1))
                    pe.wait_ge(sem("g_lo_ready"), 2 * n + 2)
                    pe.wait_ge(sem("gated"), n + 1)
                    gw = (g_hi[c], g_lo[c])
                    off = KD * 2 * P
                    x_k = lambda k: (x_hi[cc][:, k:k + 1, :], hT_lo[:, k:k + 1, ds(q * CHUNK, CHUNK)])
                    o_k = lambda k: (o_hi[cc][:, k:k + 1, :], o_lo[cc][:, k:k + 1, :])
                    jobs = [(0, k, k * 2 * P, k == 0, k == KD - 1, x_k) for k in range(KD)]
                    jobs += [(1, k, k * 2 * P + P, k == 0, k == KD - 1, x_k) for k in range(KD)]
                    jobs += [(2, k, off + k * P, k == 0, k == 1, o_k) for k in range(2)]
                    jobs += [(3, k, off + k * P, k == 2, k == OUT_K - 1, o_k) for k in range(2, OUT_K)]
                    for dst, k, col, first, last_k, xs in jobs:
                        if dst == 2 and k == 0:
                            pe.wait_ge(sem("o_lo_ready"), q + 1)
                        for a, (w, x) in enumerate(parts(gw, xs(k))):
                            last = nc.tensor.matmul(PS[4 * c + dst][:].rearrange("p (a n) -> p a n", a=1), w[:, col:col + P], x,
                                                    start=first and a == 0, stop=last_k and a == 2)
                    last.then_inc(sem("gates_done"), 1)

        chunk_loops(pe, gate_chunk)

        def out_tile(t, c, halves):
            for j in halves:
                for k in range(KD):
                    if isinstance(t, int) and t == 0 and j == 0:
                        pe.wait_ge(sem("wo_lo_ready"), k + 1)
                    for a, (x, w) in enumerate(((m_hi, wo_hi), (m_hi, wo_lo), (m_lo, wo_hi))):
                        last = nc.tensor.matmul(PS[2 * c + j][:], x[c][:, k, :], w[:, k, j * 512:(j + 1) * 512],
                                                start=(k == 0 and a == 0), stop=(k == KD - 1 and a == 2))
            if halves[-1] == 1:
                last.then_inc(sem("y_done"), 1)

        def turn_tile(t, c):
            pe.wait_ge(sem("h2_ready"), t + 1)
            wait(pe, sem("h2T_ready"), t)
            for k in range(KD):
                last = nc.tensor.transpose(PS[4 + k // 4][:, (k % 4) * P:(k % 4 + 1) * P], h2[c][:, k * P:(k + 1) * P], ident[:])
            last.then_inc(sem("h2T_done"), 1)

        def route_tile(t):
            pe.wait_ge(sem("h2T_ready"), t + 1)
            wait(pe, sem("logits_ready"), t)
            for k in range(KD):
                last = nc.tensor.matmul(PS[6][:, 0:GROUPS + E], h2T[:, k, :], w_rt[:, k, :], start=(k == 0), stop=(k == KD - 1))
            last.then_inc(sem("logits_done"), 1)

        pe.wait_ge(sem("rows_in"), 64)
        pe.wait_ge(sem("m_lo_ready"), 1)
        out_tile(0, 0, (0, 1))
        pe.wait_ge(sem("m_lo_ready"), 2)
        out_tile(1, 1, (0, 1))
        turn_tile(0, 0)
        with pe.Fori(1, TT // 2) as i:
            for c in range(2):
                t = 2 * i + c
                pe.wait_ge(sem("m_lo_ready"), t + 1)
                pe.wait_ge(sem("y_evicted"), t - 1)
                out_tile(t, c, (0,))
                route_tile(t - 2)
                out_tile(t, c, (1,))
                turn_tile(t - 1, 1 - c)
        route_tile(TT - 2)
        turn_tile(TT - 1, 1)
        route_tile(TT - 1)

        pe.wait_ge(sem("both_ready"), 1)
        M = both[:].rearrange("p t e -> p (t e)")
        nc.tensor.matmul(PS[0][:, 0:TT * E], tri[:], M, start=True, stop=False)
        for back in range(1, TT):
            nc.tensor.matmul(PS[0][:, back * E:TT * E], all_ones[:], M[:, 0:(TT - back) * E], start=False, stop=(back == TT - 1))
        for t in range(TT):
            last = nc.tensor.matmul(PS[1][:, 0:E], all_ones[:], M[:, t * E:(t + 1) * E], start=(t == 0), stop=(t == TT - 1))
        last.then_inc(sem("ranks_done"), 1)
        pe.sem_inc(sem("oh_free"), 2)

        def place(t):
            for k in range(2):
                pe.wait_ge(sem("oh_ready"), 2 * t + k + 1)
                edge = isinstance(t, int)
                nc.tensor.matmul(PS[2][:, 0:2 * MAX_BLOCKS], lane_oh[k][:], blk_oh[k][:].rearrange("p a b -> p (a b)"),
                                 start=(edge and t == 0 and k == 0), stop=(edge and t == TT - 1 and k == 1)).then_inc(sem("oh_free"), 1)

        place(0)
        with pe.Fori(1, TT - 1) as t:
            place(t)
        place(TT - 1)

        pe.wait_ge(sem("tables_ready"), 1)
        total = pe.value_load(ends[0:1, E - 1:E], min_val=E, max_val=MAX_BLOCKS)

        def turn_rows(g):
            pe.wait_ge(sem("xg_in"), 16 * (g + 1))
            wait(pe, sem("xT_ready"), g)
            for k in range(KD):
                last = nc.tensor.transpose(PS[2 + k // 4][:, (k % 4) * P:(k % 4 + 1) * P], xg[:, k * P:(k + 1) * P], ident[:])
            last.then_inc(sem("xgT_done"), 1)

        def gate_up(g, e):
            pe.wait_ge(sem("xT_ready"), g + 1)
            pe.wait_ge(sem("gu_lo_ready"), KD * (e + 1))
            wait(pe, sem("h_ready"), g)
            for k in range(KD):
                for j in range(2):
                    for a, (x, part) in enumerate(((x_hiT, 0), (x_hiT, 1), (x_loT, 0))):
                        last = nc.tensor.matmul(PS[j][:].rearrange("p (a n) -> p a n", a=1), x[:, k, :], gu[:, ds(gu_row(e, part, k), 1), j * DE:(j + 1) * DE],
                                                start=(k == 0 and a == 0), stop=(k == KD - 1 and a == 2))
            last.then_inc(sem("gu_done"), 1)

        def down(g, e):
            pe.wait_ge(sem("hT_ready"), g + 1)
            pe.wait_ge(sem("dn_lo_ready"), KE * (e + 1))
            pe.wait_ge(sem("y_ready"), g + 1)
            for k in range(KE):
                for j in range(2):
                    for a, (x, w) in enumerate(((h_hiT, dn_hi), (h_hiT, dn_lo), (h_loT, dn_hi))):
                        last = nc.tensor.matmul(PS[4 + j][:], x[:, k, :], w[:, k, j * 512:(j + 1) * 512],
                                                start=(k == 0 and a == 0), stop=(k == KE - 1 and a == 2))
            last.then_inc(sem("down_done"), 1)

        def turn_hidden(g):
            pe.wait_ge(sem("h_ready"), g + 1)
            for k in range(KE):
                last = nc.tensor.transpose(PS[6][:, k * P:(k + 1) * P], hg[:, k * P:(k + 1) * P], ident[:])
            last.then_inc(sem("hT_done"), 1)

        turn_rows(0)
        gate_up(0, 0)
        turn_rows(1)
        turn_hidden(0)
        with pe.Fori(1, total) as g:
            e = pe.value_load(expert_of[0:1, ds(g, 1)], min_val=0, max_val=E - 1)
            e_was = pe.value_load(expert_of[0:1, ds(g - 1, 1)], min_val=0, max_val=E - 1)
            gate_up(g, e)
            turn_rows(g + 1)
            down(g - 1, e_was)
            turn_hidden(g)
        down(total - 1, E - 1)


def kernel(**inputs):
    import numpy as _np
    import concourse.bacc as _bacc
    from concourse import mybir as _mybir
    from concourse.bass_utils import run_bass_kernel_spmd as _run

    a = {n: _np.asarray(v) for n, v in inputs.items()}
    w = a["w_in"][0]
    dil, qw, kvw = DIL_HEADS * HD, SWA_HEADS * HD, 2 * HD
    q0, k0, v0 = 0, 3 * dil, 6 * dil
    qb, kb, vb, gates = 9 * dil, 9 * dil + qw, 9 * dil + qw + kvw, 9 * dil + qw + 2 * kvw

    def columns(*runs):
        return _np.concatenate([w[:, at:at + n] for at, n in runs], axis=1)

    passes = [columns((q0 + p * P, P), (k0 + p * P, P), (v0 + p * P, P)) for p in range(6)]
    passes += [columns((qb + p * 4 * HD, 4 * HD), (kb + p * HD, HD), (vb + p * HD, HD)) for p in range(2)]
    gate = w[:, gates:].reshape(KD, P, 2, KD, P).transpose(3, 1, 0, 2, 4).reshape(KD, P, KD * 2 * P)
    branch = _np.concatenate([a["w_branch_a"][0], a["w_branch_b"][0]], axis=0)
    branch = branch.reshape(OUT_K, P, KD, P).transpose(2, 1, 0, 3).reshape(KD, P, OUT_K * P)
    laid = {n: a[n] for n in ("x", "c", "positions", "w_ada", "b_ada", "g_mix", "g_ffn", "g_final", "sink_logits", "w_out",
                              "w_expert_down")}
    laid["w_gate_up"] = _np.concatenate([a["w_expert_gate"][0], a["w_expert_up"][0]], axis=2)
    laid["w_qkv"] = _np.stack(passes)
    laid["w_gb"] = _np.concatenate([gate, branch], axis=2)
    laid["w_rt"] = _np.concatenate([a["w_group"][0], a["w_route"][0]], axis=1)
    laid["b_rt"] = _np.concatenate([a["b_group"], a["b_route"]], axis=1)

    nc = _bacc.Bacc("TRN2", target_bir_lowering=False, num_devices=1)
    arrays, A = {}, {}
    for n, v in laid.items():
        arrays[f"in_{n}"] = v = _np.ascontiguousarray(v)
        A[n] = nc.dram_tensor(f"in_{n}", v.shape, _mybir.dt.from_np(v.dtype), kind="ExternalInput").ap()
    out = nc.dram_tensor("out_0", (1, SEQ, D), _mybir.dt.float32, kind="ExternalOutput").ap()
    build(nc, A, out)
    r = _run(nc, [arrays], core_ids=[0])
    return r.results[0]["out_0"]
```
